# Optimizing a Trainium2 kernel written in Bass

```python
import jax, jax.numpy as jnp
from jax import lax
import numpy as np

D_MODEL = 1024
BATCH = 1
SEQ = 256
DEPTH = 1

MOBA_HEADS = 8
HEAD_DIM = 64
MOBA_WIDTH = MOBA_HEADS * HEAD_DIM
MOBA_BLOCK = 256
MOBA_TOPK = 3
MOBA_Q_CHUNK = 32
ROPE_THETA = 500000.0
ROPE_DIM = HEAD_DIM // 4
RWKV_HEADS = 8
RWKV_WIDTH = RWKV_HEADS * HEAD_DIM
RWKV_DECAY_LORA = 64
RWKV_AAA_LORA = 64
RWKV_GATE_LORA = 128
RWKV_SHIFT_WIDTH = 3 * RWKV_WIDTH + RWKV_DECAY_LORA + RWKV_AAA_LORA + RWKV_GATE_LORA
GN_EPS = 64e-5
IN_SIZES = (MOBA_WIDTH, MOBA_WIDTH, MOBA_WIDTH, RWKV_SHIFT_WIDTH, 2 * D_MODEL)
IN_WIDTH = sum(IN_SIZES)
PEER_HEADS = 8
PEER_NKEYS = 128
PEER_EXPERTS = PEER_NKEYS * PEER_NKEYS
PEER_QDIM = 256
PEER_HALF = PEER_QDIM // 2
PEER_TOPK = 16
PEER_CHUNK = 128
RMS_EPS = 1e-6
NEG_INF = -1e30


def rms_norm(x, g, eps=RMS_EPS):
    x32 = x.astype(jnp.float32)
    y = x32 * lax.rsqrt(jnp.mean(x32 * x32, axis=-1, keepdims=True) + eps)
    return (y * g.astype(jnp.float32)).astype(x.dtype)

def rope_partial(x, pos):
    half = ROPE_DIM // 2
    inv = ROPE_THETA ** (-(jnp.arange(half, dtype=jnp.float32) * 2.0) / ROPE_DIM)
    ang = pos.astype(jnp.float32)[..., None] * inv
    cos = jnp.cos(ang)[:, :, None, :]
    sin = jnp.sin(ang)[:, :, None, :]
    x32 = x.astype(jnp.float32)
    x1 = x32[..., :half]
    x2 = x32[..., half:ROPE_DIM]
    out = jnp.concatenate([x1 * cos - x2 * sin, x2 * cos + x1 * sin, x32[..., ROPE_DIM:]], axis=-1)
    return out.astype(x.dtype)

def moba_attention(q, k, v):
    B, S, H, Dh = q.shape
    nb = -(-S // MOBA_BLOCK)
    sp = nb * MOBA_BLOCK
    pad = ((0, 0), (0, 0), (0, sp - S), (0, 0))
    q, k, v = (jnp.pad(t.transpose(0, 2, 1, 3), pad) for t in (q, k, v))
    kb = k.reshape(B, H, nb, MOBA_BLOCK, Dh)
    vb = v.reshape(B, H, nb, MOBA_BLOCK, Dh)
    scale = Dh ** -0.5
    qblk = jnp.arange(sp) // MOBA_BLOCK
    n_sel = min(MOBA_TOPK, nb - 1)
    if n_sel > 0:
        kmean = jnp.mean(kb.astype(jnp.float32), axis=3)
        gscore = jnp.einsum('bhsd,bhnd->bhsn', q.astype(jnp.float32), kmean)
        past = jnp.arange(nb)[None, :] < qblk[:, None]
        gscore = jnp.where(past, gscore, NEG_INF)
        _, sel = lax.top_k(gscore, n_sel)
        sel_ok = jnp.arange(n_sel)[None, :] < qblk[:, None]
    bi = jnp.arange(B)[:, None, None, None]
    hi = jnp.arange(H)[None, :, None, None]

    def attend_chunk(i):
        s0 = i * MOBA_Q_CHUNK
        qc = lax.dynamic_slice_in_dim(q, s0, MOBA_Q_CHUNK, axis=2)
        qpos = s0 + jnp.arange(MOBA_Q_CHUNK)
        own = s0 // MOBA_BLOCK
        k_own = lax.dynamic_index_in_dim(kb, own, axis=2, keepdims=False)
        v_own = lax.dynamic_index_in_dim(vb, own, axis=2, keepdims=False)
        kpos = own * MOBA_BLOCK + jnp.arange(MOBA_BLOCK)
        s_own = jnp.einsum('bhcd,bhkd->bhck', qc, k_own).astype(jnp.float32) * scale
        s_own = jnp.where(kpos[None, :] <= qpos[:, None], s_own, NEG_INF)
        if n_sel == 0:
            p = jax.nn.softmax(s_own, axis=-1).astype(v.dtype)
            return jnp.einsum('bhck,bhkd->bhcd', p, v_own)
        selc = lax.dynamic_slice_in_dim(sel, s0, MOBA_Q_CHUNK, axis=2)
        ok = lax.dynamic_slice_in_dim(sel_ok, s0, MOBA_Q_CHUNK, axis=0)
        k_sel = kb[bi, hi, selc]
        v_sel = vb[bi, hi, selc]
        s_sel = jnp.einsum('bhcd,bhcnkd->bhcnk', qc, k_sel).astype(jnp.float32) * scale
        s_sel = jnp.where(ok[None, None, :, :, None], s_sel, NEG_INF)
        s_all = jnp.concatenate([s_sel.reshape(B, H, MOBA_Q_CHUNK, n_sel * MOBA_BLOCK), s_own], axis=-1)
        p = jax.nn.softmax(s_all, axis=-1).astype(v.dtype)
        p_sel = p[..., :n_sel * MOBA_BLOCK].reshape(B, H, MOBA_Q_CHUNK, n_sel, MOBA_BLOCK)
        p_own = p[..., n_sel * MOBA_BLOCK:]
        return (jnp.einsum('bhcnk,bhcnkd->bhcd', p_sel, v_sel)
                + jnp.einsum('bhck,bhkd->bhcd', p_own, v_own))

    out = lax.map(attend_chunk, jnp.arange(sp // MOBA_Q_CHUNK))
    out = out.transpose(1, 0, 3, 2, 4).reshape(B, sp, H, Dh)
    return out[:, :S]

def token_shift(z, mu):
    prev = jnp.pad(z, ((0, 0), (1, 0), (0, 0)))[:, :-1]
    return z + (prev - z) * mu

def rwkv7_time_mix(zr, zk, zv, zw, za, zg, w0, w2, a0, a2, g2, k_k, k_a, r_k, ln_g, ln_b):
    B, S, _ = zr.shape
    H, N = RWKV_HEADS, HEAD_DIM
    f32 = jnp.float32
    w = -jax.nn.softplus(-(w0 + jnp.tanh(zw) @ w2)) - 0.5
    decay = jnp.exp(-jnp.exp(w.astype(f32)))
    a = jax.nn.sigmoid(a0 + za @ a2)
    g = jax.nn.sigmoid(zg) @ g2
    heads = lambda t: t.reshape(B, S, H, N).astype(f32)
    kk = heads(zk * k_k)
    kk = kk / jnp.maximum(jnp.sqrt(jnp.sum(kk * kk, axis=-1, keepdims=True)), 1e-12)
    k = zk * (1.0 + (a - 1.0) * k_a)
    r_h, k_h, v_h, a_h, d_h = heads(zr), heads(k), heads(zv), heads(a), heads(decay)

    def step(state, inp):
        r_t, d_t, k_t, v_t, kk_t, a_t = inp
        sa = jnp.einsum('bhij,bhj->bhi', state, -kk_t)
        state = (state * d_t[:, :, None, :] + sa[..., None] * (kk_t * a_t)[:, :, None, :]
                 + v_t[..., None] * k_t[:, :, None, :])
        return state, jnp.einsum('bhij,bhj->bhi', state, r_t)

    xs = tuple(t.transpose(1, 0, 2, 3) for t in (r_h, d_h, k_h, v_h, kk, a_h))
    _, y = lax.scan(step, jnp.zeros((B, H, N, N), f32), xs)
    y = y.transpose(1, 0, 2, 3)
    mean = jnp.mean(y, axis=-1, keepdims=True)
    var = jnp.mean(jnp.square(y - mean), axis=-1, keepdims=True)
    y = ((y - mean) * lax.rsqrt(var + GN_EPS)).reshape(B, S, H * N)
    y = y * ln_g.astype(f32) + ln_b.astype(f32)
    bonus = jnp.sum(r_h * k_h * r_k.astype(f32), axis=-1, keepdims=True) * v_h
    y = y + bonus.reshape(B, S, H * N)
    return (y * g.astype(f32)).astype(zr.dtype)

def peer_ffn(xn, wq, subkeys, u_tab, v_tab):
    B, S, D = xn.shape
    T = B * S
    xt = xn.reshape(T, D)
    q = (xt @ wq).reshape(T, PEER_HEADS, 2, PEER_HALF)
    s = jnp.einsum('thpd,hpnd->thpn', q, subkeys).astype(jnp.float32)
    top_s, top_i = lax.top_k(s, PEER_TOPK)
    cand_s = (top_s[:, :, 0, :, None] + top_s[:, :, 1, None, :]).reshape(T, PEER_HEADS, PEER_TOPK * PEER_TOPK)
    cand_i = (top_i[:, :, 0, :, None] * PEER_NKEYS + top_i[:, :, 1, None, :]).reshape(T, PEER_HEADS, PEER_TOPK * PEER_TOPK)
    best_s, best_j = lax.top_k(cand_s, PEER_TOPK)
    idx = jnp.take_along_axis(cand_i, best_j, axis=-1)
    gates = jax.nn.softmax(best_s, axis=-1)
    nc = T // PEER_CHUNK

    def retrieve(args):
        xc, ic, gc = args
        uc = u_tab[ic]
        vc = v_tab[ic]
        hdn = jax.nn.gelu(jnp.einsum('cd,chkd->chk', xc, uc).astype(jnp.float32), approximate=False) * gc
        return jnp.einsum('chk,chkd->cd', hdn.astype(vc.dtype), vc)

    out = lax.map(retrieve, (xt.reshape(nc, PEER_CHUNK, D),
                             idx.reshape(nc, PEER_CHUNK, PEER_HEADS, PEER_TOPK),
                             gates.reshape(nc, PEER_CHUNK, PEER_HEADS, PEER_TOPK)))
    return out.reshape(B, S, D).astype(xn.dtype)

def first_inputs(seed: int = 0) -> dict:
    key = jax.random.key(seed)
    ks = iter(jax.random.split(key, 40))
    L = DEPTH
    D = D_MODEL
    nrm = lambda shape, sc: jax.random.normal(next(ks), shape, jnp.float32) * sc
    unif = lambda shape, lo, hi: jax.random.uniform(next(ks), shape, jnp.float32, lo, hi)
    x = nrm((BATCH, SEQ, D), 1.0)
    c = nrm((BATCH, D), 1.0)
    positions = jnp.tile(jnp.arange(SEQ, dtype=jnp.int32)[None, :], (BATCH, 1))
    return {
        'x': x, 'c': c, 'positions': positions,
        'w_ada': nrm((L, D, 6 * D), 0.5 * D ** -0.5),
        'b_ada': nrm((L, 6 * D), 0.02),
        'norm1_g': 1.0 + nrm((L, D), 0.05),
        'w_in': nrm((L, D, IN_WIDTH), D ** -0.5),
        'q_norm_g': 1.0 + nrm((L, HEAD_DIM), 0.05),
        'k_norm_g': 1.0 + nrm((L, HEAD_DIM), 0.05),
        'rwkv_mu': unif((L, RWKV_SHIFT_WIDTH), 0.0, 1.0),
        'rwkv_w0': nrm((L, RWKV_WIDTH), 1.0) - 2.0,
        'rwkv_w2': nrm((L, RWKV_DECAY_LORA, RWKV_WIDTH), 0.5 * RWKV_DECAY_LORA ** -0.5),
        'rwkv_a0': nrm((L, RWKV_WIDTH), 0.5),
        'rwkv_a2': nrm((L, RWKV_AAA_LORA, RWKV_WIDTH), 0.5 * RWKV_AAA_LORA ** -0.5),
        'rwkv_g2': nrm((L, RWKV_GATE_LORA, RWKV_WIDTH), RWKV_GATE_LORA ** -0.5),
        'rwkv_k_k': 0.85 + nrm((L, RWKV_WIDTH), 0.1),
        'rwkv_k_a': 1.0 + nrm((L, RWKV_WIDTH), 0.1),
        'rwkv_r_k': nrm((L, RWKV_HEADS, HEAD_DIM), 0.1),
        'rwkv_ln_g': 1.0 + nrm((L, RWKV_WIDTH), 0.05),
        'rwkv_ln_b': nrm((L, RWKV_WIDTH), 0.02),
        'w_proj_moba': nrm((L, MOBA_WIDTH, D), MOBA_WIDTH ** -0.5),
        'w_proj_rwkv': nrm((L, RWKV_WIDTH, D), RWKV_WIDTH ** -0.5),
        'w_out': nrm((L, D, D), D ** -0.5),
        'norm2_g': 1.0 + nrm((L, D), 0.05),
        'peer_wq': nrm((L, D, PEER_HEADS * PEER_QDIM), D ** -0.5),
        'peer_subkeys': nrm((L, PEER_HEADS, 2, PEER_NKEYS, PEER_HALF), PEER_HALF ** -0.5),
        'peer_u': nrm((L, PEER_EXPERTS, D), D ** -0.5),
        'peer_v': nrm((L, PEER_EXPERTS, D), PEER_HEADS ** -0.5),
    }

def first_block(x, c, positions, w_ada, b_ada, norm1_g, w_in, q_norm_g, k_norm_g, rwkv_mu,
              rwkv_w0, rwkv_w2, rwkv_a0, rwkv_a2, rwkv_g2, rwkv_k_k, rwkv_k_a, rwkv_r_k,
              rwkv_ln_g, rwkv_ln_b, w_proj_moba, w_proj_rwkv, w_out, norm2_g, peer_wq,
              peer_subkeys, peer_u, peer_v):
    B, S, D = x.shape
    split_at = [int(v) for v in np.cumsum(IN_SIZES)[:-1]]
    rwkv_split = [int(v) for v in np.cumsum((RWKV_WIDTH, RWKV_WIDTH, RWKV_WIDTH, RWKV_DECAY_LORA, RWKV_AAA_LORA))]
    h = x
    for l in range(DEPTH):
        mod = (jax.nn.silu(c) @ w_ada[l] + b_ada[l])[:, None, :]
        sh1, sc1, gt1, sh2, sc2, gt2 = jnp.split(mod, 6, axis=-1)
        xn = rms_norm(h, norm1_g[l]) * (1.0 + sc1) + sh1
        proj = xn @ w_in[l]
        qm, km, vm, zrw, gate_logits = jnp.split(proj, split_at, axis=-1)
        qm = rope_partial(rms_norm(qm.reshape(B, S, MOBA_HEADS, HEAD_DIM), q_norm_g[l]), positions)
        km = rope_partial(rms_norm(km.reshape(B, S, MOBA_HEADS, HEAD_DIM), k_norm_g[l]), positions)
        vm = vm.reshape(B, S, MOBA_HEADS, HEAD_DIM)
        o_moba = moba_attention(qm, km, vm).reshape(B, S, MOBA_WIDTH)
        zrw = token_shift(zrw, rwkv_mu[l])
        zr, zk, zv, zw, za, zg = jnp.split(zrw, rwkv_split, axis=-1)
        o_rwkv = rwkv7_time_mix(zr, zk, zv, zw, za, zg, rwkv_w0[l], rwkv_w2[l], rwkv_a0[l],
                                rwkv_a2[l], rwkv_g2[l], rwkv_k_k[l], rwkv_k_a[l], rwkv_r_k[l],
                                rwkv_ln_g[l], rwkv_ln_b[l])
        g_moba, g_rwkv = jnp.split(jax.nn.sigmoid(gate_logits), 2, axis=-1)
        mixed = g_moba * (o_moba @ w_proj_moba[l]) + g_rwkv * (o_rwkv @ w_proj_rwkv[l])
        h = h + gt1 * (mixed @ w_out[l])
        xn2 = rms_norm(h, norm2_g[l]) * (1.0 + sc2) + sh2
        h = h + gt2 * peer_ffn(xn2, peer_wq[l], peer_subkeys[l], peer_u[l], peer_v[l])
    return h


NSA_HEADS = 8
NSA_KV_HEADS = 2
NSA_GROUP = NSA_HEADS // NSA_KV_HEADS
NSA_HEAD_DIM = 128
CMP_BLOCK = 32
CMP_STRIDE = 16
CMP_HIDDEN = 256
SEL_BLOCK = 64
SEL_TOPK = 16
WINDOW = 512
NSA_Q_BLOCK = 64
MLA_HEADS = 8
MLA_Q_RANK = 384
MLA_KV_RANK = 256
MLA_NOPE_DIM = 128
MLA_ROPE_DIM = 64
MLA_QK_DIM = MLA_NOPE_DIM + MLA_ROPE_DIM
MLA_V_DIM = 128
MLA_Q_BLOCK = 128
D_FF = 2816
CONV_WIDTH = 3
ROPE_THETA_2 = 10000.0
NORM_EPS = 1e-6
NEG_INF_2 = -1e30
SEL_FORCE = 1e9

W_NSA_Q = NSA_HEADS * NSA_HEAD_DIM
W_NSA_KV = NSA_KV_HEADS * NSA_HEAD_DIM
IN_SPLITS = (W_NSA_Q,
             W_NSA_KV, W_NSA_KV,
             W_NSA_KV, W_NSA_KV,
             W_NSA_KV, W_NSA_KV,
             3 * NSA_HEADS,
             MLA_Q_RANK, MLA_KV_RANK,
             MLA_ROPE_DIM,
             2 * D_MODEL)
IN_WIDTH_2 = sum(IN_SPLITS)
IN_OFFSETS = tuple(int(v) for v in np.cumsum(IN_SPLITS)[:-1])


def rms_norm_2(x, gain):
    xf = x.astype(jnp.float32)
    y = xf * lax.rsqrt(jnp.mean(xf * xf, axis=-1, keepdims=True) + NORM_EPS)
    return (y * gain.astype(jnp.float32)).astype(x.dtype)

def rope(x, pos):
    dim = x.shape[-1]
    half = dim // 2
    inv = ROPE_THETA_2 ** (-jnp.arange(half, dtype=jnp.float32) * 2.0 / dim)
    ang = pos[:, None] * inv[None, :]
    cos = jnp.cos(ang)[None, :, None, :]
    sin = jnp.sin(ang)[None, :, None, :]
    xf = x.astype(jnp.float32)
    x1, x2 = xf[..., :half], xf[..., half:]
    return jnp.concatenate([x1 * cos - x2 * sin, x1 * sin + x2 * cos], axis=-1).astype(x.dtype)

def masked_softmax(s, mask):
    p = jax.nn.softmax(jnp.where(mask, s.astype(jnp.float32), NEG_INF_2), axis=-1)
    return jnp.where(mask, p, 0.0)

def compress(x, pe, w1, w2):
    B, S, G, hd = x.shape
    n_chunks = S // CMP_STRIDE
    r = CMP_BLOCK // CMP_STRIDE
    n_cmp = n_chunks - r + 1
    chunks = x.reshape(B, n_chunks, CMP_STRIDE, G, hd)
    blocks = jnp.concatenate([chunks[:, j:j + n_cmp] for j in range(r)], axis=2)
    blocks = blocks + pe[None, None, :, None, :].astype(x.dtype)
    flat = blocks.transpose(0, 1, 3, 2, 4).reshape(B, n_cmp, G, CMP_BLOCK * hd)
    return jax.nn.silu(flat @ w1) @ w2

def nsa_mixer(q, kc, vc, ks, vs, kw, vw, gates):
    B, S, H, hd = q.shape
    G, R, Cq = NSA_KV_HEADS, NSA_GROUP, NSA_Q_BLOCK
    scale = hd ** -0.5
    n_cmp = kc.shape[1]
    n_sel = S // SEL_BLOCK
    k_top = min(SEL_TOPK, n_sel)
    cmp_start = jnp.arange(n_cmp) * CMP_STRIDE
    cmp_end = cmp_start + CMP_BLOCK - 1
    sel_idx = jnp.arange(n_sel)
    sel_start = sel_idx * SEL_BLOCK
    overlap = ((cmp_start[:, None] <= (sel_start + SEL_BLOCK - 1)[None, :])
               & (cmp_end[:, None] >= sel_start[None, :])).astype(jnp.float32)
    ks_blk = ks.reshape(B, n_sel, SEL_BLOCK, G, hd).transpose(0, 3, 1, 2, 4)
    vs_blk = vs.reshape(B, n_sel, SEL_BLOCK, G, hd).transpose(0, 3, 1, 2, 4)
    kw_pad = jnp.pad(kw, ((0, 0), (WINDOW, 0), (0, 0), (0, 0)))
    vw_pad = jnp.pad(vw, ((0, 0), (WINDOW, 0), (0, 0), (0, 0)))
    b_ix = jnp.arange(B)[:, None, None, None]
    g_ix = jnp.arange(G)[None, :, None, None]

    def block(n):
        q0 = n * Cq
        t = q0 + jnp.arange(Cq)
        qb = lax.dynamic_slice_in_dim(q, q0, Cq, axis=1).reshape(B, Cq, G, R, hd)
        gb = lax.dynamic_slice_in_dim(gates, q0, Cq, axis=1).reshape(B, Cq, G, R, 3)
        s = jnp.einsum('bqgrd,bngd->bgrqn', qb, kc) * scale
        p_cmp = masked_softmax(s, cmp_end[None, :] <= t[:, None])
        o_cmp = jnp.einsum('bgrqn,bngd->bqgrd', p_cmp.astype(vc.dtype), vc)
        imp = jnp.einsum('bgqn,nj->bgqj', p_cmp.sum(axis=2), overlap)
        cur = t // SEL_BLOCK
        forced = ((sel_idx[None, :] == 0) | (sel_idx[None, :] == cur[:, None])
                  | (sel_idx[None, :] == cur[:, None] - 1))
        allowed = sel_start[None, :] <= t[:, None]
        score = jnp.where(forced, SEL_FORCE, jnp.where(allowed, imp, NEG_INF_2))
        _, idx = lax.top_k(score, k_top)
        k_sel = ks_blk[b_ix, g_ix, idx]
        v_sel = vs_blk[b_ix, g_ix, idx]
        kpos = idx[..., None] * SEL_BLOCK + jnp.arange(SEL_BLOCK)
        sel_mask = (kpos <= t[None, None, :, None, None]).reshape(B, G, 1, Cq, k_top * SEL_BLOCK)
        s = jnp.einsum('bqgrd,bgqkld->bgrqkl', qb, k_sel) * scale
        p = masked_softmax(s.reshape(B, G, R, Cq, k_top * SEL_BLOCK), sel_mask)
        p = p.reshape(B, G, R, Cq, k_top, SEL_BLOCK)
        o_slc = jnp.einsum('bgrqkl,bgqkld->bqgrd', p.astype(vs.dtype), v_sel)
        k_w = lax.dynamic_slice_in_dim(kw_pad, q0, Cq + WINDOW, axis=1)
        v_w = lax.dynamic_slice_in_dim(vw_pad, q0, Cq + WINDOW, axis=1)
        wpos = q0 - WINDOW + jnp.arange(Cq + WINDOW)
        win_mask = ((wpos[None, :] <= t[:, None]) & (wpos[None, :] > t[:, None] - WINDOW)
                    & (wpos[None, :] >= 0))
        s = jnp.einsum('bqgrd,bkgd->bgrqk', qb, k_w) * scale
        p = masked_softmax(s, win_mask)
        o_win = jnp.einsum('bgrqk,bkgd->bqgrd', p.astype(vw.dtype), v_w)
        o = gb[..., 0:1] * o_cmp + gb[..., 1:2] * o_slc + gb[..., 2:3] * o_win
        return o.reshape(B, Cq, H * hd)

    out = lax.map(block, jnp.arange(S // Cq))
    return out.transpose(1, 0, 2, 3).reshape(B, S, H * hd)

def mla_mixer(q, k, v):
    B, S, H, _ = q.shape
    scale = MLA_QK_DIM ** -0.5
    kpos = jnp.arange(S)

    def block(n):
        q0 = n * MLA_Q_BLOCK
        t = q0 + jnp.arange(MLA_Q_BLOCK)
        qb = lax.dynamic_slice_in_dim(q, q0, MLA_Q_BLOCK, axis=1)
        s = jnp.einsum('bqhd,bkhd->bhqk', qb, k) * scale
        p = masked_softmax(s, kpos[None, :] <= t[:, None])
        o = jnp.einsum('bhqk,bkhd->bqhd', p.astype(v.dtype), v)
        return o.reshape(B, MLA_Q_BLOCK, H * MLA_V_DIM)

    out = lax.map(block, jnp.arange(S // MLA_Q_BLOCK))
    return out.transpose(1, 0, 2, 3).reshape(B, S, H * MLA_V_DIM)

def hybrid_layer(x, c, pos, w_ada, b_ada, attn_norm, ffn_norm, w_in,
                 nsa_q_norm, nsa_kc_norm, nsa_ks_norm, nsa_kw_norm,
                 cmp_k_pe, cmp_k_w1, cmp_k_w2, cmp_v_pe, cmp_v_w1, cmp_v_w2,
                 mla_cq_norm, mla_ckv_norm, w_uq, w_ukv, mla_q_norm, mla_k_norm,
                 w_o, w_up, w_conv, b_conv, w_down):
    B, S, D = x.shape
    G = NSA_KV_HEADS
    mod = (jax.nn.silu(c) @ w_ada + b_ada)[:, None, :]
    shift_a, scale_a, gate_a, shift_f, scale_f, gate_f = jnp.split(mod, 6, axis=-1)

    h = rms_norm_2(x, attn_norm) * (1.0 + scale_a) + shift_a
    (nq, nkc, nvc, nks, nvs, nkw, nvw, ngate,
     cq, ckv, kr, bgate) = jnp.split(h @ w_in, IN_OFFSETS, axis=-1)

    def heads(t, n):
        return t.reshape(B, S, n, -1)

    q_a = rope(rms_norm_2(heads(nq, NSA_HEADS), nsa_q_norm), pos)
    kc = rms_norm_2(compress(rope(heads(nkc, G), pos), cmp_k_pe, cmp_k_w1, cmp_k_w2), nsa_kc_norm)
    vc = compress(heads(nvc, G), cmp_v_pe, cmp_v_w1, cmp_v_w2)
    ks = rope(rms_norm_2(heads(nks, G), nsa_ks_norm), pos)
    kw = rope(rms_norm_2(heads(nkw, G), nsa_kw_norm), pos)
    g_nsa = jax.nn.sigmoid(heads(ngate, NSA_HEADS))
    o_a = nsa_mixer(q_a, kc, vc, ks, heads(nvs, G), kw, heads(nvw, G), g_nsa)

    q_b = (rms_norm_2(cq, mla_cq_norm) @ w_uq).reshape(B, S, MLA_HEADS, MLA_QK_DIM)
    kv_b = (rms_norm_2(ckv, mla_ckv_norm) @ w_ukv).reshape(B, S, MLA_HEADS, MLA_NOPE_DIM + MLA_V_DIM)
    k_nope, v_b = jnp.split(kv_b, [MLA_NOPE_DIM], axis=-1)
    k_b = jnp.concatenate(
        [k_nope, jnp.broadcast_to(kr[:, :, None, :], (B, S, MLA_HEADS, MLA_ROPE_DIM))], axis=-1)
    q_b = rms_norm_2(q_b, mla_q_norm)
    k_b = rms_norm_2(k_b, mla_k_norm)
    q_b = jnp.concatenate([q_b[..., :MLA_NOPE_DIM], rope(q_b[..., MLA_NOPE_DIM:], pos)], axis=-1)
    k_b = jnp.concatenate([k_b[..., :MLA_NOPE_DIM], rope(k_b[..., MLA_NOPE_DIM:], pos)], axis=-1)
    o_b = mla_mixer(q_b, k_b, v_b)

    g_a, g_b = jnp.split(jax.nn.sigmoid(bgate), 2, axis=-1)
    x = x + gate_a * ((g_a * o_a + g_b * o_b) @ w_o)

    h = rms_norm_2(x, ffn_norm) * (1.0 + scale_f) + shift_f
    u = lax.conv_general_dilated(
        h @ w_up, w_conv[:, None, :], window_strides=(1,), padding=[(CONV_WIDTH - 1, 0)],
        dimension_numbers=('NWC', 'WIO', 'NWC'), feature_group_count=2 * D_FF) + b_conv
    val, gt = jnp.split(u, 2, axis=-1)
    x = x + gate_f * ((jax.nn.silu(gt) * val) @ w_down)
    return x

def second_inputs(seed: int = 0) -> dict:
    key = jax.random.key(seed)
    k = jax.random.split(key, 32)
    L, hd = DEPTH, NSA_HEAD_DIM

    def nrm(kk, shape, scale):
        return jax.random.normal(kk, shape, jnp.float32) * scale

    def gain(kk, n):
        return 1.0 + nrm(kk, (L, n), 0.02)

    return {
        'x': nrm(k[0], (BATCH, SEQ, D_MODEL), 1.0),
        'c': nrm(k[1], (BATCH, D_MODEL), 1.0),
        'w_ada': nrm(k[2], (L, D_MODEL, 6 * D_MODEL), D_MODEL ** -0.5),
        'b_ada': nrm(k[3], (L, 6 * D_MODEL), 0.01),
        'attn_norm': gain(k[4], D_MODEL),
        'ffn_norm': gain(k[5], D_MODEL),
        'w_in': nrm(k[6], (L, D_MODEL, IN_WIDTH_2), D_MODEL ** -0.5),
        'nsa_q_norm': gain(k[7], hd),
        'nsa_kc_norm': gain(k[8], hd),
        'nsa_ks_norm': gain(k[9], hd),
        'nsa_kw_norm': gain(k[10], hd),
        'cmp_k_pe': nrm(k[11], (L, CMP_BLOCK, hd), 0.5),
        'cmp_k_w1': nrm(k[12], (L, CMP_BLOCK * hd, CMP_HIDDEN), (CMP_BLOCK * hd) ** -0.5),
        'cmp_k_w2': nrm(k[13], (L, CMP_HIDDEN, hd), CMP_HIDDEN ** -0.5),
        'cmp_v_pe': nrm(k[14], (L, CMP_BLOCK, hd), 0.5),
        'cmp_v_w1': nrm(k[15], (L, CMP_BLOCK * hd, CMP_HIDDEN), (CMP_BLOCK * hd) ** -0.5),
        'cmp_v_w2': nrm(k[16], (L, CMP_HIDDEN, hd), CMP_HIDDEN ** -0.5),
        'mla_cq_norm': gain(k[17], MLA_Q_RANK),
        'mla_ckv_norm': gain(k[18], MLA_KV_RANK),
        'w_uq': nrm(k[19], (L, MLA_Q_RANK, MLA_HEADS * MLA_QK_DIM), MLA_Q_RANK ** -0.5),
        'w_ukv': nrm(k[20], (L, MLA_KV_RANK, MLA_HEADS * (MLA_NOPE_DIM + MLA_V_DIM)), MLA_KV_RANK ** -0.5),
        'mla_q_norm': gain(k[21], MLA_QK_DIM),
        'mla_k_norm': gain(k[22], MLA_QK_DIM),
        'w_o': nrm(k[23], (L, D_MODEL, D_MODEL), D_MODEL ** -0.5),
        'w_up': nrm(k[24], (L, D_MODEL, 2 * D_FF), D_MODEL ** -0.5),
        'w_conv': nrm(k[25], (L, CONV_WIDTH, 2 * D_FF), CONV_WIDTH ** -0.5),
        'b_conv': nrm(k[26], (L, 2 * D_FF), 0.01),
        'w_down': nrm(k[27], (L, D_FF, D_MODEL), D_FF ** -0.5),
    }

def second_block(x, c, w_ada, b_ada, attn_norm, ffn_norm, w_in,
              nsa_q_norm, nsa_kc_norm, nsa_ks_norm, nsa_kw_norm,
              cmp_k_pe, cmp_k_w1, cmp_k_w2, cmp_v_pe, cmp_v_w1, cmp_v_w2,
              mla_cq_norm, mla_ckv_norm, w_uq, w_ukv, mla_q_norm, mla_k_norm,
              w_o, w_up, w_conv, b_conv, w_down):
    pos = jnp.arange(x.shape[1], dtype=jnp.float32)
    for l in range(DEPTH):
        x = hybrid_layer(x, c, pos, w_ada[l], b_ada[l], attn_norm[l], ffn_norm[l], w_in[l],
                         nsa_q_norm[l], nsa_kc_norm[l], nsa_ks_norm[l], nsa_kw_norm[l],
                         cmp_k_pe[l], cmp_k_w1[l], cmp_k_w2[l], cmp_v_pe[l], cmp_v_w1[l], cmp_v_w2[l],
                         mla_cq_norm[l], mla_ckv_norm[l], w_uq[l], w_ukv[l], mla_q_norm[l], mla_k_norm[l],
                         w_o[l], w_up[l], w_conv[l], b_conv[l], w_down[l])
    return x


def setup_inputs(seed=0):
    out = dict(first_inputs(seed))
    for name, value in second_inputs(seed + 1).items():
        if name != "x":
            out[name + "_2"] = value
    return out


def reference(
    x, c, positions, w_ada, b_ada, norm1_g, w_in, q_norm_g, k_norm_g, rwkv_mu, rwkv_w0, rwkv_w2,
    rwkv_a0, rwkv_a2, rwkv_g2, rwkv_k_k, rwkv_k_a, rwkv_r_k, rwkv_ln_g, rwkv_ln_b, w_proj_moba,
    w_proj_rwkv, w_out, norm2_g, peer_wq, peer_subkeys, peer_u, peer_v, c_2, w_ada_2, b_ada_2,
    attn_norm_2, ffn_norm_2, w_in_2, nsa_q_norm_2, nsa_kc_norm_2, nsa_ks_norm_2, nsa_kw_norm_2,
    cmp_k_pe_2, cmp_k_w1_2, cmp_k_w2_2, cmp_v_pe_2, cmp_v_w1_2, cmp_v_w2_2, mla_cq_norm_2,
    mla_ckv_norm_2, w_uq_2, w_ukv_2, mla_q_norm_2, mla_k_norm_2, w_o_2, w_up_2, w_conv_2,
    b_conv_2, w_down_2,
):
    x = first_block(
        x, c, positions, w_ada, b_ada, norm1_g, w_in, q_norm_g, k_norm_g, rwkv_mu, rwkv_w0,
        rwkv_w2, rwkv_a0, rwkv_a2, rwkv_g2, rwkv_k_k, rwkv_k_a, rwkv_r_k, rwkv_ln_g, rwkv_ln_b,
        w_proj_moba, w_proj_rwkv, w_out, norm2_g, peer_wq, peer_subkeys, peer_u, peer_v,
    )
    return second_block(
        x, c_2, w_ada_2, b_ada_2, attn_norm_2, ffn_norm_2, w_in_2, nsa_q_norm_2, nsa_kc_norm_2,
        nsa_ks_norm_2, nsa_kw_norm_2, cmp_k_pe_2, cmp_k_w1_2, cmp_k_w2_2, cmp_v_pe_2,
        cmp_v_w1_2, cmp_v_w2_2, mla_cq_norm_2, mla_ckv_norm_2, w_uq_2, w_ukv_2, mla_q_norm_2,
        mla_k_norm_2, w_o_2, w_up_2, w_conv_2, b_conv_2, w_down_2,
    )


_drawn_inputs = setup_inputs


def setup_inputs(seed=0):
    import zlib

    import numpy as np

    out = dict(_drawn_inputs(seed))
    spreads = {}
    factors = {'b_ada': 3.548,
     'norm1_g': 5.045,
     'q_norm_g': 8.0,
     'k_norm_g': 8.0,
     'rwkv_w2': 6.459,
     'rwkv_k_k': 32.446,
     'rwkv_k_a': 4.026,
     'rwkv_ln_g': 22.42,
     'rwkv_ln_b': 58.282,
     'norm2_g': 3.846,
     'b_ada_2': 3.708,
     'attn_norm_2': 8.0,
     'ffn_norm_2': 14.9,
     'nsa_q_norm_2': 8.0,
     'nsa_kc_norm_2': 91.175,
     'nsa_ks_norm_2': 8.0,
     'nsa_kw_norm_2': 8.0,
     'cmp_k_pe_2': 5.174,
     'mla_cq_norm_2': 8.0,
     'mla_ckv_norm_2': 8.0,
     'mla_q_norm_2': 8.0,
     'mla_k_norm_2': 8.0,
     'b_conv_2': 33.562,
     'cmp_v_pe_2': 6.534}
    for name, (base, spread) in spreads.items():
        noise = np.random.default_rng([zlib.crc32(name.encode()), seed]).standard_normal(out[name].shape)
        drawn = base * np.exp(spread * noise) if base else spread * noise
        out[name] = __import__('jax').numpy.asarray(drawn.astype(out[name].dtype))
    for name, factor in factors.items():
        out[name] = (out[name] * factor).astype(out[name].dtype)
    return out
```

```python
from contextlib import ExitStack

import numpy as np

import concourse.bass as bass
from concourse import mybir

F32 = mybir.dt.float32
I32 = mybir.dt.int32
U32 = mybir.dt.uint32
ALU = mybir.AluOpType
ACT = mybir.ActivationFunctionType
AX = mybir.AxisListType.X

P = 128
S = 256
D = 1024
KT = D // P
TT = S // P
NEG = -1e30

MH, MD = 8, 64
RN = 64
CH = 64
NCH = S // CH
PAIRS = 4
UN = PAIRS * NCH
PH, PK = 8, 16
NK = 128
GN_EPS = 64e-5
RMS_EPS = 1e-6

NH, NG = 8, 2
CB, CS = 32, 16
NCMP = S // CS - CB // CS + 1
MLH = 8
FT = 2816 // P

PHASES = [("w_in", 42), ("proj", 8), ("w_out", 8), ("wq", 16), ("peer", 2 * NK),
          ("w_in2", 43), ("cmp_k", 8), ("cmp_v", 8), ("cmp_w2", 1), ("uq", 6), ("uk", 4), ("uv", 4),
          ("w_o", 8), ("ffn", 3 * FT)]
FIRST = {}
_n = 0
for _name, _count in PHASES:
    FIRST[_name] = _n
    _n += _count
TILES = _n
COUNT = dict(PHASES)
WIDTH = {"cmp_w2": 512, "uq": 768, "uk": 512, "uv": 512}
RINGED = ["w_in", "proj", "w_out", "wq", "w_in2", "uq", "uk", "uv", "w_o"]
RING0 = {}
_n = 0
for _name in RINGED:
    RING0[_name] = _n
    _n += COUNT[_name]
SLOTS = 6
BANKS = 3
ADA = 12
ASLOTS = 4

COLS = [("c", 8), ("c_2", 8), ("norm1_g", 8), ("norm2_g", 8), ("attn_norm_2", 8), ("ffn_norm_2", 8),
        ("b_ada", 48), ("b_ada_2", 48), ("rwkv_mu", 14), ("rwkv_w0", 4), ("rwkv_a0", 4), ("rwkv_k_k", 4),
        ("rwkv_k_a", 4), ("rwkv_r_k", 4), ("rwkv_ln_g", 4), ("rwkv_ln_b", 4), ("q_norm_g", 1), ("k_norm_g", 1),
        ("nsa_q_norm_2", 1), ("nsa_ks_norm_2", 1), ("nsa_kw_norm_2", 1), ("nsa_kc_norm_2", 1),
        ("mla_cq_norm_2", 3), ("mla_ckv_norm_2", 2), ("mla_q_nope", 1), ("mla_q_rope", 1),
        ("mla_k_nope", 1), ("mla_k_rope", 1), ("cmp_k_pe", CB), ("cmp_v_pe", CB), ("conv", FT * 8),
        ("rope_inv", 1), ("eps", 1), ("gn_eps", 1)]
COL = {}
_n = 0
for _name, _count in COLS:
    COL[_name] = _n
    _n += _count
NCOL = _n

KEEP = [("ident", 128), ("ones", 128), ("blk64", 128)]
KEEP_AT = {n: 128 * i for i, (n, _) in enumerate(KEEP)}
NKEEP = 384
CONST1 = [("g_mask", 512), ("mL", 6 * 128), ("mT1", 128), ("causal", 384), ("rot_moba", 128)]
CONST2 = [("rot_nsa", 128), ("rot_mla", 128), ("half0", 128), ("half1", 128), ("nsa_cos", 256), ("nsa_sin", 256),
          ("mla_cos", 256), ("mla_sin", 256), ("causal", 384), ("cmp_mask", TT * NCMP), ("cmp_valid", TT)]


def offsets(parts):
    at, n = {}, 0
    for name, count in parts:
        at[name] = n
        n += count
    return at, n


C1_AT, NC1 = offsets(CONST1)
C2_AT, NC2 = offsets(CONST2)


def shape_constants():
    p, f = np.arange(128)[:, None], np.arange(128)[None, :]
    same = (p // 64) == (f // 64)
    keep = [np.eye(128), np.ones((128, 128)), same]
    strict, incl = same & (p < f), same & (p <= f)
    g_mask = np.concatenate([strict, incl, strict, incl], 1)
    level = [(p // (2 * b) == f // (2 * b)) & (p // b % 2 == 1) & (f // b % 2 == 0) for b in (1, 2, 4, 8, 16, 32)]
    q = np.arange(128)[:, None]
    causal = np.concatenate([np.where(np.arange(128)[None] <= q, 0, NEG),
                             np.where(np.arange(256)[None] <= q + 128, 0, NEG)], 1)

    def rotation(width, half):
        r = np.zeros((128, 128))
        for base in range(0, 128, width):
            for i in range(half):
                r[base + half + i, base + i] = -1.0
                r[base + i, base + half + i] = 1.0
        return r

    one = [g_mask, np.concatenate(level, 1), level[0].T, causal, rotation(MD, MD // 8)]

    def table(width):
        half = width // 2
        inv = (np.float32(10000.0) ** (-np.arange(half, dtype=np.float32) * np.float32(2.0) / np.float32(width)))
        ang = np.arange(S, dtype=np.float32)[None, :] * inv.astype(np.float32)[:, None]
        ang = np.tile(ang, (128 // half, 1))
        return [np.cos(ang), np.sin(ang)]

    t = np.arange(S).reshape(TT, 128).T[:, :, None]
    seen = (np.arange(NCMP) * CS + CB - 1)[None, None, :] <= t
    two = [rotation(128, 64), rotation(64, 32), np.tile(p < 64, (1, 128)), np.tile(p >= 64, (1, 128)),
           *table(128), *table(64), causal, np.where(seen, 0, NEG).reshape(128, -1), seen.any(-1)]
    cat = lambda parts: np.ascontiguousarray(np.concatenate([np.asarray(a, np.float32) for a in parts], 1))
    return cat(keep), cat(one), cat(two)


ARENA = 40960


def region(arena, start, parts):
    out, at = {}, start
    for name, count in parts:
        out[name] = arena[:, at:at + count]
        at += count
    assert at <= ARENA, (start, at)
    return out, at


def build_layer_pair(nc, a):
    with ExitStack() as ctx:
        def sb(name, shape, dt=F32):
            return ctx.enter_context(nc.sbuf_tensor(name, shape, dt))

        def sem(name):
            return ctx.enter_context(nc.semaphore(name))

        wring = sb("wring", [P, SLOTS, D])
        hT = sb("hT", [P, KT, S])
        xn = sb("xn", [P, KT, S])
        cols = sb("cols", [P, NCOL])
        keep = sb("keep", [P, NKEEP])
        mod = sb("mod", [P, ADA * KT])
        gsc = sb("gsc", [P, 4, KT])
        csil = sb("csil", [P, 2 * KT])
        arena = sb("arena", [P, ARENA])
        bank = [ctx.enter_context(nc.psum_tensor(f"bank{i}", [P, 512], F32)) for i in range(8)]

        ident, ones, blk64 = (keep[:, KEEP_AT[n]:KEEP_AT[n] + 128] for n in ("ident", "ones", "blk64"))

        def col(name, i=0, n=1):
            return cols[:, COL[name] + i:COL[name] + i + n]

        def modc(vec, m, n=1):
            return mod[:, vec * KT + m:vec * KT + m + n]

        def wide(ap, n):
            return ap.unsqueeze(2).to_broadcast([ap.shape[0], ap.shape[1], n])

        def over(ap, n):
            return ap.unsqueeze(1).to_broadcast([ap.shape[0], n, ap.shape[1]])

        r0, _ = region(arena, 0, [("zs", 3584), ("gates", 4096), ("g_rw", 1024), ("Pc", 1024), ("om", 1024),
                                  ("y", 1024), ("AR", 4096), ("G3", 6144), ("LT", 2048), ("BKV", 6144),
                                  ("TTm", 2048), ("BD", 6144), ("const1", NC1)])
        zs = r0["zs"].rearrange("p (m t) -> p m t", m=14)
        gates = r0["gates"].rearrange("p (m t) -> p m t", m=16)
        om = r0["om"].rearrange("p (m t) -> p m t", m=4)
        c1 = {n: r0["const1"][:, C1_AT[n]:C1_AT[n] + k] for n, k in CONST1}
        rA, _ = region(arena, 11776, [("qk", 2048), ("vtok", 1024), ("_", 1024), ("acc", ADA * D), ("aring", ASLOTS * D),
                                      ("zraw", 14 * 257), ("pos", 256)])
        sq0 = arena[:, 3584:3584 + 2048].rearrange("p (m t) -> p m t", m=KT)
        qk = rA["qk"].rearrange("p (m t) -> p m t", m=8)
        vtok = rA["vtok"].rearrange("p (b f) -> p b f", b=TT)
        acc = rA["acc"].rearrange("p (c n) -> p c n", c=ADA)
        aring = rA["aring"].rearrange("p (s n) -> p s n", s=ASLOTS)
        zraw = rA["zraw"].rearrange("p (m t) -> p m t", m=14)
        posi = rA["pos"].bitcast(I32)
        rM, _ = region(arena, 15872, [("sq", 2048), ("rt", 2048), ("qn", 2048), ("t1", 2048), ("kz", 2048),
                                      ("cos", 256), ("sin", 256), ("ang", 256), ("kf", 256)])
        rR, _ = region(arena, 15872, [(n, 1024) for n in
                                      ("lw", "cum", "cml", "Pinv", "Pprev", "kk", "av", "sqk", "rtk", "t1", "rmask")]
                       + [("lora", 512)])
        Pc = r0["Pc"]
        g_rw = r0["g_rw"].rearrange("p (m t) -> p m t", m=4)
        yb = r0["y"]
        ARt = r0["AR"].rearrange("p (u k f) -> p u k f", u=UN, k=2)
        G3 = r0["G3"].rearrange("p (u k f) -> p u k f", u=UN, k=3)
        LT = r0["LT"].rearrange("p (u f) -> p u f", u=UN)
        BKV = r0["BKV"].rearrange("p (u k f) -> p u k f", u=UN, k=3)
        TTm = r0["TTm"].rearrange("p (u f) -> p u f", u=UN)
        BD = r0["BD"].rearrange("p (k u f) -> p k u f", k=3, u=UN)
        Tm = r0["BD"][:, 0:2048].rearrange("p (u f) -> p u f", u=UN)
        Xm = r0["BD"][:, 2048:4096].rearrange("p (u f) -> p u f", u=UN)
        st = r0["LT"][:, 0:1024].rearrange("p (b q f) -> p b q f", b=2, q=PAIRS)
        usb = r0["LT"][:, 1024:1536].rearrange("p (q f) -> p q f", q=PAIRS)
        sasb = r0["LT"][:, 1536:2048].rearrange("p (q f) -> p q f", q=PAIRS)
        rP, _ = region(arena, 15872, [("yc", 1024), ("ysq", 1024), ("rt", 1024), ("rk", 1024), ("bon", 1024)])
        mix1 = r0["AR"][:, 0:2048].rearrange("p (m t) -> p m t", m=KT)
        mixt = r0["AR"][:, 2048:3072].rearrange("p (b k t) -> p b k t", b=2, k=2)
        att1, _ = region(arena, 28160, [("sm", 768), ("pe", 1152), ("pt", 768), ("mx", 12), ("sm2", 24)])

        G = arena[:, 0:32768].rearrange("p (t j) -> p t j", t=S)
        rG, _ = region(arena, 32768, [("T3", 768), ("A8", 2048), ("B8", 2048), ("ge", 768), ("W", 768),
                                      ("iota", 128), ("iotai", 128)])
        T3 = rG["T3"].rearrange("p (k t) -> p k t", k=3)
        A8 = rG["A8"].rearrange("p (b t i) -> p b t i", b=2, t=8)
        B8 = rG["B8"].rearrange("p (b t i) -> p b t i", b=2, t=8)
        ge = rG["ge"].rearrange("p (b t) -> p b t", b=3)
        Wj = rG["W"].rearrange("p (b t) -> p b t", b=3)
        NR = TT * 2 * PH
        NQ = TT * PH
        rK, _ = region(arena, 0, [("qp", 4096), ("sc", 4096), ("subk", 2048), ("scr", 256), ("tv", 512), ("ti", 512),
                                  ("tif", 512), ("cand", 4096), ("best", 256), ("bi", 256), ("ba", 512),
                                  ("baf", 512), ("big", 4096), ("pick", 512), ("gate", 256), ("gsum", 32),
                                  ("scr2", 256), ("sq", 2048)])
        qp = rK["qp"].rearrange("p (m t) -> p m t", m=16)
        sc = rK["sc"].rearrange("p (r n) -> p r n", r=NR)
        subk = rK["subk"].rearrange("p (r n) -> p r n", r=16)
        tv = rK["tv"].rearrange("p (r k) -> p r k", r=NR)
        ti = rK["ti"].bitcast(U32).rearrange("p (r k) -> p r k", r=NR)
        tif = rK["tif"].rearrange("p (r k) -> p r k", r=NR)
        cand = rK["cand"].rearrange("p (r x) -> p r x", r=NQ)
        best = rK["best"].rearrange("p (r k) -> p r k", r=NQ)
        bi = rK["bi"].bitcast(U32).rearrange("p (r k) -> p r k", r=NQ)
        ba = rK["ba"].bitcast(U32).rearrange("p (h r) -> p h r", h=2)
        baf = rK["baf"].rearrange("p (h r) -> p h r", h=2)
        pick = rK["pick"].rearrange("p (h r) -> p h r", h=2)
        gate = rK["gate"].rearrange("p (r k) -> p r k", r=NQ)

        r2, _ = region(arena, 0, [("F2", 22 * 256), ("bg", 4096), ("vs", 512), ("vw", 512), ("vb", 2048),
                                  ("gt", 48), ("rs", 3072), ("sq", 3584), ("rot", 3584), ("qb", 3072), ("kb", 2048),
                                  ("XP", 2 * CB * 30), ("const2", NC2), ("hid", 256), ("hidT", 64), ("cmt", 512),
                                  ("kcT", 32), ("kst", 8), ("oA", 2048), ("oB", 2048), ("at", 2736)])
        F2 = r2["F2"].rearrange("p (m t) -> p m t", m=22)
        bg = r2["bg"].rearrange("p (m t) -> p m t", m=16)
        vs2 = r2["vs"].rearrange("p (b f) -> p b f", b=TT)
        vw2 = r2["vw"].rearrange("p (b f) -> p b f", b=TT)
        vb = r2["vb"].rearrange("p (b h f) -> p b h f", b=TT, h=MLH)
        gt2 = r2["gt"].rearrange("p (b k) -> p b k", b=TT)
        rs12 = r2["rs"].rearrange("p (m t) -> p m t", m=12)
        sq14 = r2["sq"].rearrange("p (m t) -> p m t", m=14)
        ro14 = r2["rot"].rearrange("p (m t) -> p m t", m=14)
        qb = r2["qb"].rearrange("p (m t) -> p m t", m=12)
        kb = r2["kb"].rearrange("p (m t) -> p m t", m=8)
        XP = r2["XP"].rearrange("p (v l n) -> p v l n", v=2, l=CB)
        c2 = {n: r2["const2"][:, C2_AT[n]:C2_AT[n] + k] for n, k in CONST2}
        oA = r2["oA"].rearrange("p (m t) -> p m t", m=NH)
        oB = r2["oB"].rearrange("p (m t) -> p m t", m=NH)
        att2, _ = region(r2["at"], 0, [("sm", 768), ("pe", 1152), ("pt", 768), ("mx", 12), ("sm2", 24)])
        sq3 = r2["sq"][:, 0:2048].rearrange("p (m t) -> p m t", m=KT)
        rF, _ = region(arena, 0, [("z", 2 * 2 * 258), ("u", 2 * 2 * 256), ("sg", 512), ("W", 512), ("sq", 2048)])
        zf = rF["z"].rearrange("p (b k t) -> p b k t", b=2, k=2)
        uf = rF["u"].rearrange("p (b k t) -> p b k t", b=2, k=2)
        sgf = rF["sg"].rearrange("p (b t) -> p b t", b=2)
        Wf = rF["W"].rearrange("p (b t) -> p b t", b=2)

        loaded = sem("loaded")
        c1_loaded, subk_loaded, c2_loaded = sem("c1_loaded"), sem("subk_loaded"), sem("c2_loaded")
        landed = [sem(f"landed{i}") for i in range(SLOTS)]
        tile_done = sem("tile_done")
        ring_free = sem("ring_free")
        alanded = [sem(f"alanded{i}") for i in range(ASLOTS)]
        ada_used = sem("ada_used")
        stored = sem("stored")
        vdone = sem("vdone")
        gdone = sem("gdone")
        sq_ready, ss_ready, rt_ready, xn_ready = sem("sq_ready"), sem("ss_ready"), sem("rt_ready"), sem("xn_ready")
        csil_ready = sem("csil_ready")
        ada_turned, ada_read = sem("ada_turned"), sem("ada_read")

        slot_of = lambda n: n % SLOTS
        count_at = lambda n: 16 * (n // SLOTS + 1)

        class Steps:

            def __init__(self, eng, s):
                self.eng, self.s, self.n = eng, s, 0

            def did(self, ins):
                ins.then_inc(self.s, 1)
                self.n += 1
                return self.n

            def settle(self):
                self.eng.wait_ge(self.s, self.n)

            def then(self, ins):
                self.did(ins)
                self.settle()

        def blocks(slot, k, width=128, at=0):
            return wring[:, slot, at + k * width:at + (k + 1) * width]

        def ring_tiles(pe, name, body):
            first, count, ring0 = FIRST[name], COUNT[name], RING0[name]

            def one(slot, bk, landing, ring_n):
                pe.wait_ge(landed[slot], landing)
                if ring_n is not None:
                    pe.wait_ge(ring_free, ring_n)
                body(slot, bank[bk]).then_inc(tile_done, 1)

            rounds = count // SLOTS if count >= 2 * SLOTS else 0
            n = 0
            if rounds and ring0 < BANKS:
                for u in range(SLOTS):
                    free = ring0 + u - BANKS + 1
                    one(slot_of(first + u), (ring0 + u) % BANKS, count_at(first + u), free if free > 0 else None)
                n, rounds = SLOTS, rounds - 1
            if rounds:
                with pe.Fori(0, rounds) as i:
                    for u in range(SLOTS):
                        t = first + n + u
                        one(slot_of(t), (ring0 + n + u) % BANKS, 16 * i + count_at(t),
                            SLOTS * i + (ring0 + n + u - BANKS + 1))
                n += rounds * SLOTS
            for k in range(n, count):
                one(slot_of(first + k), (ring0 + k) % BANKS, count_at(first + k), ring0 + k - BANKS + 1)

        def matmul8(pe, out, slot, x=None):
            x = xn if x is None else x
            for k in range(KT):
                mm = pe.matmul(out, blocks(slot, k), x[:, k, :], start=(k == 0), stop=(k == KT - 1))
            return mm

        def matmul8_tokens(pe, bk, slot, width=128):
            for b in range(TT):
                for k in range(KT):
                    mm = pe.matmul(bk[:, b * width:(b + 1) * width], xn[:, k, b * 128:(b + 1) * 128],
                                   blocks(slot, k), start=(k == 0), stop=(k == KT - 1))
            return mm

        def tile_wait(eng, name, k):
            eng.wait_ge(tile_done, FIRST[name] + k + 1)

        def ring_bank(name, k):
            return bank[(RING0[name] + k) % BANKS]

        def norm_pe(pe, n, sq):
            pe.wait_ge(sq_ready, n + 1)
            for k in range(KT):
                mm = pe.matmul(bank[3][:, 0:S], ones, sq[:, k, :], start=(k == 0), stop=(k == KT - 1))
            mm.then_inc(ss_ready, 1)

        def norm_act(act, n, rt):
            act.wait_ge(ss_ready, n + 1)
            act.activation(rt, bank[3][:, 0:S], ACT.Sqrt, scale=1.0 / D, bias=col("eps")).then_inc(rt_ready, 1)

        def norm_squares(dve, sq):
            dve.tensor_tensor(sq[:, :, :], hT[:, :, :], hT[:, :, :], ALU.mult).then_inc(sq_ready, 1)

        def norm_apply(dve, v, n, rt, shift):
            dve.wait_ge(rt_ready, n + 1)
            v.then(dve.reciprocal(rt, rt))
            v.then(dve.tensor_tensor(xn[:, :, :], hT[:, :, :], over(rt, KT), ALU.mult))
            for k in range(KT):
                ins = dve.tensor_scalar(xn[:, k, :], xn[:, k, :], gsc[:, n, k:k + 1], modc(shift, k),
                                        ALU.mult, ALU.add)
            ins.then_inc(xn_ready, 1)

        nsq = [sq0, rK["sq"].rearrange("p (m t) -> p m t", m=KT), sq3, rF["sq"].rearrange("p (m t) -> p m t", m=KT)]
        rtn = [arena[:, 5632:5888], arena[:, 25600:25856], r2["rot"][:, 0:256], rF["sg"][:, 0:256]]

        a_score, a_max, a_exp, a_rec = sem("a_score"), sem("a_max"), sem("a_exp"), sem("a_rec")
        a_prob, a_turn, a_pt, a_out, a_free = (sem("a_prob"), sem("a_turn"), sem("a_pt"), sem("a_out"), sem("a_free"))
        CAUSAL = [(0, 128), (128, 256)]
        CMP = [(0, NCMP), (NCMP, NCMP)]

        def spans(job):
            return CAUSAL if job["kind"] == "causal" else CMP

        def turns(jobs, *stages):
            first, last = jobs[0]["n"], jobs[-1]["n"]
            for t in range(first - 3, last + 3):
                for ahead, stage in stages:
                    if first <= t + ahead <= last:
                        stage(jobs[t + ahead - first])

        def att_pe(pe, jobs):
            def scores(j):
                n, bk = j["n"], bank[j["n"] % 2]
                if n >= 2:
                    pe.wait_ge(a_max, n - 1)
                for b, (at, w) in enumerate(spans(j)):
                    for i, (q, k) in enumerate(zip(j["q"], j["k"])):
                        mm = pe.matmul(bk[:, at:at + w], q[:, b * 128:(b + 1) * 128], k[:, 0:w],
                                       start=(i == 0), stop=(i == len(j["q"]) - 1))
                mm.then_inc(a_score, 1)

            def turn(j):
                n = j["n"]
                pe.wait_ge(a_prob, n + 1)
                if n >= 2:
                    pe.wait_ge(a_pt, n - 1)
                p = j["buf"]["pe"][:, (n % 3) * 384:(n % 3) * 384 + 384]
                bk = bank[3 + n % 2]
                if j["kind"] == "causal":
                    for k in range(3):
                        mm = pe.transpose(bk[:, k * 128:(k + 1) * 128], p[:, k * 128:(k + 1) * 128], ident)
                else:
                    for b in range(TT):
                        mm = pe.transpose(bk[0:NCMP, b * 128:(b + 1) * 128], p[:, b * NCMP:(b + 1) * NCMP], ident)
                mm.then_inc(a_turn, 1)

            def values(j):
                n, g = j["n"], j["group"]
                pe.wait_ge(a_pt, n + 1)
                if j["first"] and g >= 2:
                    pe.wait_ge(a_free, g - 1)
                pt = j["buf"]["pt"][:, (n % 2) * 384:(n % 2) * 384 + 384]
                out = bank[6 + g % 2][0:j["M"], 0:S]
                if j["kind"] == "causal":
                    pe.matmul(out, j["v"](0), pt[:, 0:256], start=j["first"], stop=False)
                    mm = pe.matmul(out[:, 128:256], j["v"](1), pt[:, 256:384], start=False, stop=j["last"])
                else:
                    mm = pe.matmul(out, j["v"](0), pt[0:NCMP, 0:256], start=j["first"], stop=j["last"])
                mm.then_inc(a_out, 1)

            turns(jobs, (3, scores), (0, turn), (-1, values))

        def att_act(act, jobs):
            def exps(j):
                n, buf = j["n"], j["buf"]
                act.wait_ge(a_max, n + 1)
                if n >= 3:
                    act.wait_ge(a_turn, n - 2)
                o, m = (n % 2) * 384, (n % 3) * 384
                for b, (at, w) in enumerate(spans(j)):
                    ins = act.activation(buf["pe"][:, m + at:m + at + w], buf["sm"][:, o + at:o + at + w], ACT.Exp,
                                         bias=buf["mx"][:, 4 * (n % 3) + 2 + b:4 * (n % 3) + 3 + b],
                                         accum_out=buf["sm2"][:, 8 * (n % 3) + b:8 * (n % 3) + b + 1])
                ins.then_inc(a_exp, 1)

            def copy(j):
                n, buf = j["n"], j["buf"]
                act.wait_ge(a_turn, n + 1)
                if n >= 2:
                    act.wait_ge(a_out, n - 1)
                o = (n % 2) * 384
                if j["kind"] == "causal":
                    ins = act.copy(buf["pt"][:, o:o + 384], bank[3 + n % 2][:, 0:384])
                else:
                    ins = act.copy(buf["pt"][0:NCMP, o:o + 256], bank[3 + n % 2][0:NCMP, 0:256])
                ins.then_inc(a_pt, 1)

            turns(jobs, (2, exps), (0, copy))

        def att_dve(dve, v, jobs):
            def maxima(j):
                n, buf, mask = j["n"], j["buf"], j["masks"][j["kind"]]
                dve.wait_ge(a_score, n + 1)
                if n >= 2:
                    dve.wait_ge(a_exp, n - 1)
                o, mx = (n % 2) * 384, buf["mx"][:, 4 * (n % 3):4 * (n % 3) + 4]
                for b, (at, w) in enumerate(spans(j)):
                    ins = dve.tensor_tensor_reduce(buf["sm"][:, o + at:o + at + w], bank[n % 2][:, at:at + w],
                                                   mask[:, at:at + w], j["scale"], -3e38,
                                                   ALU.add, ALU.max, mx[:, b:b + 1])
                v.then(ins)
                dve.tensor_scalar(mx[:, 2:4], mx[:, 0:2], -1.0, None, ALU.mult).then_inc(a_max, 1)

            def reciprocals(j):
                n = j["n"]
                dve.wait_ge(a_exp, n + 1)
                if n >= 3:
                    dve.wait_ge(a_prob, n - 2)
                s = j["buf"]["sm2"][:, 8 * (n % 3):8 * (n % 3) + 8]
                if j["gate"] is None:
                    dve.reciprocal(s[:, 4:6], s[:, 0:2]).then_inc(a_rec, 1)
                else:
                    v.then(dve.reciprocal(s[:, 2:4], s[:, 0:2]))
                    dve.tensor_tensor(s[:, 4:6], s[:, 2:4], j["gate"], ALU.mult).then_inc(a_rec, 1)

            def output(j):
                if j["last"]:
                    dve.wait_ge(a_out, j["n"] + 1)
                    dve.tensor_copy(j["out"], bank[6 + j["group"] % 2][j["rows"], 0:S]).then_inc(a_free, 1)

            turns(jobs, (3, maxima), (1, reciprocals), (-2, output))

        def att_pool(pool, jobs):
            for j in jobs:
                n, buf = j["n"], j["buf"]
                pool.wait_ge(a_rec, n + 1)
                o = (n % 3) * 384
                for b, (at, w) in enumerate(spans(j)):
                    p = buf["pe"][:, o + at:o + at + w]
                    f = 8 * (n % 3) + 4 + b
                    ins = pool.tensor_scalar(p, p, buf["sm2"][:, f:f + 1], None, ALU.mult)
                ins.then_inc(a_prob, 1)

        all_rows, lo, hi = slice(0, 128), slice(0, 64), slice(64, 128)
        kz = rM["kz"].rearrange("p (h t) -> p h t", h=MH)
        qr = rM["qn"].rearrange("p (m t) -> p m t", m=8)
        moba_jobs = [dict(n=h, group=h, first=True, last=True, kind="causal", scale=MD ** -0.5, gate=None,
                          q=[qr[:, h // 2, :]], k=[kz[:, h, :]], M=128, buf=att1,
                          v=lambda b, h=h: vtok[:, b, (h // 2) * 128:(h // 2) * 128 + 128],
                          rows=(lo, hi)[h % 2], out=om[(lo, hi)[h % 2], h // 2, :], masks=dict(causal=c1["causal"]))
                     for h in range(MH)]

        def sp_loads(sp):
            for dst, src in ((cols[:, :], a["cols"]), (keep[:, :], a["keep"]), (hT[:, :, :], a["xT"]),
                             (posi, a["positions"].to_broadcast([P, S]))):
                sp.dma_start(dst, src).then_inc(loaded, 16)
            sp.dma_start(r0["const1"], a["const1"]).then_inc(c1_loaded, 16)

        def sp_ada(sp):
            for t in range(ASLOTS):
                sp.dma_start(aring[:, t, :], a["ada"][t]).then_inc(alanded[t], 16)
            for t in range(ASLOTS, 2 * KT):
                sp.wait_ge(ada_used, t - ASLOTS + 1)
                sp.dma_start(aring[:, t % ASLOTS, :], a["ada"][t]).then_inc(alanded[t % ASLOTS], 16)

        def sp_w_in(sp):
            rest = 2 * KT

            def ada(k, i, step):
                n = rest + k
                sp.wait_ge(ada_used, step * i + (n - ASLOTS + 1))
                sp.dma_start(aring[:, n % ASLOTS, :], a["ada"][step * i + n]).then_inc(alanded[n % ASLOTS], 16)

            for t in range(SLOTS):
                sp.dma_start(wring[:, t, :], a["w"][t]).then_inc(landed[t], 16)
            rounds = COUNT["w_in"] // SLOTS - 1
            with sp.Fori(0, rounds) as i:
                for u in range(SLOTS):
                    sp.wait_ge(tile_done, SLOTS * i + (u + 1))
                    sp.dma_start(wring[:, u, :], a["w"][SLOTS * i + (SLOTS + u)]).then_inc(landed[u], 16)
                    ada(2 * u, i, 2 * SLOTS)
                    ada(2 * u + 1, i, 2 * SLOTS)
            for k in range(2 * SLOTS * rounds, ADA * KT - rest):
                ada(k, 0, 0)

        def sp_weights(sp, name, skip=0):
            first, count, w = FIRST[name] + skip, COUNT[name] - skip, WIDTH.get(name, D)

            def one(slot, n, freed):
                sp.wait_ge(tile_done, freed)
                sp.dma_start(wring[:, slot, 0:w], a["w"][n][:, 0:w]).then_inc(landed[slot], 16)

            rounds = count // SLOTS if count >= 2 * SLOTS else 0
            if rounds:
                with sp.Fori(0, rounds) as i:
                    for u in range(SLOTS):
                        one(slot_of(first + u), SLOTS * i + (first + u), SLOTS * i + (first + u - SLOTS + 1))
            for k in range(rounds * SLOTS, count):
                one(slot_of(first + k), first + k, first + k - SLOTS + 1)

        def act_head(act):
            act.wait_ge(loaded, 64)
            act.activation(csil[:, :], cols[:, 0:2 * KT], ACT.Silu).then_inc(csil_ready, 1)

        def dve_ada(dve, lo_c, hi_c, cofs):
            def chunk(c, t0, land):
                for k in range(KT):
                    dve.wait_ge(alanded[k % ASLOTS], land + 16 * (k // ASLOTS))
                    src = aring[:, k % ASLOTS, :]
                    if k == 0:
                        ins = dve.tensor_scalar(acc[:, c, :], src, csil[:, cofs:cofs + 1], None, ALU.mult)
                    else:
                        dve.wait_ge(ada_used, t0 + k)
                        ins = dve.scalar_tensor_tensor(acc[:, c, :], src, csil[:, cofs + k:cofs + k + 1],
                                                       acc[:, c, :], ALU.mult, ALU.add)
                    ins.then_inc(ada_used, 1)
            with dve.Fori(lo_c, hi_c) as c:
                chunk(c, KT * c, 32 * c + 16)

        def pe_ada(pe, c0, c1_):
            for c in range(c0, c1_):
                if c in (0, 2):
                    pe.wait_ge(ada_used, KT * c1_)
                for h in range(2):
                    i = 2 * c + h
                    bk = bank[4 + i % 2]
                    if i >= 2:
                        pe.wait_ge(ada_read, i - 1)
                    for m in range(4):
                        mm = pe.transpose(bk[:, m * 128:(m + 1) * 128],
                                          acc[:, c, (4 * h + m) * 128:(4 * h + m + 1) * 128], ident)
                    mm.then_inc(ada_turned, 1)

        def dve_ada_sum(dve, v, c0, c1_):
            for i in range(2 * c0, 2 * c1_):
                dve.wait_ge(ada_turned, i + 1)
                ins = dve.tensor_reduce(mod[:, 4 * i:4 * i + 4], bank[4 + i % 2][:, :].rearrange("p (m n) -> p m n", m=4),
                                        AX, ALU.add)
                ins.then_inc(ada_read, 1)
            dve.wait_ge(ada_read, 2 * c1_)
            lo_m, hi_m = KT * c0, KT * c1_
            v.then(dve.tensor_tensor(mod[:, lo_m:hi_m], mod[:, lo_m:hi_m],
                                     cols[:, COL["b_ada"] + lo_m:COL["b_ada"] + hi_m], ALU.add))

        def dve_gsc(dve, v, n):
            gain = ("norm1_g", "norm2_g", "attn_norm_2", "ffn_norm_2")[n]
            v.then(dve.scalar_tensor_tensor(gsc[:, n, :], modc(3 * n + 1, 0, KT), 1.0, col(gain, 0, KT),
                                            ALU.add, ALU.mult))

        def pe_w_in(pe):
            pe.wait_ge(xn_ready, 1)

            def feature(t, slot, bk, land, free):
                pe.wait_ge(landed[slot], land)
                if free is not None:
                    pe.wait_ge(ring_free, free)
                matmul8(pe, bk[:, 0:S], slot).then_inc(tile_done, 1)

            for t in range(SLOTS):
                feature(t, t, bank[t % BANKS], 16, t - BANKS + 1 if t >= BANKS else None)
            with pe.Fori(1, 3) as i:
                for u in range(SLOTS):
                    feature(None, u, bank[u % BANKS], 16 * i + 16, SLOTS * i + (u - BANKS + 1))
            for t in range(18, 22):
                feature(t, t % SLOTS, bank[t % BANKS], count_at(t), t - BANKS + 1)
            for t in range(22, 26):
                pe.wait_ge(landed[t % SLOTS], count_at(t))
                pe.wait_ge(ring_free, t - BANKS + 1)
                matmul8_tokens(pe, bank[t % BANKS], t % SLOTS).then_inc(tile_done, 1)
            for t in range(26, 30):
                feature(t, t % SLOTS, bank[t % BANKS], count_at(t), t - BANKS + 1)
            with pe.Fori(5, 7) as i:
                for u in range(SLOTS):
                    feature(None, u, bank[u % BANKS], 16 * i + 16, SLOTS * i + (u - BANKS + 1))

        def act_w_in(act):
            for t in range(42):
                tile_wait(act, "w_in", t)
                bk = bank[t % BANKS]
                if t < 14:
                    ins = act.copy(zraw[:, t, 1:257], bk[:, 0:S])
                elif t < 22:
                    ins = act.copy(qk[:, t - 14, :], bk[:, 0:S])
                elif t < 26:
                    ins = act.copy(vtok[:, :, (t - 22) * 128:(t - 21) * 128],
                                   bk[:, 0:S].rearrange("p (b f) -> p b f", b=TT))
                else:
                    ins = act.activation(gates[:, t - 26, :], bk[:, 0:S], ACT.Sigmoid)
                ins.then_inc(ring_free, 1)

        mb_sq, mb_ss, mb_rt, mb_qn, mb_rot, mb_q = (sem("mb_sq"), sem("mb_ss"), sem("mb_rt"), sem("mb_qn"),
                                                    sem("mb_rot"), sem("mb_q"))
        trig_arg, trig = sem("trig_arg"), sem("trig")
        zk_clear = sem("zk_clear")
        msq, mrt, mqn, mt1 = rM["sq"], rM["rt"], rM["qn"], rM["t1"]

        def dve_shift(dve, v):
            dve.wait_ge(ring_free, 14)
            v.then(dve.memset(zraw[:, :, 0:1], 0.0))
            v.then(dve.tensor_tensor(zs[:, :, :], zraw[:, :, 0:S], zraw[:, :, 1:S + 1], ALU.subtract))
            for m in range(14):
                ins = dve.scalar_tensor_tensor(zs[:, m, :], zs[:, m, :], col("rwkv_mu", m), zraw[:, m, 1:S + 1],
                                               ALU.mult, ALU.add)
            v.then(ins)

        def dve_trig(dve, v):
            ang, kf, sn, cs = rM["ang"], rM["kf"], rM["sin"], rM["cos"]
            v.then(dve.tensor_copy(ang, posi))
            v.then(dve.tensor_scalar(ang, ang, col("rope_inv"), None, ALU.mult))
            v.then(dve.tensor_scalar(kf, ang, 1.0 / (2 * np.pi), 12582912.0, ALU.mult, ALU.add))
            v.then(dve.tensor_scalar(kf, kf, 12582912.0, None, ALU.subtract))
            rest = 2 * np.pi
            for bits in (6.28125, None, 0):
                if bits is None:
                    bits = float(np.float32(np.round(rest * 2 ** 20) / 2 ** 20))
                elif bits == 0:
                    bits = float(np.float32(rest))
                v.then(dve.scalar_tensor_tensor(ang, kf, -bits, ang, ALU.mult, ALU.add))
                rest -= bits
            v.then(dve.tensor_scalar(ang, ang, float(np.float32(3.1415925)), -float(np.float32(3.1415925)),
                                     ALU.min, ALU.max))
            v.then(dve.tensor_scalar(cs, ang, -1.0, None, ALU.mult))
            v.then(dve.tensor_tensor(cs, cs, ang, ALU.min))
            dve.tensor_scalar(cs, cs, float(np.pi / 2), None, ALU.add).then_inc(trig_arg, 1)

        def act_trig(act):
            act.wait_ge(trig_arg, 1)
            act.activation(rM["sin"], rM["ang"], ACT.Sin)
            act.activation(rM["cos"], rM["cos"], ACT.Sin).then_inc(trig, 1)

        def pool_moba(pool):
            pool.wait_ge(ada_read, 2 * ADA)
            pool.memset(rM["kz"], 0.0).then_inc(zk_clear, 1)

        def dve_moba(dve, v):
            dve.wait_ge(ring_free, 26)
            dve.tensor_tensor(msq, rA["qk"], rA["qk"], ALU.mult).then_inc(mb_sq, 1)
            dve_trig(dve, v)
            dve.wait_ge(mb_rt, 4)
            v.then(dve.reciprocal(mrt, mrt))
            for i, g in enumerate(("q_norm_g", "k_norm_g")):
                ins = dve.scalar_tensor_tensor(mqn[:, 1024 * i:1024 * i + 1024], rA["qk"][:, 1024 * i:1024 * i + 1024],
                                               col(g), mrt[:, 1024 * i:1024 * i + 1024], ALU.mult, ALU.mult)
                ins.then_inc(mb_qn, 1)
            dve.wait_ge(mb_qn, 2)
            dve.wait_ge(trig, 1)
            v.then(dve.tensor_tensor(mt1.rearrange("p (m t) -> p m t", m=8), qr[:, :, :], over(rM["cos"], 8), ALU.mult))
            dve.wait_ge(mb_rot, 1)
            for g in range(4):
                ins = dve.tensor_tensor(msq.rearrange("p (m t) -> p m t", m=8)[:, 2 * g:2 * g + 2, :],
                                        bank[3 + g][:, :].rearrange("p (m t) -> p m t", m=2), over(rM["sin"], 2),
                                        ALU.mult)
            v.then(ins)
            dve.wait_ge(zk_clear, 1)
            dve.tensor_tensor(mqn[:, 0:1024], mt1[:, 0:1024], msq[:, 0:1024], ALU.add).then_inc(mb_q, 1)
            for h, r in enumerate((lo, hi)):
                dve.tensor_tensor(kz[r, h::2, :], mt1[r, 1024:2048].rearrange("p (m t) -> p m t", m=4),
                                  msq[r, 1024:2048].rearrange("p (m t) -> p m t", m=4), ALU.add).then_inc(mb_q, 1)
            att_dve(dve, v, moba_jobs)

        def pe_moba(pe):
            pe.wait_ge(mb_sq, 1)
            for g in range(4):
                mm = pe.matmul(bank[3 + g][:, :], blk64, msq[:, 512 * g:512 * g + 512], start=True, stop=True)
            mm.then_inc(mb_ss, 1)
            pe.wait_ge(mb_qn, 2)
            pe.wait_ge(c1_loaded, 16)
            for g in range(4):
                mm = pe.matmul(bank[3 + g][:, :], c1["rot_moba"], mqn[:, 512 * g:512 * g + 512], start=True, stop=True)
            mm.then_inc(mb_rot, 1)
            pe.wait_ge(mb_q, 3)
            att_pe(pe, moba_jobs)

        def act_moba(act):
            act.wait_ge(mb_ss, 1)
            for g in range(4):
                act.activation(mrt[:, 512 * g:512 * g + 512], bank[3 + g][:, :], ACT.Sqrt, scale=1.0 / MD,
                               bias=col("eps")).then_inc(mb_rt, 1)
            act_trig(act)
            act_lora(act)
            att_act(act, moba_jobs)

        lora_in, lora_w, lora_loaded = sem("lora_in"), sem("lora_w"), sem("lora_loaded")
        rw_exp, rw_cum, rw_cml = sem("rw_exp"), sem("rw_cum"), sem("rw_cml")
        rw_sq, rw_ss, rw_rt = sem("rw_sq"), sem("rw_ss"), sem("rw_rt")
        bd_clear, bd_ready, u_ready, u_masked, u_copied = (sem("bd_clear"), sem("bd_ready"), sem("u_ready"),
                                                           sem("u_masked"), sem("u_copied"))
        t_init, t_x, t_xm, t_d, t_new = sem("t_init"), sem("t_x"), sem("t_xm"), sem("t_d"), sem("t_new")
        q_u, q_us, q_sa, q_sas, q_s, q_st, q_y, q_yc = (sem("q_u"), sem("q_us"), sem("q_sa"), sem("q_sas"),
                                                        sem("q_s"), sem("q_st"), sem("q_y"), sem("q_yc"))
        lora_in_t = rR["lora"].rearrange("p (k t) -> p k t", k=2)
        lora_wt = r0["AR"][:, 0:1536].rearrange("p (k f) -> p k f", k=3)
        four = lambda ap: ap.rearrange("p (m t) -> p m t", m=4)
        sixteen = lambda ap: ap.rearrange("p (u t) -> p u t", u=UN)

        def act_lora(act):
            act.wait_ge(mb_qn, 2)
            act.dma_start(lora_wt, a["lora"]).then_inc(lora_loaded, 16)

        def pool_rwkv(pool):
            pool.wait_ge(a_free, MH)
            pool.memset(rR["rmask"], 1.0).then_inc(gdone, 1)
            pool.wait_ge(gdone, 1)
            pool.memset(sixteen(rR["rmask"])[:, :, 0:1], 0.0).then_inc(bd_clear, 1)
            pool.memset(r0["BD"], 0.0).then_inc(bd_clear, 1)
            pool.wait_ge(lora_w, 2)
            pool.memset(r0["AR"], 0.0).then_inc(bd_clear, 1)

        def act_rwkv(act):
            act.wait_ge(a_free, MH)
            act.activation(lora_in_t[0:64, 0, :], zs[0:64, 12, :], ACT.Tanh)
            act.copy(lora_in_t[64:128, 0, :], zs[64:128, 12, :])
            act.activation(lora_in_t[:, 1, :], zs[:, 13, :], ACT.Sigmoid).then_inc(lora_in, 1)
            act.wait_ge(lora_w, 1)
            for m in range(4):
                act.activation(four(rR["lw"])[:, m, :], bank[3 + m][:, 0:S], ACT.Sigmoid, bias=col("rwkv_w0", m))
                ins = act.activation(four(rR["av"])[:, m, :], bank[3 + m][:, S:2 * S], ACT.Sigmoid,
                                     bias=col("rwkv_a0", m))
            ins.then_inc(lora_in, 1)
            act.wait_ge(lora_w, 2)
            act.copy(r0["g_rw"][:, 0:512], bank[7][:, :])
            act.copy(r0["g_rw"][:, 512:1024], bank[3][:, :]).then_inc(lora_in, 1)
            act.wait_ge(rw_ss, 1)
            for g in range(2):
                ins = act.activation(rR["rtk"][:, 512 * g:512 * g + 512], bank[4 + g][:, :], ACT.Sqrt)
            ins.then_inc(rw_rt, 1)
            act.wait_ge(rw_cum, 1)
            act.activation(Pc, rR["cum"], ACT.Exp)
            act.activation(rR["Pinv"], rR["cum"], ACT.Exp, scale=-1.0).then_inc(rw_exp, 1)
            act.activation(rR["Pprev"], rR["cml"], ACT.Exp).then_inc(rw_exp, 1)
            act.wait_ge(bd_ready, 1)
            for u in range(UN):
                act.wait_ge(u_ready, u + 1)
                act.copy(BKV[:, u, :, :], bank[5 + u % 2][:, 0:384].rearrange("p (k f) -> p k f", k=3)).then_inc(u_copied, 1)
            for c in range(NCH):
                act.wait_ge(q_u, c + 1)
                act.copy(usb[:, :, :], bank[3][:, :].rearrange("p (q f) -> p q f", q=PAIRS)).then_inc(q_us, 1)
                act.wait_ge(q_y, c + 1)
                yv = yb.rearrange("p (q c t) -> p q c t", q=PAIRS, c=NCH)
                bkv = bank[6 + c % 2][:, :].rearrange("p (q f) -> p q f", q=PAIRS)
                act.copy(yv[0:64, :, c, :], bkv[0:64, :, 0:64])
                act.copy(yv[64:128, :, c, :], bkv[64:128, :, 64:128]).then_inc(q_yc, 1)

        def dve_rwkv(dve, v):
            lw, cum, cml, av, kk, t1 = (rR[n] for n in ("lw", "cum", "cml", "av", "kk", "t1"))
            zk = zs[:, 4:8, :]
            for m in range(4):
                ins = dve.tensor_scalar(four(kk)[:, m, :], zs[:, 4 + m, :], col("rwkv_k_k", m), None, ALU.mult)
            v.then(ins)
            dve.tensor_tensor(rR["sqk"], kk, kk, ALU.mult).then_inc(rw_sq, 1)
            dve.wait_ge(lora_in, 2)
            dve.wait_ge(bd_clear, 1)
            v.then(dve.tensor_scalar(lw, lw, -float(np.exp(-0.5)), None, ALU.mult))
            v.then(dve.tensor_tensor_scan(cum, rR["rmask"], lw, 0.0, ALU.mult, ALU.add))
            dve.tensor_tensor(cml, cum, lw, ALU.subtract).then_inc(rw_cum, 1)
            v.then(dve.tensor_scalar(t1, av, 1.0, None, ALU.subtract))
            for m in range(4):
                ins = dve.tensor_scalar(four(t1)[:, m, :], four(t1)[:, m, :], col("rwkv_k_a", m), 1.0, ALU.mult, ALU.add)
            v.then(ins)
            v.then(dve.tensor_tensor(zk, zk, four(t1), ALU.mult))
            dve.wait_ge(rw_rt, 1)
            v.then(dve.tensor_scalar(rR["rtk"], rR["rtk"], 1e-12, None, ALU.max))
            v.then(dve.reciprocal(rR["rtk"], rR["rtk"]))
            v.then(dve.tensor_tensor(kk, kk, rR["rtk"], ALU.mult))
            dve.wait_ge(rw_exp, 1)
            v.then(dve.tensor_tensor(t1, av, rR["Pinv"], ALU.mult))
            dve.wait_ge(rw_exp, 2)
            dve.wait_ge(bd_clear, 3)
            for h, r in enumerate((lo, hi)):
                c = slice(64 * h, 64 * h + 64)
                dve.scalar_tensor_tensor(ARt[r, :, 0, c], sixteen(rR["Pprev"])[r], -1.0, sixteen(kk)[r], ALU.mult, ALU.mult)
                dve.tensor_tensor(ARt[r, :, 1, c], sixteen(Pc)[r], sixteen(r0["zs"][:, 0:1024])[r], ALU.mult)
                dve.tensor_tensor(BD[r, 0, :, c], sixteen(kk)[r], sixteen(t1)[r], ALU.mult)
                dve.tensor_tensor(BD[r, 1, :, c], sixteen(r0["zs"][:, 1024:2048])[r], sixteen(rR["Pinv"])[r], ALU.mult)
                ins = dve.tensor_copy(BD[r, 2, :, c], sixteen(r0["zs"][:, 2048:3072])[r])
            ins.then_inc(bd_ready, 1)
            dve.wait_ge(bd_ready, 1)
            level = lambda k: over(c1["mL"][:, 128 * k:128 * k + 128], 4)
            quad = lambda bk: bk[:, :].rearrange("p (q f) -> p q f", q=4)
            for u in range(UN):
                dve.wait_ge(u_ready, u + 1)
                bk = bank[3 + u % 2]
                dve.tensor_tensor(LT[:, u, :], bk[:, 0:128], c1["g_mask"][:, 0:128], ALU.mult)
                ins = dve.tensor_tensor(G3[:, u, :, :], bk[:, 128:512].rearrange("p (k f) -> p k f", k=3),
                                        c1["g_mask"][:, 128:512].rearrange("p (k f) -> p k f", k=3), ALU.mult)
                ins.then_inc(u_masked, 1)
            dve.wait_ge(u_masked, UN)
            for q in range(4):
                s = slice(4 * q, 4 * q + 4)
                dve.wait_ge(t_x, q + 1)
                v.then(dve.tensor_tensor(Tm[:, s, :], quad(bank[(3, 4, 7, 5)[q]]), level(0), ALU.mult))
                v.did(dve.tensor_tensor(TTm[:, s, :], LT[:, s, :], over(c1["mT1"], 4), ALU.mult))
                dve.tensor_tensor(Tm[:, s, :], Tm[:, s, :], over(ident, 4), ALU.add)
                v.settle()
                dve.tensor_tensor(TTm[:, s, :], TTm[:, s, :], over(ident, 4), ALU.add).then_inc(t_init, 1)
            dve.wait_ge(t_init, 4)

            def masked(n):
                dve.wait_ge(t_x, 4 + n + 1)
                s = slice(4 * (n % 4), 4 * (n % 4) + 4)
                dve.tensor_tensor(Xm[:, s, :], quad(bank[3 + n % 2]), level(1 + n // 4), ALU.mult).then_inc(t_xm, 1)

            def update(n):
                dve.wait_ge(t_d, n + 1)
                if n >= 4:
                    dve.wait_ge(t_new, n - 3)
                s = slice(4 * (n % 4), 4 * (n % 4) + 4)
                if n // 4 < 4:
                    dve.tensor_tensor(Tm[:, s, :], Tm[:, s, :], quad(bank[5]), ALU.add)
                dve.tensor_tensor(TTm[:, s, :], TTm[:, s, :], quad(bank[6 + n % 2]), ALU.add).then_inc(t_new, 1)

            masked(0)
            masked(1)
            for n in range(20):
                update(n)
                if n + 2 < 20:
                    masked(n + 2)
            dve.wait_ge(t_new, 20)
            last = sixteen(Pc)[:, :, CH - 1:CH]
            for c in range(NCH):
                old, new = st[:, c % 2], st[:, (c + 1) % 2]
                dve.wait_ge(q_sa, c + 1)
                dve.tensor_copy(sasb[:, :, :], bank[4][:, :].rearrange("p (q f) -> p q f", q=PAIRS)).then_inc(q_sas, 1)
                if c + 1 == NCH:
                    break
                if c:
                    dve.wait_ge(q_y, c)
                    for q in range(PAIRS):
                        ins = dve.tensor_scalar(new[:, q, :], old[:, q, :], last[:, NCH * q + c, :], None, ALU.mult)
                    v.then(ins)
                dve.wait_ge(q_s, c + 1)
                for q in range(PAIRS):
                    inc = bank[5][:, q * 128:(q + 1) * 128]
                    if c:
                        ins = dve.scalar_tensor_tensor(new[:, q, :], inc, last[:, NCH * q + c, :], new[:, q, :],
                                                       ALU.mult, ALU.add)
                    else:
                        ins = dve.tensor_scalar(new[:, q, :], inc, last[:, NCH * q + c, :], None, ALU.mult)
                ins.then_inc(q_st, 1)
                dve.wait_ge(q_st, c + 1)
            dve_rwkv_out(dve, v)

        gn_in, gn_ss, gn_rt, bon_in, bon_ss, rw_out = (sem("gn_in"), sem("gn_ss"), sem("gn_rt"), sem("bon_in"),
                                                       sem("bon_ss"), sem("rw_out"))

        def dve_rwkv_out(dve, v):
            dve.wait_ge(q_y, NCH)
            for m in range(4):
                ins = dve.scalar_tensor_tensor(four(rP["rk"])[:, m, :], zs[:, m, :], col("rwkv_r_k", m),
                                               zs[:, 4 + m, :], ALU.mult, ALU.mult)
            ins.then_inc(bon_in, 1)
            dve.wait_ge(gn_ss, 1)
            for g in range(2):
                ins = dve.scalar_tensor_tensor(rP["yc"][:, 512 * g:512 * g + 512], bank[3 + g][:, :], -1.0 / RN,
                                               yb[:, 512 * g:512 * g + 512], ALU.mult, ALU.add)
            v.then(ins)
            dve.tensor_tensor(rP["ysq"], rP["yc"], rP["yc"], ALU.mult).then_inc(gn_in, 1)
            dve.wait_ge(bon_ss, 1)
            for g in range(2):
                ins = dve.tensor_tensor(rP["bon"][:, 512 * g:512 * g + 512], bank[5 + g][:, :],
                                        r0["zs"][:, 2048 + 512 * g:2048 + 512 * g + 512], ALU.mult)
            v.then(ins)
            dve.wait_ge(gn_rt, 1)
            v.then(dve.reciprocal(rP["rt"], rP["rt"]))
            v.then(dve.tensor_tensor(rP["yc"], rP["yc"], rP["rt"], ALU.mult))
            for m in range(4):
                ins = dve.tensor_scalar(four(rP["yc"])[:, m, :], four(rP["yc"])[:, m, :], col("rwkv_ln_g", m),
                                        col("rwkv_ln_b", m), ALU.mult, ALU.add)
            v.then(ins)
            v.then(dve.tensor_tensor(rP["yc"], rP["yc"], rP["bon"], ALU.add))
            dve.tensor_tensor(yb, rP["yc"], r0["g_rw"], ALU.mult).then_inc(rw_out, 1)

        def pe_rwkv(pe):
            pe.wait_ge(lora_loaded, 16)
            pe.wait_ge(lora_in, 1)
            for m in range(4):
                for k in range(2):
                    mm = pe.matmul(bank[3 + m][:, k * S:(k + 1) * S], lora_wt[:, k, m * 128:(m + 1) * 128],
                                   lora_in_t[:, 0, :], start=True, stop=True)
            mm.then_inc(lora_w, 1)
            for m in range(4):
                if m == 2:
                    pe.wait_ge(lora_in, 2)
                mm = pe.matmul((bank[7], bank[3])[m // 2][:, (m % 2) * S:(m % 2 + 1) * S],
                               lora_wt[:, 2, m * 128:(m + 1) * 128], lora_in_t[:, 1, :], start=True, stop=True)
            mm.then_inc(lora_w, 1)
            mm = None
            pe.wait_ge(rw_sq, 1)
            for g in range(2):
                mm = pe.matmul(bank[4 + g][:, :], blk64, rR["sqk"][:, 512 * g:512 * g + 512], start=True, stop=True)
            mm.then_inc(rw_ss, 1)
            pe.wait_ge(bd_ready, 1)
            for u in range(UN):
                if u >= 2:
                    pe.wait_ge(u_masked, u - 1)
                    pe.wait_ge(u_copied, u - 1)
                ar = ARt[:, u, :, :].rearrange("p k f -> p (k f)")
                bk, bt = bank[3 + u % 2], bank[5 + u % 2]
                pe.matmul(bk[:, 0:256], BD[:, 0, u, :], ar, start=True, stop=True)
                pe.matmul(bk[:, 256:512], BD[:, 1, u, :], ar, start=True, stop=True)
                for k in range(3):
                    mm = pe.transpose(bt[:, k * 128:(k + 1) * 128], BD[:, k, u, :], ident)
                mm.then_inc(u_ready, 1)
            pe.wait_ge(u_masked, UN)
            for q in range(4):
                bk = bank[(3, 4, 7, 5)[q]]
                if q == 3:
                    pe.wait_ge(u_copied, UN)
                for i in range(4):
                    u = 4 * q + i
                    mm = pe.matmul(bk[:, i * 128:(i + 1) * 128], ARt[:, u, 0, :], BD[:, 0, u, :], start=True, stop=True)
            mm.then_inc(t_x, 4)

            def quads(q):
                return range(4 * (q % 4), 4 * (q % 4) + 4)

            def product(n):
                for i, u in enumerate(quads(n)):
                    mm = pe.matmul(bank[3 + n % 2][:, i * 128:(i + 1) * 128], LT[:, u, :], Tm[:, u, :],
                                   start=True, stop=True)
                mm.then_inc(t_x, 1)

            def increments(n):
                pe.wait_ge(t_xm, n + 1)
                if n >= 1:
                    pe.wait_ge(t_new, n)
                if n // 4 < 4:
                    for i, u in enumerate(quads(n)):
                        pe.matmul(bank[5][:, i * 128:(i + 1) * 128], TTm[:, u, :], Xm[:, u, :], start=True, stop=True)
                for i, u in enumerate(quads(n)):
                    mm = pe.matmul(bank[6 + n % 2][:, i * 128:(i + 1) * 128], Xm[:, u, :], TTm[:, u, :],
                                   start=True, stop=True)
                mm.then_inc(t_d, 1)

            pe.wait_ge(t_init, 4)
            product(0)
            product(1)
            for n in range(20):
                increments(n)
                if n + 2 < 20:
                    if n + 2 >= 4:
                        pe.wait_ge(t_new, n - 1)
                    product(n + 2)
            for c in range(NCH):
                old = st[:, c % 2]
                us = [NCH * q + c for q in range(PAIRS)]
                if c == 0:
                    pe.wait_ge(t_new, 20)
                else:
                    pe.wait_ge(q_st, c)
                for q, u in enumerate(us):
                    out = bank[3][:, q * 128:(q + 1) * 128]
                    if c:
                        pe.matmul(out, ARt[:, u, 0, :], old[:, q, :], start=True, stop=False)
                    mm = pe.matmul(out, G3[:, u, 1, :], BKV[:, u, 2, :], start=(c == 0), stop=True)
                mm.then_inc(q_u, 1)
                pe.wait_ge(q_us, c + 1)
                for q, u in enumerate(us):
                    mm = pe.matmul(bank[4][:, q * 128:(q + 1) * 128], TTm[:, u, :], usb[:, q, :], start=True, stop=True)
                mm.then_inc(q_sa, 1)
                pe.wait_ge(q_sas, c + 1)
                if c + 1 < NCH:
                    for q, u in enumerate(us):
                        out = bank[5][:, q * 128:(q + 1) * 128]
                        pe.matmul(out, BKV[:, u, 0, :], sasb[:, q, :], start=True, stop=False)
                        mm = pe.matmul(out, BKV[:, u, 1, :], BKV[:, u, 2, :], start=False, stop=True)
                    mm.then_inc(q_s, 1)
                if c >= 2:
                    pe.wait_ge(q_yc, c - 1)
                for q, u in enumerate(us):
                    out = bank[6 + c % 2][:, q * 128:(q + 1) * 128]
                    if c:
                        pe.matmul(out, old[:, q, :], ARt[:, u, 1, :], start=True, stop=False)
                    pe.matmul(out, sasb[:, q, :], G3[:, u, 0, :], start=(c == 0), stop=False)
                    mm = pe.matmul(out, BKV[:, u, 2, :], G3[:, u, 2, :], start=False, stop=True)
                mm.then_inc(q_y, 1)
            pe.wait_ge(q_yc, NCH)
            for g in range(2):
                mm = pe.matmul(bank[3 + g][:, :], blk64, yb[:, 512 * g:512 * g + 512], start=True, stop=True)
            mm.then_inc(gn_ss, 1)
            pe.wait_ge(bon_in, 1)
            for g in range(2):
                mm = pe.matmul(bank[5 + g][:, :], blk64, rP["rk"][:, 512 * g:512 * g + 512], start=True, stop=True)
            mm.then_inc(bon_ss, 1)
            pe.wait_ge(gn_in, 1)
            for g in range(2):
                mm = pe.matmul(bank[3 + g][:, :], blk64, rP["ysq"][:, 512 * g:512 * g + 512], start=True, stop=True)
            mm.then_inc(gn_ss, 1)

        def act_rwkv_out(act):
            act.wait_ge(gn_ss, 2)
            for g in range(2):
                ins = act.activation(rP["rt"][:, 512 * g:512 * g + 512], bank[3 + g][:, :], ACT.Sqrt, scale=1.0 / RN,
                                     bias=col("gn_eps"))
            ins.then_inc(gn_rt, 1)

        mix_ready = sem("mix_ready")

        def pe_proj(pe):
            pe.wait_ge(rw_out, 1)
            y4 = four(yb)

            def body(slot, bk):
                for half, x in enumerate((om, y4)):
                    for k in range(4):
                        mm = pe.matmul(bk[:, half * S:(half + 1) * S], blocks(slot, 4 * half + k), x[:, k, :],
                                       start=(k == 0), stop=(k == 3))
                return mm
            ring_tiles(pe, "proj", body)

        def dve_proj(dve, v):
            g2v = gates.rearrange("p (k m) t -> p k m t", k=2)
            for m in range(KT):
                tile_wait(dve, "proj", m)
                v.then(dve.tensor_tensor(mixt[:, m % 2], ring_bank("proj", m)[:, :].rearrange("p (k t) -> p k t", k=2),
                                         g2v[:, :, m, :], ALU.mult))
                dve.tensor_tensor(mix1[:, m, :], mixt[:, m % 2, 0, :], mixt[:, m % 2, 1, :], ALU.add).then_inc(ring_free, 1)

        def pe_w_out(pe):
            pe.wait_ge(ring_free, RING0["w_out"])
            ring_tiles(pe, "w_out", lambda slot, bk: matmul8(pe, bk[:, 0:S], slot, mix1))

        def dve_residual(dve, name, vec):
            for m in range(KT):
                tile_wait(dve, name, m)
                ins = dve.scalar_tensor_tensor(hT[:, m, :], ring_bank(name, m)[:, 0:S], modc(vec, m), hT[:, m, :],
                                               ALU.mult, ALU.add)
                ins.then_inc(ring_free, 1)
            dve.wait_ge(ring_free, RING0[name] + COUNT[name])

        sc_ready, sc_copied, pick_ready, t3_turned, t3_ready = (sem("sc_ready"), sem("sc_copied"), sem("pick_ready"),
                                                                sem("t3_turned"), sem("t3_ready"))
        gate_arg, gate_exp, iota_ready = sem("gate_arg"), sem("gate_exp"), sem("iota_ready")
        hot, g_ready, g_copied = sem("hot"), sem("g_ready"), sem("g_copied")
        gelu_ready, w_ready = sem("gelu_ready"), sem("w_ready")

        def act_subk(act):
            act.wait_ge(xn_ready, 2)
            act.dma_start(rK["subk"], a["subk"]).then_inc(subk_loaded, 16)

        def pe_route(pe):
            pe.wait_ge(xn_ready, 2)
            ring_tiles(pe, "wq", lambda slot, bk: matmul8(pe, bk[:, 0:S], slot))
            pe.wait_ge(ring_free, RING0["wq"] + COUNT["wq"])
            pe.wait_ge(subk_loaded, 16)
            for n in range(NR // 4):
                if n >= 4:
                    pe.wait_ge(sc_copied, n - 3)
                for i in range(4):
                    b, r = divmod(4 * n + i, 16)
                    mm = pe.matmul(bank[3 + n % 4][:, i * 128:(i + 1) * 128], qp[:, r, b * 128:(b + 1) * 128],
                                   subk[:, r, :], start=True, stop=True)
                mm.then_inc(sc_ready, 1)

        def act_route(act):
            act_subk(act)
            for t in range(COUNT["wq"]):
                tile_wait(act, "wq", t)
                act.copy(qp[:, t, :], ring_bank("wq", t)[:, 0:S]).then_inc(ring_free, 1)
            for n in range(NR // 4):
                act.wait_ge(sc_ready, n + 1)
                act.copy(sc[:, 4 * n:4 * n + 4, :], bank[3 + n % 4][:, :].rearrange("p (r n) -> p r n", r=4))\
                   .then_inc(sc_copied, 1)
            act.wait_ge(gate_arg, 1)
            act.activation(rK["gate"], rK["gate"], ACT.Exp).then_inc(gate_exp, 1)

        def pool_route(pool):
            pool.wait_ge(rw_out, 1)
            pool.iota(rG["iotai"].bitcast(I32), [[1, 128]], base=0, channel_multiplier=0).then_inc(gdone, 1)
            pool.wait_ge(gdone, 2)
            pool.tensor_copy(rG["iota"], rG["iotai"].bitcast(I32)).then_inc(iota_ready, 1)

        def top16(dve, v, values, index, rows, scratch):
            v.then(dve.max(values[:, 0:8], rows))
            v.did(dve.max_index(index[:, 0:8], values[:, 0:8], rows))
            v.then(dve.match_replace(scratch, values[:, 0:8], rows, -3e38))
            v.then(dve.max(values[:, 8:16], scratch))
            v.did(dve.max_index(index[:, 8:16], values[:, 8:16], scratch))

        def dve_route(dve, v):
            for r in range(NR):
                dve.wait_ge(sc_copied, r // 4 + 1)
                top16(dve, v, tv[:, r, :], ti[:, r, :], sc[:, r, :], rK["scr"][:, (r % 2) * 128:(r % 2) * 128 + 128])
            v.settle()
            v.did(dve.tensor_copy(rK["tif"], rK["ti"].bitcast(U32)))
            t4 = rK["tv"].rearrange("p (r h k) -> p r h k", r=NQ, h=2)
            c4 = rK["cand"].rearrange("p (r a b) -> p r a b", r=NQ, a=PK)
            first = t4[:, :, 0, :].unsqueeze(3).to_broadcast([P, NQ, PK, PK])
            second = t4[:, :, 1, :].unsqueeze(2).to_broadcast([P, NQ, PK, PK])
            v.then(dve.tensor_tensor(c4, first, second, ALU.add))
            for r in range(NQ):
                top16(dve, v, best[:, r, :], bi[:, r, :], cand[:, r, :], rK["scr2"])
            v.settle()
            dve.tensor_tensor(gate[:, :, :], best[:, :, :], best[:, :, 0:1].to_broadcast([P, NQ, PK]), ALU.subtract)\
               .then_inc(gate_arg, 1)
            v.did(dve.tensor_scalar(ba[:, 0, :], rK["bi"].bitcast(U32), 4, None, ALU.logical_shift_right))
            v.then(dve.tensor_scalar(ba[:, 1, :], rK["bi"].bitcast(U32), 15, None, ALU.bitwise_and))
            v.then(dve.tensor_copy(rK["baf"], rK["ba"].bitcast(U32)))
            dve.wait_ge(iota_ready, 1)
            f4 = rK["tif"].rearrange("p (r h k) -> p r h k", r=NQ, h=2)
            big = rK["big"].rearrange("p (r k x) -> p r k x", r=NQ, k=PK)
            iota16 = rG["iota"][:, 0:PK].unsqueeze(1).unsqueeze(1).to_broadcast([P, NQ, PK, PK])
            for h in range(2):
                rank = baf[:, h, :].rearrange("p (r k) -> p r k", r=NQ).unsqueeze(3).to_broadcast([P, NQ, PK, PK])
                v.then(dve.tensor_tensor(big, rank, iota16, ALU.is_equal))
                table = f4[:, :, h, :].unsqueeze(2).to_broadcast([P, NQ, PK, PK])
                v.then(dve.tensor_tensor(big, big, table, ALU.mult))
                v.then(dve.tensor_reduce(pick[:, h, :].rearrange("p (r k) -> p r k", r=NQ), big, AX, ALU.add))
            dve.wait_ge(gate_exp, 1)
            v.then(dve.tensor_reduce(rK["gsum"][:, 0:NQ], gate[:, :, :], AX, ALU.add))
            v.then(dve.reciprocal(rK["gsum"][:, NQ:2 * NQ], rK["gsum"][:, 0:NQ]))
            dve.tensor_tensor(gate[:, :, :], gate[:, :, :], wide(rK["gsum"][:, NQ:2 * NQ], PK), ALU.mult)\
               .then_inc(pick_ready, 1)
            dve.wait_ge(t3_turned, 1)
            v.did(dve.tensor_copy(T3[:, 0:2, :], bank[3][:, :].rearrange("p (k t) -> p k t", k=2)))
            dve.tensor_copy(T3[:, 2, :], bank[4][:, 0:S]).then_inc(t3_ready, 1)
            dve.wait_ge(t3_ready, 1)

        def pe_turn_routes(pe):
            pe.wait_ge(pick_ready, 1)
            for k, x in enumerate((pick[:, 0, :], pick[:, 1, :], rK["gate"])):
                for b in range(TT):
                    mm = pe.transpose(bank[3 + k // 2][:, (k % 2) * S + b * 128:(k % 2) * S + (b + 1) * 128],
                                      x[:, b * 128:(b + 1) * 128], ident)
            mm.then_inc(t3_turned, 1)

        GROUPS = S // 8

        def dve_hot(dve):
            def group(b, t0, used):
                if used is not None:
                    dve.wait_ge(g_ready, used)
                dve.tensor_tensor(A8[:, b], over(rG["iota"], 8), wide(T3[:, 0, bass.ds(t0, 8)], 128), ALU.is_equal)
                for t in range(8):
                    ins = dve.tensor_scalar(B8[:, b, t, :], rG["iota"], T3[:, 1, bass.ds(t0 + t, 1)],
                                            T3[:, 2, bass.ds(t0 + t, 1)], ALU.is_equal, ALU.mult)
                ins.then_inc(hot, 1)
            group(0, 0, None)
            group(1, 8, None)
            with dve.Fori(1, GROUPS // 2) as i:
                for b in range(2):
                    group(b, 16 * i + 8 * b, 2 * i + (b - 1))

        def pe_gates(pe):
            def group(b, n, free):
                pe.wait_ge(hot, n)
                if free is not None:
                    pe.wait_ge(g_copied, free)
                for t in range(8):
                    mm = pe.matmul(bank[3 + 2 * b + t // 4][:, (t % 4) * 128:(t % 4) * 128 + 128], A8[:, b, t, :],
                                   B8[:, b, t, :], start=True, stop=True)
                mm.then_inc(g_ready, 1)
            group(0, 1, None)
            group(1, 2, None)
            with pe.Fori(1, GROUPS // 2) as i:
                for b in range(2):
                    group(b, 2 * i + (b + 1), 2 * i + (b - 1))

        def act_gates(act):
            with act.Fori(0, GROUPS // 2) as i:
                for b in range(2):
                    act.wait_ge(g_ready, 2 * i + (b + 1))
                    for h in range(2):
                        ins = act.copy(G[:, bass.ds(16 * i + 8 * b + 4 * h, 4), :],
                                       bank[3 + 2 * b + h][:, :].rearrange("p (t j) -> p t j", t=4))
                    ins.then_inc(g_copied, 1)

        P0 = FIRST["peer"]
        u_tile = lambda j: P0 + (0 if j == 0 else 2 * j - 1)
        v_tile = lambda j: P0 + (2 * j + 2 if j < NK - 1 else 2 * NK - 1)
        accs = [bank[4 + m // 2][:, (m % 2) * S:(m % 2 + 1) * S] for m in range(KT)]

        def accumulate8(pe, slot, w, first, last):
            for m in range(KT):
                mm = pe.matmul(accs[m], blocks(slot, m), w, start=first and m % 2 == 0, stop=last,
                               skip_group_check=True)
            return mm

        def pe_peer(pe):
            def up(j, slot, bk, land, free):
                pe.wait_ge(landed[slot], land)
                if free is not None:
                    pe.wait_ge(gelu_ready, free)
                matmul8(pe, bank[bk][:, 0:S], slot).then_inc(tile_done, 1)

            def down(slot, wb, land, weighed, first=False, last=False):
                pe.wait_ge(landed[slot], land)
                pe.wait_ge(w_ready, weighed)
                accumulate8(pe, slot, Wj[:, wb, :], first, last).then_inc(tile_done, 1)

            pe.wait_ge(g_copied, GROUPS)
            up(0, slot_of(u_tile(0)), 0, count_at(u_tile(0)), None)
            for j in range(1, 4):
                up(j, slot_of(u_tile(j)), j % 3, count_at(u_tile(j)), j - 2 if j >= 3 else None)
                down(slot_of(v_tile(j - 1)), (j - 1) % 3, count_at(v_tile(j - 1)), j, first=(j == 1))
            with pe.Fori(0, (NK - 2 - 4 + 1) // 3) as i:
                for u in range(3):
                    j = 4 + u
                    up(None, slot_of(u_tile(j)), j % 3, 16 * i + count_at(u_tile(j)), 3 * i + (j - 2))
                    down(slot_of(v_tile(j - 1)), (j - 1) % 3, 16 * i + count_at(v_tile(j - 1)), 3 * i + j)
            for j in range(4 + 3 * ((NK - 5) // 3), NK):
                up(j, slot_of(u_tile(j)), j % 3, count_at(u_tile(j)), j - 2)
                down(slot_of(v_tile(j - 1)), (j - 1) % 3, count_at(v_tile(j - 1)), j)
            j = NK - 1
            down(slot_of(v_tile(j)), j % 3, count_at(v_tile(j)), NK, last=True)

        def act_peer(act):
            def one(b, done, used):
                act.wait_ge(tile_done, done)
                if used is not None:
                    act.wait_ge(w_ready, used)
                act.activation(ge[:, b, :], bank[b][:, 0:S], ACT.Gelu).then_inc(gelu_ready, 1)
            for j in range(3):
                one(j % 3, u_tile(j) + 1, None)
            with act.Fori(0, (NK - 3) // 3) as i:
                for u in range(3):
                    one(u, 6 * i + (u_tile(3 + u) + 1), 3 * i + (u + 1))
            for j in range(3 + 3 * ((NK - 3) // 3), NK):
                one(j % 3, u_tile(j) + 1, j - 2)

        def dve_peer(dve, v):
            def one(j, b, ready, used):
                dve.wait_ge(gelu_ready, ready)
                if used is not None:
                    dve.wait_ge(tile_done, used)
                dve.tensor_tensor(Wj[:, b, :], ge[:, b, :], G[:, :, j], ALU.mult).then_inc(w_ready, 1)
            dve.wait_ge(g_copied, GROUPS)
            for j in range(3):
                one(j, j % 3, j + 1, None)
            with dve.Fori(0, (NK - 3) // 3) as i:
                for u in range(3):
                    one(3 * i + (3 + u), u, 3 * i + (4 + u), 6 * i + (v_tile(u) + 1))
            for j in range(3 + 3 * ((NK - 3) // 3), NK):
                one(j, j % 3, j + 1, v_tile(j - 3) + 1)
            dve.wait_ge(tile_done, FIRST["peer"] + COUNT["peer"])
            dve_add_accs(dve, v, 5)

        acc_read = sem("acc_read")

        def dve_add_accs(dve, v, vec):
            for m in range(KT):
                ins = dve.scalar_tensor_tensor(hT[:, m, :], accs[m], modc(vec, m), hT[:, m, :], ALU.mult, ALU.add)
            ins.then_inc(acc_read, 1)
            dve.wait_ge(acc_read, 1 if vec == 5 else 2)

        def act_const2(act):
            act.wait_ge(acc_read, 1)
            act.dma_start(r2["const2"], a["const2"]).then_inc(c2_loaded, 16)

        def pe_w_in2(pe):
            pe.wait_ge(xn_ready, 3)
            first, ring0 = FIRST["w_in2"], RING0["w_in2"]
            def one(k, i, body):
                t, r = first + k, ring0 + k
                pe.wait_ge(landed[t % SLOTS], 16 * i + count_at(t))
                pe.wait_ge(ring_free, SLOTS * i + (r - BANKS + 1))
                body(t % SLOTS, bank[r % BANKS]).then_inc(tile_done, 1)
            feature = lambda slot, bk: matmul8(pe, bk[:, 0:S], slot)
            with pe.Fori(0, 6) as i:
                for k in range(SLOTS):
                    one(k, i, feature)
            for k in range(36, 38):
                one(k, 0, feature)
            for k in range(38, 43):
                one(k, 0, lambda slot, bk: matmul8_tokens(pe, bk, slot))

        def act_w_in2(act):
            for k in range(43):
                tile_wait(act, "w_in2", k)
                bk = ring_bank("w_in2", k)
                two = bk[:, 0:S].rearrange("p (b f) -> p b f", b=TT)
                if k < 22:
                    ins = act.copy(F2[:, k, :], bk[:, 0:S])
                elif k < 38:
                    ins = act.activation(bg[:, k - 22, :], bk[:, 0:S], ACT.Sigmoid)
                elif k < 42:
                    f = (k % 2) * 128
                    ins = act.copy((vs2, vw2)[(k - 38) // 2][:, :, f:f + 128], two)
                else:
                    ins = act.activation(gt2[:, :, :], two[:, :, 0:24], ACT.Sigmoid)
                ins.then_inc(ring_free, 1)

        n_sq, n_ss, n_rt, n_qn, n_rot, n_q = (sem("n_sq"), sem("n_ss"), sem("n_rt"), sem("n_qn"), sem("n_rot"),
                                              sem("n_q"))
        cm_x, cm_hs, cm_t, cm_ts, cm_o0, cm_kn, cm_kt, cm_kc, cm_rt = (sem(f"cm_{x}") for x in
                                    ("x", "hs", "t", "ts", "o0", "kn", "kt", "kc", "rt"))

        def dve_nsa(dve, v):
            f = r2["F2"]
            dve.wait_ge(ring_free, RING0["w_in2"] + 22)
            dve.tensor_tensor(sq14[:, 0:12, :], F2[:, 0:12, :], F2[:, 0:12, :], ALU.mult).then_inc(n_sq, 1)
            dve.wait_ge(n_rt, 6)
            v.then(dve.reciprocal(r2["rs"], r2["rs"]))
            for at, n, g in ((0, 8, "nsa_q_norm_2"), (8, 2, "nsa_ks_norm_2"), (10, 2, "nsa_kw_norm_2")):
                ins = dve.scalar_tensor_tensor(f[:, at * S:(at + n) * S], f[:, at * S:(at + n) * S], col(g),
                                               r2["rs"][:, at * S:(at + n) * S], ALU.mult, ALU.mult)
            ins.then_inc(n_qn, 1)
            dve.wait_ge(n_qn, 1)
            for g in range(7):
                dve.wait_ge(n_rot, g + 1)
                ins = dve.tensor_tensor(ro14[:, 2 * g:2 * g + 2, :], bank[3 + g % 5][:, :].rearrange("p (m t) -> p m t", m=2),
                                        over(c2["nsa_sin"], 2), ALU.mult)
                ins.then_inc(n_q, 1)
            dve.wait_ge(n_q, 7)
            v.then(dve.tensor_tensor(F2[:, 0:14, :], F2[:, 0:14, :], over(c2["nsa_cos"], 14), ALU.mult))
            v.then(dve.tensor_tensor(F2[:, 0:14, :], F2[:, 0:14, :], ro14[:, :, :], ALU.add))
            for i, pe_name in enumerate(("cmp_k_pe", "cmp_v_pe")):
                for g in range(NG):
                    src = F2[:, 12 + 2 * i + g, :]
                    for half in range(CB // CS):
                        part = src[:, half * CS:half * CS + NCMP * CS].rearrange("p (n l) -> p l n", l=CS)
                        ins = dve.tensor_tensor(XP[:, i, half * CS:(half + 1) * CS, g * NCMP:(g + 1) * NCMP], part,
                                                wide(col(pe_name, half * CS, CS), NCMP), ALU.add)
            ins.then_inc(cm_x, 1)
            kt = r2["cmt"][0:NCMP, 0:256].rearrange("p (g f) -> p g f", g=NG)
            st8 = r2["kst"][0:NCMP, :]
            dve.wait_ge(tile_done, FIRST["cmp_w2"] + 1)
            v.then(dve.tensor_copy(r2["cmt"][0:NCMP, 0:512], bank[6][0:NCMP, :]))
            for g in range(NG):
                ins = dve.tensor_tensor_reduce(r2["hid"][0:NCMP, g * 128:(g + 1) * 128], kt[:, g, :], kt[:, g, :],
                                               1.0, 0.0, ALU.mult, ALU.add, st8[:, g:g + 1])
            ins.then_inc(cm_kn, 1)
            dve.wait_ge(cm_rt, 1)
            v.then(dve.reciprocal(st8[:, 4:6], st8[:, 2:4]))
            for g in range(NG):
                ins = dve.tensor_scalar(kt[:, g, :], kt[:, g, :], st8[:, 4 + g:5 + g], None, ALU.mult)
            ins.then_inc(cm_kn, 1)
            dve.wait_ge(cm_kt, 1)
            dve.tensor_scalar(r2["kcT"][:, 0:30], bank[7][:, 0:30], col("nsa_kc_norm_2"), None, ALU.mult).then_inc(cm_kc, 1)
            dve.wait_ge(ring_free, RING0["w_in2"] + 43)
            g3 = r2["gt"].rearrange("p (b h k) -> p b h k", b=TT, h=NH)
            v.then(dve.tensor_tensor(g3[:, :, :, 0], g3[:, :, :, 0], wide(c2["cmp_valid"], NH), ALU.mult))
            att_dve(dve, v, nsa_jobs)

        def pe_nsa(pe):
            pe.wait_ge(n_sq, 1)
            for g in range(6):
                if g == 5:
                    pe.wait_ge(n_rt, 1)
                pe.matmul(bank[3 + g % 5][:, :], ones, r2["sq"][:, 512 * g:512 * g + 512], start=True,
                          stop=True).then_inc(n_ss, 1)
            pe.wait_ge(n_qn, 1)
            pe.wait_ge(c2_loaded, 16)
            for g in range(7):
                if g >= 5:
                    pe.wait_ge(n_q, g - 4)
                pe.matmul(bank[3 + g % 5][:, :], c2["rot_nsa"], r2["F2"][:, 512 * g:512 * g + 512], start=True,
                          stop=True).then_inc(n_rot, 1)
            pe.wait_ge(cm_x, 1)
            for i, name in enumerate(("cmp_k", "cmp_v")):
                for t in range(8):
                    n = FIRST[name] + t
                    pe.wait_ge(landed[slot_of(n)], count_at(n))
                    for k in range(4):
                        l = 4 * t + k
                        mm = pe.matmul(bank[3 + i][0:30, 0:256], XP[:, i, l, :], blocks(slot_of(n), k, 256),
                                       start=(l == 0), stop=(l == CB - 1))
                    mm.then_inc(tile_done, 1)
            n = FIRST["cmp_w2"]
            pe.wait_ge(landed[slot_of(n)], count_at(n))
            for i in range(2):
                pe.wait_ge(cm_hs, i + 1)
                if i:
                    pe.wait_ge(cm_ts, 1)
                for h in range(2):
                    mm = pe.transpose(bank[5][:, h * 30:(h + 1) * 30], r2["hid"][0:30, h * 128:(h + 1) * 128],
                                      ident[0:30, 0:30])
                mm.then_inc(cm_t, 1)
                pe.wait_ge(cm_ts, i + 1)
                for g in range(NG):
                    for h in range(2):
                        mm = pe.matmul(bank[6][0:NCMP, i * 256 + g * 128:i * 256 + (g + 1) * 128],
                                       r2["hidT"][:, h * 30 + g * NCMP:h * 30 + (g + 1) * NCMP],
                                       blocks(slot_of(n), 2 * i + h), start=(h == 0), stop=(h == 1))
                if i == 0:
                    mm.then_inc(cm_o0, 1)
            mm.then_inc(tile_done, 1)
            pe.wait_ge(cm_kn, 2)
            for g in range(NG):
                mm = pe.transpose(bank[7][:, g * NCMP:(g + 1) * NCMP], r2["cmt"][0:NCMP, g * 128:(g + 1) * 128],
                                  ident[0:NCMP, 0:NCMP])
            mm.then_inc(cm_kt, 1)
            pe.wait_ge(cm_kc, 1)
            att_pe(pe, nsa_jobs)

        def act_nsa(act):
            for g in range(6):
                act.wait_ge(n_ss, g + 1)
                act.activation(r2["rs"][:, 512 * g:512 * g + 512], bank[3 + g % 5][:, :], ACT.Sqrt, scale=1.0 / 128,
                               bias=col("eps")).then_inc(n_rt, 1)
            for i, name in enumerate(("cmp_k", "cmp_v")):
                act.wait_ge(tile_done, FIRST[name] + 8)
                if i:
                    act.wait_ge(cm_t, 1)
                act.activation(r2["hid"][0:30, :], bank[3 + i][0:30, 0:256], ACT.Silu).then_inc(cm_hs, 1)
                act.wait_ge(cm_t, i + 1)
                if i:
                    act.wait_ge(cm_o0, 1)
                act.copy(r2["hidT"][:, 0:60], bank[5][:, 0:60]).then_inc(cm_ts, 1)
            act.wait_ge(cm_kn, 1)
            act.activation(r2["kst"][0:NCMP, 2:4], r2["kst"][0:NCMP, 0:2], ACT.Sqrt, scale=1.0 / 128,
                           bias=col("eps")[0:NCMP]).then_inc(cm_rt, 1)
            att_act(act, nsa_jobs)

        vcv = r2["cmt"][0:NCMP, 256:512].rearrange("p (g f) -> p g f", g=NG)
        g3v = r2["gt"].rearrange("p (b h k) -> p b h k", b=TT, h=NH)
        masks2 = dict(causal=c2["causal"], cmp=c2["cmp_mask"])
        nsa_jobs = []
        for h in range(NH):
            g = h // (NH // NG)
            for k, (kind, key, val) in enumerate((("cmp", r2["kcT"][:, g * NCMP:(g + 1) * NCMP], lambda b, g=g: vcv[:, g, :]),
                                                  ("causal", F2[:, 8 + g, :], lambda b, g=g: vs2[:, b, g * 128:(g + 1) * 128]),
                                                  ("causal", F2[:, 10 + g, :], lambda b, g=g: vw2[:, b, g * 128:(g + 1) * 128]))):
                nsa_jobs.append(dict(n=MH + 3 * h + k, group=MH + h, first=(k == 0), last=(k == 2), kind=kind,
                                     scale=128 ** -0.5, gate=g3v[:, :, h, k], q=[F2[:, h, :]], k=[key], M=128,
                                     v=val, rows=all_rows, out=oA[:, h, :], buf=att2, masks=masks2))

        c_sq, c_ss, c_rt, c_n = sem("c_sq"), sem("c_ss"), sem("c_rt"), sem("c_n")
        l_sq, l_ss, l_rt, l_q, l_rot, l_k = (sem(f"l_{x}") for x in ("sq", "ss", "rt", "q", "rot", "k"))
        crs = r2["rot"][:, 0:512].rearrange("p (k t) -> p k t", k=2)
        kro = r2["rot"][:, 512:512 + 2048].rearrange("p (h t) -> p h t", h=MLH)
        krr = r2["rot"][:, 2560:2816]
        krt = r2["rot"][:, 2816:3072]

        def dve_mla(dve, v):
            c_in = F2[:, 16:21, :]
            dve.tensor_tensor(sq14[:, 0:5, :], c_in, c_in, ALU.mult).then_inc(c_sq, 1)
            dve.wait_ge(c_rt, 2)
            v.then(dve.reciprocal(crs, crs))
            for k in range(5):
                g = col("mla_cq_norm_2", k) if k < 3 else col("mla_ckv_norm_2", k - 3)
                ins = dve.scalar_tensor_tensor(F2[:, 16 + k, :], F2[:, 16 + k, :], g, crs[:, k // 3, :], ALU.mult, ALU.mult)
            ins.then_inc(c_n, 1)
            v.then(dve.memset(kro[:, :, :], 0.0))
            dve.wait_ge(ring_free, RING0["uq"] + 6)
            dve.tensor_tensor(sq14[:, 0:12, :], qb[:, :, :], qb[:, :, :], ALU.mult).then_inc(l_sq, 1)
            dve.wait_ge(l_rt, 4)
            rsv = rs12[:, 0:8, :]
            v.then(dve.reciprocal(rsv, rsv))
            v.did(dve.scalar_tensor_tensor(qb[:, 0:8, :], qb[:, 0:8, :], col("mla_q_nope"), rsv, ALU.mult, ALU.mult))
            pairs = r2["rs"][:, 0:2048].rearrange("p (m h t) -> p h m t", h=2, t=S)
            for h, r in enumerate((lo, hi)):
                ins = dve.scalar_tensor_tensor(qb[r, 8:12, :], qb[r, 8:12, :], col("mla_q_rope")[r], pairs[r, h],
                                               ALU.mult, ALU.mult)
            v.then(ins)
            dve.tensor_scalar(krr, F2[:, 21, :], col("mla_k_rope"), None, ALU.mult).then_inc(l_q, 1)
            dve.wait_ge(l_q, 1)
            ro = sq14[:, 0:5, :]
            dve.wait_ge(l_rot, 1)
            for g in range(2):
                dve.tensor_tensor(ro[:, 2 * g:2 * g + 2, :], bank[3 + g][:, :].rearrange("p (m t) -> p m t", m=2),
                                  over(c2["mla_sin"], 2), ALU.mult)
            v.did(dve.tensor_tensor(ro[:, 4, :], bank[5][:, 0:S], c2["mla_sin"], ALU.mult))
            v.did(dve.tensor_tensor(qb[:, 8:12, :], qb[:, 8:12, :], over(c2["mla_cos"], 4), ALU.mult))
            v.then(dve.tensor_tensor(krt, krr, c2["mla_cos"], ALU.mult))
            v.did(dve.tensor_tensor(qb[:, 8:12, :], qb[:, 8:12, :], ro[:, 0:4, :], ALU.add))
            v.then(dve.tensor_tensor(krt, krt, ro[:, 4, :], ALU.add))
            dve.wait_ge(ring_free, RING0["uk"] + 4)
            v.did(dve.tensor_tensor(sq14[:, 0:8, :], kb[:, :, :], kb[:, :, :], ALU.mult))
            dve.tensor_tensor(sq14[:, 8, :], F2[:, 21, :], F2[:, 21, :], ALU.mult).then_inc(l_sq, 1)
            dve.wait_ge(l_rt, 8)
            v.then(dve.reciprocal(rsv, rsv))
            v.did(dve.scalar_tensor_tensor(kb[:, :, :], kb[:, :, :], col("mla_k_nope"), rsv, ALU.mult, ALU.mult))
            for h, r in enumerate((lo, hi)):
                kr4 = kro.rearrange("p (m h) t -> p h m t", h=2)
                ins = dve.tensor_tensor(kr4[r, h], pairs[r, h], over(krt, 4)[r], ALU.mult)
            ins.then_inc(l_k, 1)
            dve.wait_ge(ring_free, RING0["uv"] + 4)
            att_dve(dve, v, mla_jobs)
            dve.wait_ge(a_free, MH + NH + MLH)
            v.did(dve.tensor_tensor(oA[:, :, :], oA[:, :, :], bg[:, 0:8, :], ALU.mult))
            v.then(dve.tensor_tensor(oB[:, :, :], oB[:, :, :], bg[:, 8:16, :], ALU.mult))
            dve.tensor_tensor(oA[:, :, :], oA[:, :, :], oB[:, :, :], ALU.add).then_inc(mix_ready, 1)

        def pe_mla(pe):
            pe.wait_ge(c_sq, 1)
            for k in range(5):
                mm = pe.matmul(bank[3 + k // 3][:, 0:S], ones, sq14[:, k, :], start=(k in (0, 3)), stop=(k in (2, 4)))
            mm.then_inc(c_ss, 1)
            pe.wait_ge(c_n, 1)

            def uq(slot, bk):
                for o in range(2):
                    for k in range(3):
                        mm = pe.matmul(bk[:, o * S:(o + 1) * S], blocks(slot, 3 * o + k), F2[:, 16 + k, :],
                                       start=(k == 0), stop=(k == 2))
                return mm

            def uk(slot, bk):
                for o in range(2):
                    for k in range(2):
                        mm = pe.matmul(bk[:, o * S:(o + 1) * S], blocks(slot, 2 * o + k), F2[:, 19 + k, :],
                                       start=(k == 0), stop=(k == 1))
                return mm

            def uv(slot, bk):
                for b in range(TT):
                    for k in range(2):
                        mm = pe.matmul(bk[:, b * S:(b + 1) * S], F2[:, 19 + k, b * 128:(b + 1) * 128],
                                       blocks(slot, k, 256), start=(k == 0), stop=(k == 1))
                return mm

            def sums(sq_count, rope_tile, rt0):
                pe.wait_ge(l_sq, sq_count)
                for g in range(4):
                    for i in range(2):
                        h = 2 * g + i
                        out = bank[3 + g][:, i * S:(i + 1) * S]
                        pe.matmul(out, ones, sq14[:, h, :], start=True, stop=False)
                        half = c2[("half0", "half1")[i]] if rope_tile is None else c2["half0"]
                        rope = sq14[:, 8 + g, :] if rope_tile is None else sq14[:, rope_tile, :]
                        mm = pe.matmul(out, half, rope, start=False, stop=True)
                    mm.then_inc(l_ss, 1)

            ring_tiles(pe, "uq", uq)
            ring_tiles(pe, "uk", uk)
            ring_tiles(pe, "uv", uv)
            sums(1, None, 0)
            pe.wait_ge(l_q, 1)
            for g in range(2):
                pe.matmul(bank[3 + g][:, :], c2["rot_mla"], r2["qb"][:, (8 + 2 * g) * S:(10 + 2 * g) * S],
                          start=True, stop=True)
            pe.matmul(bank[5][:, 0:S], c2["rot_mla"], krr, start=True, stop=True).then_inc(l_rot, 1)
            sums(2, 8, 4)
            pe.wait_ge(l_k, 1)
            att_pe(pe, mla_jobs)

        def act_mla(act):
            act.wait_ge(c_ss, 1)
            for k, n in enumerate((3, 2)):
                act.activation(crs[:, k, :], bank[3 + k][:, 0:S], ACT.Sqrt, scale=1.0 / (n * 128),
                               bias=col("eps")).then_inc(c_rt, 1)
            for t in range(6):
                tile_wait(act, "uq", t)
                act.copy(qb[:, 2 * t:2 * t + 2, :], ring_bank("uq", t)[:, :].rearrange("p (m t) -> p m t", m=2))\
                   .then_inc(ring_free, 1)
            for t in range(4):
                tile_wait(act, "uk", t)
                act.copy(kb[:, 2 * t:2 * t + 2, :], ring_bank("uk", t)[:, :].rearrange("p (m t) -> p m t", m=2))\
                   .then_inc(ring_free, 1)
            for t in range(4):
                tile_wait(act, "uv", t)
                act.copy(vb[:, :, 2 * t:2 * t + 2, :],
                         ring_bank("uv", t)[:, :].rearrange("p (b h f) -> p b h f", b=TT, h=2)).then_inc(ring_free, 1)
            for g in range(8):
                act.wait_ge(l_ss, g + 1)
                if g == 4:
                    act.wait_ge(l_q, 1)
                act.activation(r2["rs"][:, 512 * (g % 4):512 * (g % 4) + 512], bank[3 + g % 4][:, :], ACT.Sqrt,
                               scale=1.0 / 192, bias=col("eps")).then_inc(l_rt, 1)
            att_act(act, mla_jobs)

        mla_jobs = [dict(n=MH + 3 * NH + h, group=MH + NH + h, first=True, last=True, kind="causal", scale=192 ** -0.5,
                         gate=None, q=[qb[:, h, :], qb[:, 8 + h // 2, :]], k=[kb[:, h, :], kro[:, h, :]], M=128,
                         v=lambda b, h=h: vb[:, b, h, :], rows=all_rows, out=oB[:, h, :], buf=att2, masks=masks2)
                    for h in range(MLH)]

        def pe_w_o(pe):
            pe.wait_ge(mix_ready, 1)
            ring_tiles(pe, "w_o", lambda slot, bk: matmul8(pe, bk[:, 0:S], slot, oA))

        f_z, f_u, f_g, f_w = sem("f_z"), sem("f_u"), sem("f_g"), sem("f_w")
        F0 = FIRST["ffn"]
        up_tile = lambda f: F0 + (0 if f == 0 else 3 * f - 1)
        down_tile = lambda f: F0 + (3 * f + 4 if f < FT - 1 else 3 * FT - 1)

        def pe_ffn(pe):
            pe.wait_ge(xn_ready, 4)

            def up(f, i):
                for k in range(2):
                    n = up_tile(f) + k
                    pe.wait_ge(landed[slot_of(n)], 16 * i + count_at(n))
                    if k == 0 and f >= 2:
                        pe.wait_ge(f_z, 2 * i + (f - 1))
                    matmul8(pe, bank[f % 2][:, k * S:(k + 1) * S], slot_of(n)).then_inc(tile_done, 1)

            def down(f, i, first=False, last=False):
                n = down_tile(f)
                pe.wait_ge(landed[slot_of(n)], 16 * i + count_at(n))
                pe.wait_ge(f_w, 2 * i + (f + 1))
                accumulate8(pe, slot_of(n), Wf[:, f % 2, :], first, last).then_inc(tile_done, 1)

            up(0, 0)
            up(1, 0)
            down(0, 0, first=True)
            with pe.Fori(0, (FT - 2) // 2) as i:
                for u in range(2):
                    up(2 + u, i)
                    down(1 + u, i)
            down(FT - 1, 0, last=True)

        def act_ffn(act):
            def z(f, i):
                act.wait_ge(tile_done, 6 * i + (up_tile(f) + 2))
                if f >= 2:
                    act.wait_ge(f_u, 2 * i + (f - 1))
                act.copy(zf[:, f % 2, :, 2:258], bank[f % 2][:, :].rearrange("p (k t) -> p k t", k=2)).then_inc(f_z, 1)

            def silu(f, i):
                act.wait_ge(f_u, 2 * i + (f + 1))
                if f >= 2:
                    act.wait_ge(f_w, 2 * i + (f - 1))
                act.activation(sgf[:, f % 2, :], uf[:, f % 2, 1, :], ACT.Silu).then_inc(f_g, 1)
            act.wait_ge(pad_ready, 1)
            for f in range(2):
                z(f, 0)
                silu(f, 0)
            with act.Fori(0, (FT - 2) // 2) as i:
                for u in range(2):
                    z(2 + u, i)
                    silu(2 + u, i)

        pad_ready = sem("pad_ready")

        def dve_ffn(dve, v):
            dve.memset(zf[:, :, :, 0:2], 0.0).then_inc(pad_ready, 1)
            taps = [sem("tap0"), sem("tap1")]

            def one(f, i):
                dve.wait_ge(f_z, 2 * i + (f + 1))
                if f >= 2:
                    dve.wait_ge(f_w, 2 * i + (f - 1))
                b = f % 2
                for k in range(2):
                    c = COL["conv"] + f * 8 + 4 * k
                    cc = (lambda x: cols[:, bass.ds(16 * i + (c + x), 1)]) if not isinstance(i, int) else \
                        (lambda x: cols[:, c + x:c + x + 1])
                    ins = dve.tensor_scalar(uf[:, b, k, :], zf[:, b, k, 2:258], cc(2), cc(3), ALU.mult, ALU.add)
                    if k == 1:
                        ins.then_inc(taps[0], 1)
                dve.wait_ge(taps[0], 2 * i + (f + 1))
                for x in (1, 0):
                    for k in range(2):
                        c = COL["conv"] + f * 8 + 4 * k
                        w = cols[:, bass.ds(16 * i + (c + x), 1)] if not isinstance(i, int) else cols[:, c + x:c + x + 1]
                        ins = dve.scalar_tensor_tensor(uf[:, b, k, :], zf[:, b, k, x:x + 256], w, uf[:, b, k, :],
                                                       ALU.mult, ALU.add)
                    ins.then_inc(taps[1] if x == 1 else f_u, 1)
                    if x == 1:
                        dve.wait_ge(taps[1], 2 * i + (f + 1))
                dve.wait_ge(f_g, 2 * i + (f + 1))
                if f >= 2:
                    dve.wait_ge(tile_done, 6 * i + (down_tile(f - 2) + 1))
                dve.tensor_tensor(Wf[:, b, :], uf[:, b, 0, :], sgf[:, b, :], ALU.mult).then_inc(f_w, 1)
            one(0, 0)
            one(1, 0)
            with dve.Fori(0, (FT - 2) // 2) as i:
                for u in range(2):
                    one(2 + u, i)
            dve.wait_ge(tile_done, TILES)
            dve_add_accs(dve, v, 11)

        def sp_out(sp):
            sp.wait_ge(acc_read, 2)
            sp.dma_start(a["out"], hT[:, :, :]).then_inc(stored, 16)
            sp.wait_ge(stored, 16)

        block = ctx.enter_context(nc.Block())

        @block.sync
        def _(sp):
            sp_loads(sp)
            sp_ada(sp)
            sp_w_in(sp)
            for name, _ in PHASES[1:]:
                sp_weights(sp, name)
            sp_out(sp)

        @block.tensor
        def _(pe):
            norm_pe(pe, 0, sq0)
            pe_ada(pe, 0, 2)
            pe_w_in(pe)
            pe_ada(pe, 2, ADA)
            pe_moba(pe)
            pe_rwkv(pe)
            pe_proj(pe)
            pe_w_out(pe)
            norm_pe(pe, 1, nsq[1])
            pe_route(pe)
            pe_turn_routes(pe)
            pe_gates(pe)
            pe_peer(pe)
            norm_pe(pe, 2, nsq[2])
            pe_w_in2(pe)
            pe_nsa(pe)
            pe_mla(pe)
            pe_w_o(pe)
            norm_pe(pe, 3, nsq[3])
            pe_ffn(pe)

        @block.scalar
        def _(act):
            act_head(act)
            norm_act(act, 0, rtn[0])
            act_w_in(act)
            act_moba(act)
            act_rwkv(act)
            act_rwkv_out(act)
            norm_act(act, 1, rtn[1])
            act_route(act)
            act_gates(act)
            act_peer(act)
            act_const2(act)
            norm_act(act, 2, rtn[2])
            act_w_in2(act)
            act_nsa(act)
            act_mla(act)
            norm_act(act, 3, rtn[3])
            act_ffn(act)

        @block.vector
        def _(dve):
            v = Steps(dve, vdone)
            dve.wait_ge(loaded, 64)
            norm_squares(dve, sq0)
            dve.wait_ge(csil_ready, 1)
            dve_ada(dve, 0, 2, 0)
            dve_ada_sum(dve, v, 0, 2)
            dve_gsc(dve, v, 0)
            norm_apply(dve, v, 0, rtn[0], 0)
            dve_ada(dve, 2, 6, 0)
            dve_ada(dve, 6, ADA, KT)
            dve_ada_sum(dve, v, 2, ADA)
            for n in range(1, 4):
                dve_gsc(dve, v, n)
            dve_shift(dve, v)
            dve_moba(dve, v)
            dve_rwkv(dve, v)
            dve_proj(dve, v)
            dve_residual(dve, "w_out", 2)
            norm_squares(dve, nsq[1])
            norm_apply(dve, v, 1, rtn[1], 3)
            dve_route(dve, v)
            dve_hot(dve)
            dve_peer(dve, v)
            norm_squares(dve, nsq[2])
            norm_apply(dve, v, 2, rtn[2], 6)
            dve_nsa(dve, v)
            dve_mla(dve, v)
            dve_residual(dve, "w_o", 8)
            norm_squares(dve, nsq[3])
            norm_apply(dve, v, 3, rtn[3], 9)
            dve_ffn(dve, v)

        @block.gpsimd
        def _(pool):
            pool_moba(pool)
            att_pool(pool, moba_jobs)
            pool_rwkv(pool)
            pool_route(pool)
            att_pool(pool, nsa_jobs)
            att_pool(pool, mla_jobs)


def column_tiles(w):
    k, n = w.shape
    return w.reshape(k // 128, 128, n // 128, 128).transpose(2, 1, 0, 3).reshape(n // 128, 128, k)


def pack_weights(x):
    w = np.zeros((TILES, 128, D), np.float32)

    def put(name, tiles, at=0):
        first = FIRST[name] + at
        w[first:first + len(tiles), :, :tiles.shape[2]] = tiles

    w_in = x["w_in"][0]
    put("w_in", column_tiles(np.concatenate([w_in[:, 1536:3328], w_in[:, 0:1536], w_in[:, 3328:]], 1)))
    put("proj", np.concatenate([column_tiles(x["w_proj_moba"][0]), column_tiles(x["w_proj_rwkv"][0])], 2))
    put("w_out", column_tiles(x["w_out"][0]))
    put("wq", column_tiles(x["peer_wq"][0]))
    u = x["peer_u"][0].reshape(NK, NK, KT, 128).transpose(1, 3, 2, 0).reshape(NK, 128, D)
    v = x["peer_v"][0].reshape(NK, NK, D).transpose(1, 0, 2)
    p0 = FIRST["peer"]
    w[p0] = u[0]
    w[p0 + 1:p0 + 2 * NK - 1:2] = u[1:]
    w[p0 + 2:p0 + 2 * NK - 1:2] = v[:-1]
    w[p0 + 2 * NK - 1] = v[-1]
    w2 = x["w_in_2"][0]
    kr = w2[:, 3224:3288]
    gate = np.concatenate([w2[:, 2560:2584], np.zeros((D, 104), np.float32)], 1)
    put("w_in2", column_tiles(np.concatenate(
        [w2[:, 0:1024], w2[:, 1536:1792], w2[:, 2048:2304], w2[:, 1024:1280], w2[:, 1280:1536], w2[:, 2584:3224],
         kr, kr, w2[:, 3288:5336], w2[:, 1792:2048], w2[:, 2304:2560], gate], 1)))
    for name in ("k", "v"):
        put(f"cmp_{name}", x[f"cmp_{name}_w1_2"][0].reshape(8, 4, 128, 256).transpose(0, 2, 1, 3).reshape(8, 128, D))
    second = [x[f"cmp_{n}_w2_2"][0].reshape(2, 128, 128).transpose(1, 0, 2).reshape(128, 256) for n in "kv"]
    put("cmp_w2", np.concatenate(second, 1)[None])
    uq = x["w_uq_2"][0].reshape(384, MLH, 192)
    uq = np.concatenate([uq[:, :, :128].reshape(384, -1), uq[:, :, 128:].reshape(384, -1)], 1)
    put("uq", column_tiles(uq).reshape(6, 2, 128, 384).transpose(0, 2, 1, 3).reshape(6, 128, 768))
    ukv = x["w_ukv_2"][0].reshape(256, MLH, 2, 128)
    put("uk", column_tiles(ukv[:, :, 0].reshape(256, -1)).reshape(4, 2, 128, 256).transpose(0, 2, 1, 3).reshape(4, 128, 512))
    put("uv", ukv[:, :, 1].reshape(2, 128, 4, 256).transpose(2, 1, 0, 3).reshape(4, 128, 512))
    put("w_o", column_tiles(x["w_o_2"][0]))
    up, down = column_tiles(x["w_up_2"][0]), x["w_down_2"][0].reshape(FT, 128, D)
    order = [up[0], up[FT]]
    for f in range(1, FT):
        order += [up[f], up[FT + f], down[f - 1]]
    put("ffn", np.stack(order + [down[FT - 1]]))
    return w


def pack_columns(x):
    turned = lambda t: t.reshape(-1, 128).T
    twice = lambda t: np.tile(t.reshape(-1), 2).reshape(128, 1)
    inv = np.float32(500000.0) ** (-(np.arange(MD // 8, dtype=np.float32) * np.float32(2.0)) / np.float32(MD // 4))
    inv64 = np.zeros(64, np.float32)
    inv64[:MD // 4] = np.tile(inv, 2)
    part = {n: turned(x[n]) for n, k in COLS if n in x and x[n].size == 128 * k}
    part["q_norm_g"], part["k_norm_g"] = twice(x["q_norm_g"]), twice(x["k_norm_g"])
    for n in "qk":
        g = x[f"mla_{n}_norm_2"].reshape(-1)
        part[f"mla_{n}_nope"], part[f"mla_{n}_rope"] = g[:128].reshape(128, 1), twice(g[128:])
        part[f"cmp_{'kv'['qk'.index(n)]}_pe"] = x[f"cmp_{'kv'['qk'.index(n)]}_pe_2"][0].T
    conv = np.concatenate([x["w_conv_2"][0], x["b_conv_2"]], 0)
    part["conv"] = conv.reshape(4, 2, FT, 128).transpose(3, 2, 1, 0).reshape(128, FT * 8)
    part["rope_inv"] = twice(inv64)
    part["eps"], part["gn_eps"] = np.full((128, 1), RMS_EPS), np.full((128, 1), GN_EPS)
    return np.ascontiguousarray(np.concatenate([part[n].astype(np.float32) for n, _ in COLS], 1))


def lay_out(x):
    x = {k: np.asarray(v) for k, v in x.items()}
    keep, const1, const2 = shape_constants()
    ada = [x[n][0].reshape(KT, 128, 6, D).transpose(2, 0, 1, 3).reshape(6 * KT, 128, D) for n in ("w_ada", "w_ada_2")]
    lora = np.zeros((128, 3, 512), np.float32)
    lora[:64, 0], lora[64:, 1], lora[:, 2] = x["rwkv_w2"][0], x["rwkv_a2"][0], x["rwkv_g2"][0]
    return {
        "xT": np.ascontiguousarray(x["x"][0].T.reshape(KT, 128, S).transpose(1, 0, 2)),
        "positions": np.ascontiguousarray(x["positions"]), "cols": pack_columns(x), "keep": keep,
        "const1": const1, "const2": const2, "ada": np.concatenate(ada), "lora": lora,
        "subk": np.ascontiguousarray(x["peer_subkeys"][0].transpose(3, 0, 1, 2).reshape(128, 2 * PH * NK)),
        "w": pack_weights(x),
    }


def kernel(**inputs):
    import concourse.bacc as bacc
    from concourse.bass_utils import run_bass_kernel_spmd

    nc = bacc.Bacc("TRN2", target_bir_lowering=False, num_devices=1)
    arrays = {f"in_{k}": v for k, v in lay_out(inputs).items()}
    a = {k[3:]: nc.dram_tensor(k, v.shape, mybir.dt.from_np(v.dtype), kind="ExternalInput").ap()
         for k, v in arrays.items()}
    a["out"] = nc.dram_tensor("out_hT", [128, KT, S], F32, kind="ExternalOutput").ap()
    build_layer_pair(nc, a)
    r = run_bass_kernel_spmd(nc, [arrays], core_ids=[0])
    hT = r.results[0]["out_hT"]
    return np.ascontiguousarray(hT.transpose(2, 1, 0).reshape(1, S, D))
```

```python
from contextlib import ExitStack

import numpy as np

import concourse.bass as bass
from concourse import mybir

F32 = mybir.dt.float32
F32R = mybir.dt.float32r
I32 = mybir.dt.int32
U32 = mybir.dt.uint32
ALU = mybir.AluOpType
ACT = mybir.ActivationFunctionType
AX = mybir.AxisListType.X

P = 128
S = 256
D = 1024
KT = D // P
TT = S // P
NEG = -1e30

MH, MD = 8, 64
RN = 64
CH = 64
NCH = S // CH
PAIRS = 4
UN = PAIRS * NCH
PH, PK = 8, 16
NK = 128
GN_EPS = 64e-5
RMS_EPS = 1e-6

NH, NG = 8, 2
CB, CS = 32, 16
NCMP = S // CS - CB // CS + 1
MLH = 8
FT = 2816 // P

PHASES = [("w_in", 42), ("proj", 8), ("w_out", 8), ("wq", 16), ("peer", 2 * NK),
          ("w_in2", 43), ("uq", 6), ("uk", 4), ("uv", 4), ("cmp_k", 8), ("cmp_v", 8), ("cmp_w2", 1),
          ("w_o", 8), ("ffn", 3 * FT)]
FIRST = {}
_n = 0
for _name, _count in PHASES:
    FIRST[_name] = _n
    _n += _count
TILES = _n
COUNT = dict(PHASES)
WIDTH = {"cmp_w2": 512, "uq": 768, "uk": 512, "uv": 512}
RINGED = ["w_in", "proj", "w_out", "wq", "w_in2", "uq", "uk", "uv", "w_o"]
RING0 = {}
_n = 0
for _name in RINGED:
    RING0[_name] = _n
    _n += COUNT[_name]
SLOTS = 6
BANKS = 3
HSLOTS = 3
SPLIT = ["w_in", "wq", "peer", "w_in2", "ffn"]
SKIP = {"w_in": 4, "w_in2": 5}
ADA = 12
ASLOTS = 4
AHALF = D // 2

COLS = [("norm1_g", 8), ("norm2_g", 8), ("attn_norm_2", 8), ("ffn_norm_2", 8),
        ("b_ada", 48), ("b_ada_2", 48), ("rwkv_mu", 14), ("rwkv_w0", 4), ("rwkv_a0", 4), ("rwkv_k_k", 4),
        ("rwkv_k_a", 4), ("rwkv_r_k", 4), ("rwkv_ln_g", 4), ("rwkv_ln_b", 4), ("q_norm_g", 1), ("k_norm_g", 1),
        ("nsa_q_norm_2", 1), ("nsa_ks_norm_2", 1), ("nsa_kw_norm_2", 1), ("nsa_kc_norm_2", 1),
        ("mla_cq_norm_2", 3), ("mla_ckv_norm_2", 2), ("mla_q_nope", 1), ("mla_q_rope", 1),
        ("mla_k_nope", 1), ("mla_k_rope", 1), ("cmp_k_pe", CB), ("cmp_v_pe", CB), ("conv", FT * 8),
        ("rope_inv", 1), ("eps", 1), ("gn_eps", 1)]
COL = {}
_n = 0
for _name, _count in COLS:
    COL[_name] = _n
    _n += _count
NCOL = _n

KEEP = [("ident", 128), ("ones", 128), ("blk64", 128)]
KEEP_AT = {n: 128 * i for i, (n, _) in enumerate(KEEP)}
NKEEP = 384
CONST1 = [("g_mask", 512), ("mL", 6 * 128), ("mT1", 128), ("causal", 384), ("rot_moba", 128)]
CONST2 = [("rot_nsa", 128), ("rot_mla", 128), ("half0", 128), ("half1", 128), ("nsa_cos", 256), ("nsa_sin", 256),
          ("mla_cos", 256), ("mla_sin", 256), ("causal", 384), ("cmp_mask", TT * NCMP), ("cmp_valid", TT)]


def offsets(parts):
    at, n = {}, 0
    for name, count in parts:
        at[name] = n
        n += count
    return at, n


C1_AT, NC1 = offsets(CONST1)
C2_AT, NC2 = offsets(CONST2)


def shape_constants():
    p, f = np.arange(128)[:, None], np.arange(128)[None, :]
    same = (p // 64) == (f // 64)
    keep = [np.eye(128), np.ones((128, 128)), same]
    strict, incl = same & (p < f), same & (p <= f)
    g_mask = np.concatenate([strict, incl, strict, incl], 1)
    level = [(p // (2 * b) == f // (2 * b)) & (p // b % 2 == 1) & (f // b % 2 == 0) for b in (1, 2, 4, 8, 16, 32)]
    q = np.arange(128)[:, None]
    causal = np.concatenate([np.where(np.arange(128)[None] <= q, 0, NEG),
                             np.where(np.arange(256)[None] <= q + 128, 0, NEG)], 1)

    def rotation(width, half):
        r = np.zeros((128, 128))
        for base in range(0, 128, width):
            for i in range(half):
                r[base + half + i, base + i] = -1.0
                r[base + i, base + half + i] = 1.0
        return r

    one = [g_mask, np.concatenate(level, 1), level[0].T, causal, rotation(MD, MD // 8)]

    def table(width):
        half = width // 2
        inv = (np.float32(10000.0) ** (-np.arange(half, dtype=np.float32) * np.float32(2.0) / np.float32(width)))
        ang = np.arange(S, dtype=np.float32)[None, :] * inv.astype(np.float32)[:, None]
        ang = np.tile(ang, (128 // half, 1))
        return [np.cos(ang), np.sin(ang)]

    t = np.arange(S).reshape(TT, 128).T[:, :, None]
    seen = (np.arange(NCMP) * CS + CB - 1)[None, None, :] <= t
    two = [rotation(128, 64), rotation(64, 32), np.tile(p < 64, (1, 128)), np.tile(p >= 64, (1, 128)),
           *table(128), *table(64), causal, np.where(seen, 0, NEG).reshape(128, -1), seen.any(-1)]
    cat = lambda parts: np.ascontiguousarray(np.concatenate([np.asarray(a, np.float32) for a in parts], 1))
    return cat(keep), cat(one), cat(two)


ARENA = 41728


def region(arena, start, parts):
    out, at = {}, start
    for name, count in parts:
        out[name] = arena[:, at:at + count]
        at += count
    assert at <= ARENA, (start, at)
    return out, at


def build_layer_pair(nc, a):
    with ExitStack() as ctx:
        def sb(name, shape, dt=F32):
            return ctx.enter_context(nc.sbuf_tensor(name, shape, dt))

        def sem(name):
            return ctx.enter_context(nc.semaphore(name))

        hT = sb("hT", [P, KT, S])
        cols = sb("cols", [P, NCOL])
        keep = sb("keep", [P, NKEEP])
        mod = sb("mod", [P, ADA * KT])
        gsc = sb("gsc", [P, 4, KT])
        part = sb("part", [P, 4])
        mod2 = sb("mod2", [P, ADA * KT])
        with ExitStack() as plain:
            def plain_sb(name, shape):
                return plain.enter_context(nc.sbuf_tensor(name, shape, F32))

            wring = plain_sb("wring", [P, SLOTS, D])
            xn = plain_sb("xn", [P, KT, S])
            arena = plain_sb("arena", [P, ARENA])
        wlo = sb("wlo", [P, SLOTS, D], F32R)
        xlo = sb("xlo", [P, KT, S], F32R)
        sb("arena_start", [P, S * NK])
        xhi = sb("xhi", [P, KT, S], F32R)
        whi = sb("whi", [P, HSLOTS, D], F32R)
        Whi = sb("Whi", [P, 3, S], F32R)
        Wlo = sb("Wlo", [P, 3, S], F32R)
        bank = [ctx.enter_context(nc.psum_tensor(f"bank{i}", [P, 512], F32)) for i in range(8)]

        ident, ones, blk64 = (keep[:, KEEP_AT[n]:KEEP_AT[n] + 128] for n in ("ident", "ones", "blk64"))

        def col(name, i=0, n=1):
            return cols[:, COL[name] + i:COL[name] + i + n]

        def modc(vec, m, n=1):
            return mod[:, vec * KT + m:vec * KT + m + n]

        def wide(ap, n):
            return ap.unsqueeze(2).to_broadcast([ap.shape[0], ap.shape[1], n])

        def over(ap, n):
            return ap.unsqueeze(1).to_broadcast([ap.shape[0], n, ap.shape[1]])

        r0, _ = region(arena, 0, [("zs", 3584), ("gates", 4096), ("g_rw", 1024), ("Pc", 1024), ("om", 1024),
                                  ("y", 1024), ("AR", 4096), ("G3", 6144), ("LT", 2048), ("BKV", 6144),
                                  ("TTm", 2048), ("BD", 6144), ("const1", NC1)])
        zs = r0["zs"].rearrange("p (m t) -> p m t", m=14)
        gates = r0["gates"].rearrange("p (m t) -> p m t", m=16)
        om = r0["om"].rearrange("p (m t) -> p m t", m=4)
        c1 = {n: r0["const1"][:, C1_AT[n]:C1_AT[n] + k] for n, k in CONST1}
        rA, _ = region(arena, 11776, [("qk", 2048), ("vtok", 1024)])
        rA.update(region(arena, 27136, [("crow", D), ("aring", ASLOTS * D), ("pos", 256)])[0])
        sq0 = arena[:, 3584:3584 + 2048].rearrange("p (m t) -> p m t", m=KT)
        qk = rA["qk"].rearrange("p (m t) -> p m t", m=8)
        vtok = rA["vtok"].rearrange("p (b f) -> p b f", b=TT)
        crow = rA["crow"]
        aring = rA["aring"].rearrange("p (s n) -> p s n", s=ASLOTS)
        zraw = arena[:, 7680:7680 + 14 * 257].rearrange("p (m t) -> p m t", m=14)
        posi = rA["pos"].bitcast(I32)
        rM, _ = region(arena, 15872, [("sq", 2048), ("rt", 2048), ("qn", 2048), ("t1", 2048), ("kz", 2048),
                                      ("cos", 256), ("sin", 256), ("ang", 256), ("kf", 256)])
        rR, _ = region(arena, 15872, [(n, 1024) for n in
                                      ("lw", "cum", "cml", "Pinv", "Pprev", "kk", "av", "sqk", "rtk", "t1", "rmask")]
                       + [("lora", 512)])
        Pc = r0["Pc"]
        g_rw = r0["g_rw"].rearrange("p (m t) -> p m t", m=4)
        yb = r0["y"]
        ARt = r0["AR"].rearrange("p (u k f) -> p u k f", u=UN, k=2)
        G3 = r0["G3"].rearrange("p (u k f) -> p u k f", u=UN, k=3)
        LT = r0["LT"].rearrange("p (u f) -> p u f", u=UN)
        BKV = r0["BKV"].rearrange("p (u k f) -> p u k f", u=UN, k=3)
        TTm = r0["TTm"].rearrange("p (u f) -> p u f", u=UN)
        BD = r0["BD"].rearrange("p (k u f) -> p k u f", k=3, u=UN)
        Tm = r0["BD"][:, 0:2048].rearrange("p (u f) -> p u f", u=UN)
        Xm = r0["BD"][:, 2048:4096].rearrange("p (u f) -> p u f", u=UN)
        st = r0["LT"][:, 0:1024].rearrange("p (b q f) -> p b q f", b=2, q=PAIRS)
        usb = r0["LT"][:, 1024:1536].rearrange("p (q f) -> p q f", q=PAIRS)
        sasb = r0["LT"][:, 1536:2048].rearrange("p (q f) -> p q f", q=PAIRS)
        rP, _ = region(arena, 15872, [("yc", 1024), ("ysq", 1024), ("rt", 1024), ("rk", 1024), ("bon", 1024)])
        mix1 = r0["AR"][:, 0:2048].rearrange("p (m t) -> p m t", m=KT)
        mixt = r0["AR"][:, 2048:3072].rearrange("p (b k t) -> p b k t", b=2, k=2)
        att1, _ = region(arena, 28160, [("sm", 768), ("pe", 1152), ("pt", 768), ("mx", 12), ("sm2", 24)])

        G = arena[:, 0:S * NK].rearrange("p (t j) -> p t j", t=S)
        rG, _ = region(arena, S * NK + KT * S, [("T3", 768), ("A8", 2048), ("B8", 2048)])
        after_w = S * NK + KT * S + HSLOTS * D + 6 * S
        rG.update(region(arena, after_w, [("ge", 768), ("iota", 128), ("iotai", 128)])[0])
        rG.update(region(arena, after_w + 768, [("crow2", D), ("half", AHALF)])[0])

        T3 = rG["T3"].rearrange("p (k t) -> p k t", k=3)
        A8 = rG["A8"].rearrange("p (b t i) -> p b t i", b=2, t=8)
        B8 = rG["B8"].rearrange("p (b t i) -> p b t i", b=2, t=8)
        ge = rG["ge"].rearrange("p (b t) -> p b t", b=3)
        NR = TT * 2 * PH
        NQ = TT * PH
        rK, _ = region(arena, 0, [("qp", 4096), ("sc", 4096), ("subk", 2048), ("scr", 512), ("tv", 512), ("ti", 512),
                                  ("tif", 512), ("cand", 4096), ("best", 256), ("bi", 256), ("ba", 512),
                                  ("baf", 512), ("big", 4096), ("pick", 512), ("gate", 256), ("gsum", 32),
                                  ("scr2", 1024), ("sq", 2048)])
        qp = rK["qp"].rearrange("p (m t) -> p m t", m=16)
        sc = rK["sc"].rearrange("p (r n) -> p r n", r=NR)
        subk = rK["subk"].rearrange("p (r n) -> p r n", r=16)
        tv = rK["tv"].rearrange("p (r k) -> p r k", r=NR)
        ti = rK["ti"].bitcast(U32).rearrange("p (r k) -> p r k", r=NR)
        tif = rK["tif"].rearrange("p (r k) -> p r k", r=NR)
        cand = rK["cand"].rearrange("p (r x) -> p r x", r=NQ)
        best = rK["best"].rearrange("p (r k) -> p r k", r=NQ)
        bi = rK["bi"].bitcast(U32).rearrange("p (r k) -> p r k", r=NQ)
        ba = rK["ba"].bitcast(U32).rearrange("p (h r) -> p h r", h=2)
        baf = rK["baf"].rearrange("p (h r) -> p h r", h=2)
        pick = rK["pick"].rearrange("p (h r) -> p h r", h=2)
        gate = rK["gate"].rearrange("p (r k) -> p r k", r=NQ)

        r2, _ = region(arena, 0, [("F2", 22 * 256), ("bg", 4096), ("vs", 512), ("vw", 512), ("vb", 2048),
                                  ("gt", 48), ("rs", 3072), ("sq", 3584), ("rot", 3584), ("qb", 3072), ("kb", 2048),
                                  ("XP", 2 * CB * 30), ("const2", NC2), ("hid", 256), ("hidT", 64), ("cmt", 512),
                                  ("kcT", 32), ("kst", 8), ("oA", 2048), ("oB", 2048), ("at", 2736)])
        F2 = r2["F2"].rearrange("p (m t) -> p m t", m=22)
        bg = r2["bg"].rearrange("p (m t) -> p m t", m=16)
        vs2 = r2["vs"].rearrange("p (b f) -> p b f", b=TT)
        vw2 = r2["vw"].rearrange("p (b f) -> p b f", b=TT)
        vb = r2["vb"].rearrange("p (b h f) -> p b h f", b=TT, h=MLH)
        gt2 = r2["gt"].rearrange("p (b k) -> p b k", b=TT)
        rs12 = r2["rs"].rearrange("p (m t) -> p m t", m=12)
        sq14 = r2["sq"].rearrange("p (m t) -> p m t", m=14)
        ro14 = r2["rot"].rearrange("p (m t) -> p m t", m=14)
        qb = r2["qb"].rearrange("p (m t) -> p m t", m=12)
        kb = r2["kb"].rearrange("p (m t) -> p m t", m=8)
        XP = r2["XP"].rearrange("p (v l n) -> p v l n", v=2, l=CB)
        c2 = {n: r2["const2"][:, C2_AT[n]:C2_AT[n] + k] for n, k in CONST2}
        oA = r2["oA"].rearrange("p (m t) -> p m t", m=NH)
        oB = r2["oB"].rearrange("p (m t) -> p m t", m=NH)
        att2, _ = region(r2["at"], 0, [("sm", 768), ("pe", 1152), ("pt", 768), ("mx", 12), ("sm2", 24)])
        sq3 = r2["sq"][:, 0:2048].rearrange("p (m t) -> p m t", m=KT)
        rF, _ = region(arena, 0, [("z", 2 * 2 * 258), ("u", 2 * 2 * 256), ("sg", 512), ("W", 512), ("sq", 2048)])
        zf = rF["z"].rearrange("p (b k t) -> p b k t", b=2, k=2)
        uf = rF["u"].rearrange("p (b k t) -> p b k t", b=2, k=2)
        sgf = rF["sg"].rearrange("p (b t) -> p b t", b=2)
        Wf = rF["W"].rearrange("p (b t) -> p b t", b=2)

        loaded = sem("loaded")
        c1_loaded, subk_loaded, c2_loaded = sem("c1_loaded"), sem("subk_loaded"), sem("c2_loaded")
        landed = [sem(f"landed{i}") for i in range(SLOTS)]
        tile_done = sem("tile_done")
        ring_free = sem("ring_free")
        alanded = [sem(f"alanded{i}") for i in range(ASLOTS)]
        ada_used = sem("ada_used")
        stored = sem("stored")
        vdone = sem("vdone")
        gdone = sem("gdone")
        sq_ready, ss_ready, rt_ready, xn_ready = sem("sq_ready"), sem("ss_ready"), sem("rt_ready"), sem("xn_ready")
        crow_loaded, crow_ready = sem("crow_loaded"), sem("crow_ready")
        half_landed, half_free, half_kept = sem("half_landed"), sem("half_free"), sem("half_kept")

        slot_of = lambda n: n % SLOTS
        count_at = lambda n: 16 * (n // SLOTS + 1)

        class Steps:

            def __init__(self, eng, s):
                self.eng, self.s, self.n = eng, s, 0

            def did(self, ins):
                ins.then_inc(self.s, 1)
                self.n += 1
                return self.n

            def settle(self):
                self.eng.wait_ge(self.s, self.n)

            def then(self, ins):
                self.did(ins)
                self.settle()

        def blocks(slot, k, width=128, at=0):
            return wring[:, slot, at + k * width:at + (k + 1) * width]

        def ring_tiles(pe, name, body):
            first, count, ring0 = FIRST[name], COUNT[name], RING0[name]

            def one(slot, bk, landing, ring_n):
                pe.wait_ge(landed[slot], landing)
                if ring_n is not None:
                    pe.wait_ge(ring_free, ring_n)
                body(slot, bank[bk]).then_inc(tile_done, 1)

            rounds = count // SLOTS if count >= 2 * SLOTS else 0
            n = 0
            if rounds and ring0 < BANKS:
                for u in range(SLOTS):
                    free = ring0 + u - BANKS + 1
                    one(slot_of(first + u), (ring0 + u) % BANKS, count_at(first + u), free if free > 0 else None)
                n, rounds = SLOTS, rounds - 1
            if rounds:
                with pe.Fori(0, rounds) as i:
                    for u in range(SLOTS):
                        t = first + n + u
                        one(slot_of(t), (ring0 + n + u) % BANKS, 16 * i + count_at(t),
                            SLOTS * i + (ring0 + n + u - BANKS + 1))
                n += rounds * SLOTS
            for k in range(n, count):
                one(slot_of(first + k), (ring0 + k) % BANKS, count_at(first + k), ring0 + k - BANKS + 1)

        def ring_tiles_split(pe, name, k0=None, k1=None):
            first, ring0 = FIRST[name], RING0[name]
            k0 = SKIP.get(name, 0) if k0 is None else k0
            k1 = COUNT[name] if k1 is None else k1

            def one(k, i=0):
                n = first + k
                pe.wait_ge(lo_ready, SLOTS * i + nth_split[n])
                pe.wait_ge(ring_free, SLOTS * i + (ring0 + k - BANKS + 1))
                split8(pe, bank[(ring0 + k) % BANKS][:, 0:S], n).then_inc(tile_done, 1)

            rounds = (k1 - k0) // SLOTS if k1 - k0 >= 2 * SLOTS else 0
            if rounds:
                with pe.Fori(0, rounds) as i:
                    for k in range(k0, k0 + SLOTS):
                        one(k, i)
            for k in range(k0 + rounds * SLOTS, k1):
                one(k)

        def act_hi_of(act, name, k):
            n = FIRST[name] + k
            if k < COUNT[name]:
                act_hi(act, n, count_at(n), n - HSLOTS + 1)

        def lo_phase(eng, name, k0=None, k1=None):
            k0 = SKIP.get(name, 0) if k0 is None else k0
            k1 = COUNT[name] if k1 is None else k1
            first, rounds = FIRST[name], (k1 - k0) // SLOTS
            with eng.Fori(0, rounds) as i:
                for n in range(first + k0, first + k0 + SLOTS):
                    tile_lo(eng, n, SLOTS * i + nth_split[n])
            for n in range(first + k0 + rounds * SLOTS, first + k1):
                tile_lo(eng, n, nth_split[n])

        def matmul8(pe, out, slot, x=None):
            x = xn if x is None else x
            for k in range(KT):
                mm = pe.matmul(out, blocks(slot, k), x[:, k, :], start=(k == 0), stop=(k == KT - 1))
            return mm

        hi_ready, lo_ready = sem("hi_ready"), sem("lo_ready")
        x_hi, x_lo = sem("x_hi"), sem("x_lo")
        split_tiles = [FIRST[name] + k for name in SPLIT for k in range(SKIP.get(name, 0), COUNT[name])]
        nth_split = {n: i + 1 for i, n in enumerate(split_tiles)}

        def act_hi(act, n, landing, used):
            act.wait_ge(landed[n % SLOTS], landing)
            if used is not None:
                act.wait_ge(tile_done, used)
            act.copy(whi[:, n % HSLOTS, :], wring[:, n % SLOTS, :]).then_inc(hi_ready, 1)

        def tile_lo(eng, n, upper):
            eng.wait_ge(hi_ready, upper)
            eng.tensor_tensor(wlo[:, n % SLOTS, :], wring[:, n % SLOTS, :], whi[:, n % HSLOTS, :].bitcast(F32),
                              ALU.subtract).then_inc(lo_ready, 1)

        def three(pe, out, n, k, xh, xl, start, stop, **kw):
            h, l = whi[:, n % HSLOTS, k * 128:k * 128 + 128], wlo[:, n % SLOTS, k * 128:k * 128 + 128]
            pe.matmul(out, h, xh, start=start, stop=False, **kw)
            pe.matmul(out, h, xl, start=False, stop=False, **kw)
            return pe.matmul(out, l, xh, start=False, stop=stop, **kw)

        def split8(pe, out, n):
            for k in range(KT):
                mm = three(pe, out, n, k, xhi[:, k, :], xlo[:, k, :], k == 0, k == KT - 1)
            return mm

        def matmul8_tokens(pe, bk, slot, width=128):
            for b in range(TT):
                for k in range(KT):
                    mm = pe.matmul(bk[:, b * width:(b + 1) * width], xn[:, k, b * 128:(b + 1) * 128],
                                   blocks(slot, k), start=(k == 0), stop=(k == KT - 1))
            return mm

        def tile_wait(eng, name, k):
            eng.wait_ge(tile_done, FIRST[name] + k + 1)

        def ring_bank(name, k):
            return bank[(RING0[name] + k) % BANKS]

        def norm_pe(pe, n, sq):
            pe.wait_ge(sq_ready, n + 1)
            for k in range(KT):
                mm = pe.matmul(bank[3][:, 0:S], ones, sq[:, k, :], start=(k == 0), stop=(k == KT - 1))
            mm.then_inc(ss_ready, 1)

        def norm_act(act, n, rt):
            act.wait_ge(ss_ready, n + 1)
            act.activation(rt, bank[3][:, 0:S], ACT.Sqrt, scale=1.0 / D, bias=col("eps")).then_inc(rt_ready, 1)

        def norm_squares(dve, sq):
            dve.tensor_tensor(sq[:, :, :], hT[:, :, :], hT[:, :, :], ALU.mult).then_inc(sq_ready, 1)

        def norm_scale(dve, v, n, rt):
            dve.wait_ge(rt_ready, n + 1)
            v.then(dve.reciprocal(rt, rt))
            v.then(dve.tensor_tensor(xn[:, :, :], hT[:, :, :], over(rt, KT), ALU.mult))

        def norm_shift(dve, n, shift):
            for k in range(KT):
                dve.tensor_scalar(xn[:, k, :], xn[:, k, :], gsc[:, n, k:k + 1], modc(shift, k),
                                  ALU.mult, ALU.add).then_inc(xn_ready, 1)

        def x_upper(act, n):
            for k in range(KT):
                act.wait_ge(xn_ready, KT * n + k + 1)
                act.copy(xhi[:, k, :], xn[:, k, :]).then_inc(x_hi, 1)

        def x_rest(eng, n):
            for k in range(0, KT, 2):
                eng.wait_ge(x_hi, KT * n + k + 2)
                eng.tensor_tensor(xlo[:, k:k + 2, :], xn[:, k:k + 2, :], xhi[:, k:k + 2, :].bitcast(F32),
                                  ALU.subtract).then_inc(x_lo, 1)


        nsq = [sq0, rK["sq"].rearrange("p (m t) -> p m t", m=KT), sq3, rF["sq"].rearrange("p (m t) -> p m t", m=KT)]
        rtn = [arena[:, 5632:5888], arena[:, 28672:28928], r2["rot"][:, 0:256], rF["sg"][:, 0:256]]

        a_score, a_max, a_exp, a_rec = sem("a_score"), sem("a_max"), sem("a_exp"), sem("a_rec")
        a_prob, a_turn, a_pt, a_out, a_free = (sem("a_prob"), sem("a_turn"), sem("a_pt"), sem("a_out"), sem("a_free"))
        CAUSAL = [(0, 128), (128, 256)]
        CMP = [(0, NCMP), (NCMP, NCMP)]

        def spans(job):
            return CAUSAL if job["kind"] == "causal" else CMP

        def turns(jobs, *stages):
            first, last = jobs[0]["n"], jobs[-1]["n"]
            for t in range(first - 3, last + 3):
                for ahead, stage in stages:
                    if first <= t + ahead <= last:
                        stage(jobs[t + ahead - first])

        def att_pe(pe, jobs):
            def scores(j):
                n, bk = j["n"], bank[j["n"] % 2]
                if n >= 2:
                    pe.wait_ge(a_max, n - 1)
                for b, (at, w) in enumerate(spans(j)):
                    for i, (q, k) in enumerate(zip(j["q"], j["k"])):
                        mm = pe.matmul(bk[:, at:at + w], q[:, b * 128:(b + 1) * 128], k[:, 0:w],
                                       start=(i == 0), stop=(i == len(j["q"]) - 1))
                mm.then_inc(a_score, 1)

            def turn(j):
                n = j["n"]
                pe.wait_ge(a_prob, n + 1)
                if n >= 2:
                    pe.wait_ge(a_pt, n - 1)
                p = j["buf"]["pe"][:, (n % 3) * 384:(n % 3) * 384 + 384]
                bk = bank[3 + n % 2]
                if j["kind"] == "causal":
                    for k in range(3):
                        mm = pe.transpose(bk[:, k * 128:(k + 1) * 128], p[:, k * 128:(k + 1) * 128], ident)
                else:
                    for b in range(TT):
                        mm = pe.transpose(bk[0:NCMP, b * 128:(b + 1) * 128], p[:, b * NCMP:(b + 1) * NCMP], ident)
                mm.then_inc(a_turn, 1)

            def values(j):
                n, g = j["n"], j["group"]
                pe.wait_ge(a_pt, n + 1)
                if j["first"] and g >= 2:
                    pe.wait_ge(a_free, g - 1)
                pt = j["buf"]["pt"][:, (n % 2) * 384:(n % 2) * 384 + 384]
                out = bank[6 + g % 2][0:j["M"], 0:S]
                if j["kind"] == "causal":
                    pe.matmul(out, j["v"](0), pt[:, 0:256], start=j["first"], stop=False)
                    mm = pe.matmul(out[:, 128:256], j["v"](1), pt[:, 256:384], start=False, stop=j["last"])
                else:
                    mm = pe.matmul(out, j["v"](0), pt[0:NCMP, 0:256], start=j["first"], stop=j["last"])
                mm.then_inc(a_out, 1)

            turns(jobs, (3, scores), (0, turn), (-1, values))

        def att_act(act, jobs):
            def exps(j):
                n, buf = j["n"], j["buf"]
                act.wait_ge(a_max, n + 1)
                if n >= 3:
                    act.wait_ge(a_turn, n - 2)
                o, m = (n % 2) * 384, (n % 3) * 384
                for b, (at, w) in enumerate(spans(j)):
                    ins = act.activation(buf["pe"][:, m + at:m + at + w], buf["sm"][:, o + at:o + at + w], ACT.Exp,
                                         bias=buf["mx"][:, 4 * (n % 3) + 2 + b:4 * (n % 3) + 3 + b],
                                         accum_out=buf["sm2"][:, 8 * (n % 3) + b:8 * (n % 3) + b + 1])
                ins.then_inc(a_exp, 1)

            def copy(j):
                n, buf = j["n"], j["buf"]
                act.wait_ge(a_turn, n + 1)
                if n >= 2:
                    act.wait_ge(a_out, n - 1)
                o = (n % 2) * 384
                if j["kind"] == "causal":
                    ins = act.copy(buf["pt"][:, o:o + 384], bank[3 + n % 2][:, 0:384])
                else:
                    ins = act.copy(buf["pt"][0:NCMP, o:o + 256], bank[3 + n % 2][0:NCMP, 0:256])
                ins.then_inc(a_pt, 1)

            turns(jobs, (2, exps), (0, copy))

        def att_dve(dve, v, jobs):
            def maxima(j):
                n, buf, mask = j["n"], j["buf"], j["masks"][j["kind"]]
                dve.wait_ge(a_score, n + 1)
                if n >= 2:
                    dve.wait_ge(a_exp, n - 1)
                o, mx = (n % 2) * 384, buf["mx"][:, 4 * (n % 3):4 * (n % 3) + 4]
                for b, (at, w) in enumerate(spans(j)):
                    ins = dve.tensor_tensor_reduce(buf["sm"][:, o + at:o + at + w], bank[n % 2][:, at:at + w],
                                                   mask[:, at:at + w], j["scale"], -3e38,
                                                   ALU.add, ALU.max, mx[:, b:b + 1])
                v.then(ins)
                dve.tensor_scalar(mx[:, 2:4], mx[:, 0:2], -1.0, None, ALU.mult).then_inc(a_max, 1)

            def reciprocals(j):
                n = j["n"]
                dve.wait_ge(a_exp, n + 1)
                if n >= 3:
                    dve.wait_ge(a_prob, n - 2)
                s = j["buf"]["sm2"][:, 8 * (n % 3):8 * (n % 3) + 8]
                if j["gate"] is None:
                    dve.reciprocal(s[:, 4:6], s[:, 0:2]).then_inc(a_rec, 1)
                else:
                    v.then(dve.reciprocal(s[:, 2:4], s[:, 0:2]))
                    dve.tensor_tensor(s[:, 4:6], s[:, 2:4], j["gate"], ALU.mult).then_inc(a_rec, 1)

            def output(j):
                if j["last"]:
                    dve.wait_ge(a_out, j["n"] + 1)
                    dve.tensor_copy(j["out"], bank[6 + j["group"] % 2][j["rows"], 0:S]).then_inc(a_free, 1)

            turns(jobs, (3, maxima), (1, reciprocals), (-2, output))

        def att_pool(pool, jobs):
            for j in jobs:
                n, buf = j["n"], j["buf"]
                pool.wait_ge(a_rec, n + 1)
                o = (n % 3) * 384
                for b, (at, w) in enumerate(spans(j)):
                    p = buf["pe"][:, o + at:o + at + w]
                    f = 8 * (n % 3) + 4 + b
                    ins = pool.tensor_scalar(p, p, buf["sm2"][:, f:f + 1], None, ALU.mult)
                ins.then_inc(a_prob, 1)

        all_rows, lo, hi = slice(0, 128), slice(0, 64), slice(64, 128)
        kz = rM["kz"].rearrange("p (h t) -> p h t", h=MH)
        qr = rM["qn"].rearrange("p (m t) -> p m t", m=8)
        moba_jobs = [dict(n=h, group=h, first=True, last=True, kind="causal", scale=MD ** -0.5, gate=None,
                          q=[qr[:, h // 2, :]], k=[kz[:, h, :]], M=128, buf=att1,
                          v=lambda b, h=h: vtok[:, b, (h // 2) * 128:(h // 2) * 128 + 128],
                          rows=(lo, hi)[h % 2], out=om[(lo, hi)[h % 2], h // 2, :], masks=dict(causal=c1["causal"]))
                     for h in range(MH)]

        def sp_loads(sp):
            for dst, src in ((cols[:, :], a["cols"]), (keep[:, :], a["keep"]), (hT[:, :, :], a["xT"]),
                             (posi, a["positions"].to_broadcast([P, S]))):
                sp.dma_start(dst, src).then_inc(loaded, 16)

        def sp_ada(sp):
            sp.dma_start(crow, a["crow"][0:1, :].to_broadcast([P, D])).then_inc(crow_loaded, 16)
            for t in range(2 * KT):
                if t == ASLOTS:
                    sp_loads(sp)
                if t >= ASLOTS:
                    sp.wait_ge(ada_used, t - ASLOTS + 1)
                sp.dma_start(aring[:, t % ASLOTS, :], a["ada"][t]).then_inc(alanded[t % ASLOTS], 16)

        def sp_w_in(sp):
            def tile(t, i=0):
                sp.wait_ge(tile_done, 12 * i + (t - SLOTS + 1))
                sp.dma_start(wring[:, t % SLOTS, :], a["w"][12 * i + t]).then_inc(landed[t % SLOTS], 16)

            def ada(n, i=0):
                sp.wait_ge(ada_used, 12 * i + (n - ASLOTS + 1))
                sp.dma_start(aring[:, n % ASLOTS, :], a["ada"][12 * i + n]).then_inc(alanded[n % ASLOTS], 16)

            rest = 6 * KT - 2 * KT
            for t in range(SLOTS):
                sp.dma_start(wring[:, t, :], a["w"][t]).then_inc(landed[t], 16)
            sp.dma_start(r0["const1"], a["const1"]).then_inc(c1_loaded, 16)
            turn = 12
            with sp.Fori(0, rest // turn) as i:
                for u in range(turn):
                    tile(SLOTS + u, i)
                    ada(2 * KT + u, i)
            for k in range(rest // turn * turn, COUNT["w_in"] - SLOTS):
                tile(SLOTS + k)
                if k < rest:
                    ada(2 * KT + k)

        def sp_weights(sp, name, skip=0):
            first, count, w = FIRST[name] + skip, COUNT[name] - skip, WIDTH.get(name, D)

            def one(slot, n, freed):
                sp.wait_ge(tile_done, freed)
                sp.dma_start(wring[:, slot, 0:w], a["w"][n][:, 0:w]).then_inc(landed[slot], 16)

            rounds = count // SLOTS if count >= 2 * SLOTS else 0
            if rounds:
                with sp.Fori(0, rounds) as i:
                    for u in range(SLOTS):
                        one(slot_of(first + u), SLOTS * i + (first + u), SLOTS * i + (first + u - SLOTS + 1))
            for k in range(rounds * SLOTS, count):
                one(slot_of(first + k), first + k, first + k - SLOTS + 1)

        def sp_peer(sp):
            def tile(u, i):
                n = P0 + u
                sp.wait_ge(tile_done, SLOTS * i + (n - SLOTS + 1))
                sp.dma_start(wring[:, n % SLOTS, :], a["w"][SLOTS * i + n]).then_inc(landed[n % SLOTS], 16)

            def half(u, i):
                sp.wait_ge(half_free, 3 * i + (u - 5))
                sp.dma_start(rG["half"], a["ada2"][3 * i + (u - 6)]).then_inc(half_landed, 16)

            with_half = 2 + 2 * 6 * KT // 3
            for start, end in ((0, 2), (2, with_half), (with_half, COUNT["peer"] // SLOTS)):
                with sp.Fori(start, end) as i:
                    for u in range(SLOTS):
                        tile(u, i)
                        if start == 2 and u % 2 == 0:
                            half(u // 2, i)
            for u in range(COUNT["peer"] // SLOTS * SLOTS, COUNT["peer"]):
                tile(u, 0)

        def act_head(act):
            act.wait_ge(crow_loaded, 16)
            act.activation(crow, crow, ACT.Silu).then_inc(crow_ready, 1)

        def dve_ada(dve, n):
            dve.wait_ge(alanded[n % ASLOTS], 16 * (n // ASLOTS + 1))
            src = aring[:, n % ASLOTS, :]
            dve.tensor_tensor_reduce(src, src, crow, 1.0, 0.0, ALU.mult, ALU.add, mod[:, n:n + 1]).then_inc(ada_used, 1)

        def dve_add_bias(dve, v, lo_m, hi_m):
            v.then(dve.tensor_tensor(mod[:, lo_m:hi_m], mod[:, lo_m:hi_m],
                                     cols[:, COL["b_ada"] + lo_m:COL["b_ada"] + hi_m], ALU.add))

        def dve_gsc(dve, v, n):
            gain = ("norm1_g", "norm2_g", "attn_norm_2", "ffn_norm_2")[n]
            v.then(dve.scalar_tensor_tensor(gsc[:, n, :], modc(3 * n + 1, 0, KT), 1.0, col(gain, 0, KT),
                                            ALU.add, ALU.mult))

        def pe_w_in(pe):
            pe.wait_ge(xn_ready, KT)

            for t in range(4):
                pe.wait_ge(landed[t], 16)
                if t >= BANKS:
                    pe.wait_ge(ring_free, t - BANKS + 1)
                matmul8_tokens(pe, bank[t % BANKS], t).then_inc(tile_done, 1)
            pe.wait_ge(x_lo, 4)
            ring_tiles_split(pe, "w_in", 4, MB_SUMS_AT)
            pe_moba_sums(pe)
            ring_tiles_split(pe, "w_in", MB_SUMS_AT, MB_ROT_AT)
            pe_moba_turn(pe)
            ring_tiles_split(pe, "w_in", MB_ROT_AT, 42)

        MB_SUMS_AT, MB_ROT_AT = 31, 40

        def act_w_in(act):
            for t in range(42):
                if t + 2 >= SKIP["w_in"]:
                    act_hi_of(act, "w_in", t + 2)
                tile_wait(act, "w_in", t)
                bk = bank[t % BANKS]
                if t < 4:
                    ins = act.copy(vtok[:, :, t * 128:(t + 1) * 128], bk[:, 0:S].rearrange("p (b f) -> p b f", b=TT))
                elif t < 18:
                    ins = act.copy(zraw[:, t - 4, 1:257], bk[:, 0:S])
                elif t < 26:
                    ins = act.copy(qk[:, t - 18, :], bk[:, 0:S])
                else:
                    ins = act.activation(gates[:, t - 26, :], bk[:, 0:S], ACT.Sigmoid)
                ins.then_inc(ring_free, 1)
                if t == MB_SUMS_AT - 1:
                    act_moba_roots(act)

        def pool_w_in(pool):
            pool.wait_ge(tile_done, 4)
            x_rest(pool, 0)
            lo_phase(pool, "w_in")

        mb_sq, mb_ss, mb_rt, mb_qn, mb_rot, mb_q = (sem("mb_sq"), sem("mb_ss"), sem("mb_rt"), sem("mb_qn"),
                                                    sem("mb_rot"), sem("mb_q"))
        trig_arg, trig = sem("trig_arg"), sem("trig")
        zk_clear = sem("zk_clear")
        msq, mrt, mqn, mt1 = rM["sq"], rM["rt"], rM["qn"], rM["t1"]

        def dve_shift(dve, v):
            dve.wait_ge(ring_free, 18)
            v.then(dve.memset(zraw[:, :, 0:1], 0.0))
            v.then(dve.tensor_tensor(zs[:, :, :], zraw[:, :, 0:S], zraw[:, :, 1:S + 1], ALU.subtract))
            for m in range(14):
                ins = dve.scalar_tensor_tensor(zs[:, m, :], zs[:, m, :], col("rwkv_mu", m), zraw[:, m, 1:S + 1],
                                               ALU.mult, ALU.add)
            v.then(ins)

        def dve_trig(dve, v):
            ang, kf, sn, cs = rM["ang"], rM["kf"], rM["sin"], rM["cos"]
            v.then(dve.tensor_copy(ang, posi))
            v.then(dve.tensor_scalar(ang, ang, col("rope_inv"), None, ALU.mult))
            v.then(dve.tensor_scalar(kf, ang, 1.0 / (2 * np.pi), 12582912.0, ALU.mult, ALU.add))
            v.then(dve.tensor_scalar(kf, kf, 12582912.0, None, ALU.subtract))
            rest = 2 * np.pi
            for bits in (6.28125, None, 0):
                if bits is None:
                    bits = float(np.float32(np.round(rest * 2 ** 20) / 2 ** 20))
                elif bits == 0:
                    bits = float(np.float32(rest))
                v.then(dve.scalar_tensor_tensor(ang, kf, -bits, ang, ALU.mult, ALU.add))
                rest -= bits
            v.then(dve.tensor_scalar(ang, ang, float(np.float32(3.1415925)), -float(np.float32(3.1415925)),
                                     ALU.min, ALU.max))
            v.then(dve.tensor_scalar(cs, ang, -1.0, None, ALU.mult))
            v.then(dve.tensor_tensor(cs, cs, ang, ALU.min))
            dve.tensor_scalar(cs, cs, float(np.pi / 2), None, ALU.add).then_inc(trig_arg, 1)

        def act_trig(act):
            act.wait_ge(trig_arg, 1)
            act.activation(rM["sin"], rM["ang"], ACT.Sin)
            act.activation(rM["cos"], rM["cos"], ACT.Sin).then_inc(trig, 1)

        def pool_moba(pool):
            pool.memset(rM["kz"], 0.0).then_inc(zk_clear, 1)

        SHIFT_AT, MOBA_AT = 34, 42

        def dve_moba_start(dve, v):
            dve.wait_ge(ring_free, 26)
            dve.tensor_tensor(msq, rA["qk"], rA["qk"], ALU.mult).then_inc(mb_sq, 1)
            dve_trig(dve, v)

        def dve_moba(dve, v):
            dve.wait_ge(mb_rt, 4)
            v.then(dve.reciprocal(mrt, mrt))
            for i, g in enumerate(("q_norm_g", "k_norm_g")):
                ins = dve.scalar_tensor_tensor(mqn[:, 1024 * i:1024 * i + 1024], rA["qk"][:, 1024 * i:1024 * i + 1024],
                                               col(g), mrt[:, 1024 * i:1024 * i + 1024], ALU.mult, ALU.mult)
                ins.then_inc(mb_qn, 1)
            dve.wait_ge(mb_qn, 2)
            dve.wait_ge(trig, 1)
            v.then(dve.tensor_tensor(mt1.rearrange("p (m t) -> p m t", m=8), qr[:, :, :], over(rM["cos"], 8), ALU.mult))
            dve.wait_ge(mb_rot, 1)
            for g in range(4):
                ins = dve.tensor_tensor(msq.rearrange("p (m t) -> p m t", m=8)[:, 2 * g:2 * g + 2, :],
                                        bank[3 + g][:, :].rearrange("p (m t) -> p m t", m=2), over(rM["sin"], 2),
                                        ALU.mult)
            v.then(ins)
            dve.wait_ge(zk_clear, 1)
            dve.tensor_tensor(mqn[:, 0:1024], mt1[:, 0:1024], msq[:, 0:1024], ALU.add).then_inc(mb_q, 1)
            for h, r in enumerate((lo, hi)):
                dve.tensor_tensor(kz[r, h::2, :], mt1[r, 1024:2048].rearrange("p (m t) -> p m t", m=4),
                                  msq[r, 1024:2048].rearrange("p (m t) -> p m t", m=4), ALU.add).then_inc(mb_q, 1)
            att_dve(dve, v, moba_jobs)

        def pe_moba_sums(pe):
            pe.wait_ge(mb_sq, 1)
            for g in range(4):
                mm = pe.matmul(bank[3 + g][:, :], blk64, msq[:, 512 * g:512 * g + 512], start=True, stop=True)
            mm.then_inc(mb_ss, 1)

        def pe_moba_turn(pe):
            pe.wait_ge(mb_qn, 2)
            pe.wait_ge(c1_loaded, 16)
            for g in range(4):
                mm = pe.matmul(bank[3 + g][:, :], c1["rot_moba"], mqn[:, 512 * g:512 * g + 512], start=True, stop=True)
            mm.then_inc(mb_rot, 1)

        def pe_moba(pe):
            pe.wait_ge(ring_free, COUNT["w_in"])
            pe.wait_ge(mb_q, 3)
            att_pe(pe, moba_jobs)

        def act_moba_roots(act):
            act.wait_ge(mb_ss, 1)
            for g in range(4):
                act.activation(mrt[:, 512 * g:512 * g + 512], bank[3 + g][:, :], ACT.Sqrt, scale=1.0 / MD,
                               bias=col("eps")).then_inc(mb_rt, 1)
            act_trig(act)

        def act_moba(act):
            act_lora(act)
            att_act(act, moba_jobs)

        lora_in, lora_w, lora_loaded = sem("lora_in"), sem("lora_w"), sem("lora_loaded")
        rw_exp, rw_cum, rw_cml = sem("rw_exp"), sem("rw_cum"), sem("rw_cml")
        rw_sq, rw_ss, rw_rt = sem("rw_sq"), sem("rw_ss"), sem("rw_rt")
        bd_clear, bd_ready, u_ready, u_masked, u_copied = (sem("bd_clear"), sem("bd_ready"), sem("u_ready"),
                                                           sem("u_masked"), sem("u_copied"))
        t_init, t_x, t_xm, t_d, t_new = sem("t_init"), sem("t_x"), sem("t_xm"), sem("t_d"), sem("t_new")
        q_u, q_us, q_sa, q_sas, q_s, q_st, q_y, q_yc = (sem("q_u"), sem("q_us"), sem("q_sa"), sem("q_sas"),
                                                        sem("q_s"), sem("q_st"), sem("q_y"), sem("q_yc"))
        lora_in_t = rR["lora"].rearrange("p (k t) -> p k t", k=2)
        lora_wt = r0["AR"][:, 0:1536].rearrange("p (k f) -> p k f", k=3)
        four = lambda ap: ap.rearrange("p (m t) -> p m t", m=4)
        sixteen = lambda ap: ap.rearrange("p (u t) -> p u t", u=UN)

        def act_lora(act):
            act.wait_ge(mb_qn, 2)
            act.dma_start(lora_wt, a["lora"]).then_inc(lora_loaded, 16)

        def pool_rwkv(pool):
            pool.wait_ge(a_free, MH)
            pool.memset(rR["rmask"], 1.0).then_inc(gdone, 1)
            pool.wait_ge(gdone, 1)
            pool.memset(sixteen(rR["rmask"])[:, :, 0:1], 0.0).then_inc(bd_clear, 1)
            pool.memset(r0["BD"], 0.0).then_inc(bd_clear, 1)
            pool.wait_ge(lora_w, 2)
            pool.memset(r0["AR"], 0.0).then_inc(bd_clear, 1)

        def act_rwkv(act):
            act.wait_ge(a_free, MH)
            act.activation(lora_in_t[0:64, 0, :], zs[0:64, 12, :], ACT.Tanh)
            act.copy(lora_in_t[64:128, 0, :], zs[64:128, 12, :])
            act.activation(lora_in_t[:, 1, :], zs[:, 13, :], ACT.Sigmoid).then_inc(lora_in, 1)
            act.wait_ge(lora_w, 1)
            for m in range(4):
                act.activation(four(rR["lw"])[:, m, :], bank[3 + m][:, 0:S], ACT.Sigmoid, bias=col("rwkv_w0", m))
                ins = act.activation(four(rR["av"])[:, m, :], bank[3 + m][:, S:2 * S], ACT.Sigmoid,
                                     bias=col("rwkv_a0", m))
            ins.then_inc(lora_in, 1)
            act.wait_ge(lora_w, 2)
            act.copy(r0["g_rw"][:, 0:512], bank[7][:, :])
            act.copy(r0["g_rw"][:, 512:1024], bank[3][:, :]).then_inc(lora_in, 1)
            act.wait_ge(rw_ss, 1)
            for g in range(2):
                ins = act.activation(rR["rtk"][:, 512 * g:512 * g + 512], bank[4 + g][:, :], ACT.Sqrt)
            ins.then_inc(rw_rt, 1)
            act.wait_ge(rw_cum, 1)
            act.activation(Pc, rR["cum"], ACT.Exp)
            act.activation(rR["Pinv"], rR["cum"], ACT.Exp, scale=-1.0).then_inc(rw_exp, 1)
            act.activation(rR["Pprev"], rR["cml"], ACT.Exp).then_inc(rw_exp, 1)
            act.wait_ge(bd_ready, 1)
            for u in range(UN):
                act.wait_ge(u_ready, u + 1)
                act.copy(BKV[:, u, :, :], bank[5 + u % 2][:, 0:384].rearrange("p (k f) -> p k f", k=3)).then_inc(u_copied, 1)
            for c in range(NCH):
                act.wait_ge(q_u, c + 1)
                act.copy(usb[:, :, :], bank[3][:, :].rearrange("p (q f) -> p q f", q=PAIRS)).then_inc(q_us, 1)
                act.wait_ge(q_y, c + 1)
                yv = yb.rearrange("p (q c t) -> p q c t", q=PAIRS, c=NCH)
                bkv = bank[6 + c % 2][:, :].rearrange("p (q f) -> p q f", q=PAIRS)
                act.copy(yv[0:64, :, c, :], bkv[0:64, :, 0:64])
                act.copy(yv[64:128, :, c, :], bkv[64:128, :, 64:128]).then_inc(q_yc, 1)

        def dve_rwkv(dve, v):
            lw, cum, cml, av, kk, t1 = (rR[n] for n in ("lw", "cum", "cml", "av", "kk", "t1"))
            zk = zs[:, 4:8, :]
            for m in range(4):
                ins = dve.tensor_scalar(four(kk)[:, m, :], zs[:, 4 + m, :], col("rwkv_k_k", m), None, ALU.mult)
            v.then(ins)
            dve.tensor_tensor(rR["sqk"], kk, kk, ALU.mult).then_inc(rw_sq, 1)
            dve.wait_ge(lora_in, 2)
            dve.wait_ge(bd_clear, 1)
            v.then(dve.tensor_scalar(lw, lw, -float(np.exp(-0.5)), None, ALU.mult))
            v.then(dve.tensor_tensor_scan(cum, rR["rmask"], lw, 0.0, ALU.mult, ALU.add))
            dve.tensor_tensor(cml, cum, lw, ALU.subtract).then_inc(rw_cum, 1)
            v.then(dve.tensor_scalar(t1, av, 1.0, None, ALU.subtract))
            for m in range(4):
                ins = dve.tensor_scalar(four(t1)[:, m, :], four(t1)[:, m, :], col("rwkv_k_a", m), 1.0, ALU.mult, ALU.add)
            v.then(ins)
            v.then(dve.tensor_tensor(zk, zk, four(t1), ALU.mult))
            dve.wait_ge(rw_rt, 1)
            v.then(dve.tensor_scalar(rR["rtk"], rR["rtk"], 1e-12, None, ALU.max))
            v.then(dve.reciprocal(rR["rtk"], rR["rtk"]))
            v.then(dve.tensor_tensor(kk, kk, rR["rtk"], ALU.mult))
            dve.wait_ge(rw_exp, 1)
            v.then(dve.tensor_tensor(t1, av, rR["Pinv"], ALU.mult))
            dve.wait_ge(rw_exp, 2)
            dve.wait_ge(bd_clear, 3)
            for h, r in enumerate((lo, hi)):
                c = slice(64 * h, 64 * h + 64)
                dve.scalar_tensor_tensor(ARt[r, :, 0, c], sixteen(rR["Pprev"])[r], -1.0, sixteen(kk)[r], ALU.mult, ALU.mult)
                dve.tensor_tensor(ARt[r, :, 1, c], sixteen(Pc)[r], sixteen(r0["zs"][:, 0:1024])[r], ALU.mult)
                dve.tensor_tensor(BD[r, 0, :, c], sixteen(kk)[r], sixteen(t1)[r], ALU.mult)
                dve.tensor_tensor(BD[r, 1, :, c], sixteen(r0["zs"][:, 1024:2048])[r], sixteen(rR["Pinv"])[r], ALU.mult)
                ins = dve.tensor_copy(BD[r, 2, :, c], sixteen(r0["zs"][:, 2048:3072])[r])
            ins.then_inc(bd_ready, 1)
            dve.wait_ge(bd_ready, 1)
            level = lambda k: over(c1["mL"][:, 128 * k:128 * k + 128], 4)
            quad = lambda bk: bk[:, :].rearrange("p (q f) -> p q f", q=4)
            for u in range(UN):
                dve.wait_ge(u_ready, u + 1)
                bk = bank[3 + u % 2]
                dve.tensor_tensor(LT[:, u, :], bk[:, 0:128], c1["g_mask"][:, 0:128], ALU.mult)
                ins = dve.tensor_tensor(G3[:, u, :, :], bk[:, 128:512].rearrange("p (k f) -> p k f", k=3),
                                        c1["g_mask"][:, 128:512].rearrange("p (k f) -> p k f", k=3), ALU.mult)
                ins.then_inc(u_masked, 1)
            dve.wait_ge(u_masked, UN)
            for q in range(4):
                s = slice(4 * q, 4 * q + 4)
                dve.wait_ge(t_x, q + 1)
                v.then(dve.tensor_tensor(Tm[:, s, :], quad(bank[(3, 4, 7, 5)[q]]), level(0), ALU.mult))
                v.did(dve.tensor_tensor(TTm[:, s, :], LT[:, s, :], over(c1["mT1"], 4), ALU.mult))
                dve.tensor_tensor(Tm[:, s, :], Tm[:, s, :], over(ident, 4), ALU.add)
                v.settle()
                dve.tensor_tensor(TTm[:, s, :], TTm[:, s, :], over(ident, 4), ALU.add).then_inc(t_init, 1)
            dve.wait_ge(t_init, 4)

            def masked(n):
                dve.wait_ge(t_x, 4 + n + 1)
                s = slice(4 * (n % 4), 4 * (n % 4) + 4)
                dve.tensor_tensor(Xm[:, s, :], quad(bank[3 + n % 2]), level(1 + n // 4), ALU.mult).then_inc(t_xm, 1)

            def update(n):
                dve.wait_ge(t_d, n + 1)
                if n >= 4:
                    dve.wait_ge(t_new, n - 3)
                s = slice(4 * (n % 4), 4 * (n % 4) + 4)
                if n // 4 < 4:
                    dve.tensor_tensor(Tm[:, s, :], Tm[:, s, :], quad(bank[5]), ALU.add)
                dve.tensor_tensor(TTm[:, s, :], TTm[:, s, :], quad(bank[6 + n % 2]), ALU.add).then_inc(t_new, 1)

            masked(0)
            masked(1)
            for n in range(20):
                update(n)
                if n + 2 < 20:
                    masked(n + 2)
            dve.wait_ge(t_new, 20)
            last = sixteen(Pc)[:, :, CH - 1:CH]
            for c in range(NCH):
                old, new = st[:, c % 2], st[:, (c + 1) % 2]
                dve.wait_ge(q_sa, c + 1)
                dve.tensor_copy(sasb[:, :, :], bank[4][:, :].rearrange("p (q f) -> p q f", q=PAIRS)).then_inc(q_sas, 1)
                if c + 1 == NCH:
                    break
                if c:
                    dve.wait_ge(q_y, c)
                    for q in range(PAIRS):
                        ins = dve.tensor_scalar(new[:, q, :], old[:, q, :], last[:, NCH * q + c, :], None, ALU.mult)
                    v.then(ins)
                dve.wait_ge(q_s, c + 1)
                for q in range(PAIRS):
                    inc = bank[5][:, q * 128:(q + 1) * 128]
                    if c:
                        ins = dve.scalar_tensor_tensor(new[:, q, :], inc, last[:, NCH * q + c, :], new[:, q, :],
                                                       ALU.mult, ALU.add)
                    else:
                        ins = dve.tensor_scalar(new[:, q, :], inc, last[:, NCH * q + c, :], None, ALU.mult)
                ins.then_inc(q_st, 1)
                dve.wait_ge(q_st, c + 1)
            dve_rwkv_out(dve, v)

        gn_in, gn_ss, gn_rt, bon_in, bon_ss, rw_out = (sem("gn_in"), sem("gn_ss"), sem("gn_rt"), sem("bon_in"),
                                                       sem("bon_ss"), sem("rw_out"))

        def dve_rwkv_out(dve, v):
            dve.wait_ge(q_y, NCH)
            for m in range(4):
                ins = dve.scalar_tensor_tensor(four(rP["rk"])[:, m, :], zs[:, m, :], col("rwkv_r_k", m),
                                               zs[:, 4 + m, :], ALU.mult, ALU.mult)
            ins.then_inc(bon_in, 1)
            dve.wait_ge(gn_ss, 1)
            for g in range(2):
                ins = dve.scalar_tensor_tensor(rP["yc"][:, 512 * g:512 * g + 512], bank[3 + g][:, :], -1.0 / RN,
                                               yb[:, 512 * g:512 * g + 512], ALU.mult, ALU.add)
            v.then(ins)
            dve.tensor_tensor(rP["ysq"], rP["yc"], rP["yc"], ALU.mult).then_inc(gn_in, 1)
            dve.wait_ge(bon_ss, 1)
            for g in range(2):
                ins = dve.tensor_tensor(rP["bon"][:, 512 * g:512 * g + 512], bank[5 + g][:, :],
                                        r0["zs"][:, 2048 + 512 * g:2048 + 512 * g + 512], ALU.mult)
            v.then(ins)
            dve.wait_ge(gn_rt, 1)
            v.then(dve.reciprocal(rP["rt"], rP["rt"]))
            v.then(dve.tensor_tensor(rP["yc"], rP["yc"], rP["rt"], ALU.mult))
            for m in range(4):
                ins = dve.tensor_scalar(four(rP["yc"])[:, m, :], four(rP["yc"])[:, m, :], col("rwkv_ln_g", m),
                                        col("rwkv_ln_b", m), ALU.mult, ALU.add)
            v.then(ins)
            v.then(dve.tensor_tensor(rP["yc"], rP["yc"], rP["bon"], ALU.add))
            dve.tensor_tensor(yb, rP["yc"], r0["g_rw"], ALU.mult).then_inc(rw_out, 1)

        def pe_rwkv(pe):
            pe.wait_ge(lora_loaded, 16)
            pe.wait_ge(lora_in, 1)
            for m in range(4):
                for k in range(2):
                    mm = pe.matmul(bank[3 + m][:, k * S:(k + 1) * S], lora_wt[:, k, m * 128:(m + 1) * 128],
                                   lora_in_t[:, 0, :], start=True, stop=True)
            mm.then_inc(lora_w, 1)
            for m in range(4):
                if m == 2:
                    pe.wait_ge(lora_in, 2)
                mm = pe.matmul((bank[7], bank[3])[m // 2][:, (m % 2) * S:(m % 2 + 1) * S],
                               lora_wt[:, 2, m * 128:(m + 1) * 128], lora_in_t[:, 1, :], start=True, stop=True)
            mm.then_inc(lora_w, 1)
            mm = None
            pe.wait_ge(rw_sq, 1)
            for g in range(2):
                mm = pe.matmul(bank[4 + g][:, :], blk64, rR["sqk"][:, 512 * g:512 * g + 512], start=True, stop=True)
            mm.then_inc(rw_ss, 1)
            pe.wait_ge(bd_ready, 1)
            for u in range(UN):
                if u >= 2:
                    pe.wait_ge(u_masked, u - 1)
                    pe.wait_ge(u_copied, u - 1)
                ar = ARt[:, u, :, :].rearrange("p k f -> p (k f)")
                bk, bt = bank[3 + u % 2], bank[5 + u % 2]
                pe.matmul(bk[:, 0:256], BD[:, 0, u, :], ar, start=True, stop=True)
                pe.matmul(bk[:, 256:512], BD[:, 1, u, :], ar, start=True, stop=True)
                for k in range(3):
                    mm = pe.transpose(bt[:, k * 128:(k + 1) * 128], BD[:, k, u, :], ident)
                mm.then_inc(u_ready, 1)
            pe.wait_ge(u_masked, UN)
            for q in range(4):
                bk = bank[(3, 4, 7, 5)[q]]
                if q == 3:
                    pe.wait_ge(u_copied, UN)
                for i in range(4):
                    u = 4 * q + i
                    mm = pe.matmul(bk[:, i * 128:(i + 1) * 128], ARt[:, u, 0, :], BD[:, 0, u, :], start=True, stop=True)
            mm.then_inc(t_x, 4)

            def quads(q):
                return range(4 * (q % 4), 4 * (q % 4) + 4)

            def product(n):
                for i, u in enumerate(quads(n)):
                    mm = pe.matmul(bank[3 + n % 2][:, i * 128:(i + 1) * 128], LT[:, u, :], Tm[:, u, :],
                                   start=True, stop=True)
                mm.then_inc(t_x, 1)

            def increments(n):
                pe.wait_ge(t_xm, n + 1)
                if n >= 1:
                    pe.wait_ge(t_new, n)
                if n // 4 < 4:
                    for i, u in enumerate(quads(n)):
                        pe.matmul(bank[5][:, i * 128:(i + 1) * 128], TTm[:, u, :], Xm[:, u, :], start=True, stop=True)
                for i, u in enumerate(quads(n)):
                    mm = pe.matmul(bank[6 + n % 2][:, i * 128:(i + 1) * 128], Xm[:, u, :], TTm[:, u, :],
                                   start=True, stop=True)
                mm.then_inc(t_d, 1)

            pe.wait_ge(t_init, 4)
            product(0)
            product(1)
            for n in range(20):
                increments(n)
                if n + 2 < 20:
                    if n + 2 >= 4:
                        pe.wait_ge(t_new, n - 1)
                    product(n + 2)
            for c in range(NCH):
                old = st[:, c % 2]
                us = [NCH * q + c for q in range(PAIRS)]
                if c == 0:
                    pe.wait_ge(t_new, 20)
                else:
                    pe.wait_ge(q_st, c)
                for q, u in enumerate(us):
                    out = bank[3][:, q * 128:(q + 1) * 128]
                    if c:
                        pe.matmul(out, ARt[:, u, 0, :], old[:, q, :], start=True, stop=False)
                    mm = pe.matmul(out, G3[:, u, 1, :], BKV[:, u, 2, :], start=(c == 0), stop=True)
                mm.then_inc(q_u, 1)
                pe.wait_ge(q_us, c + 1)
                for q, u in enumerate(us):
                    mm = pe.matmul(bank[4][:, q * 128:(q + 1) * 128], TTm[:, u, :], usb[:, q, :], start=True, stop=True)
                mm.then_inc(q_sa, 1)
                pe.wait_ge(q_sas, c + 1)
                if c + 1 < NCH:
                    for q, u in enumerate(us):
                        out = bank[5][:, q * 128:(q + 1) * 128]
                        pe.matmul(out, BKV[:, u, 0, :], sasb[:, q, :], start=True, stop=False)
                        mm = pe.matmul(out, BKV[:, u, 1, :], BKV[:, u, 2, :], start=False, stop=True)
                    mm.then_inc(q_s, 1)
                if c >= 2:
                    pe.wait_ge(q_yc, c - 1)
                for q, u in enumerate(us):
                    out = bank[6 + c % 2][:, q * 128:(q + 1) * 128]
                    if c:
                        pe.matmul(out, old[:, q, :], ARt[:, u, 1, :], start=True, stop=False)
                    pe.matmul(out, sasb[:, q, :], G3[:, u, 0, :], start=(c == 0), stop=False)
                    mm = pe.matmul(out, BKV[:, u, 2, :], G3[:, u, 2, :], start=False, stop=True)
                mm.then_inc(q_y, 1)
            pe.wait_ge(q_yc, NCH)
            for g in range(2):
                mm = pe.matmul(bank[3 + g][:, :], blk64, yb[:, 512 * g:512 * g + 512], start=True, stop=True)
            mm.then_inc(gn_ss, 1)
            pe.wait_ge(bon_in, 1)
            for g in range(2):
                mm = pe.matmul(bank[5 + g][:, :], blk64, rP["rk"][:, 512 * g:512 * g + 512], start=True, stop=True)
            mm.then_inc(bon_ss, 1)
            pe.wait_ge(gn_in, 1)
            for g in range(2):
                mm = pe.matmul(bank[3 + g][:, :], blk64, rP["ysq"][:, 512 * g:512 * g + 512], start=True, stop=True)
            mm.then_inc(gn_ss, 1)

        def act_rwkv_out(act):
            act.wait_ge(gn_ss, 2)
            for g in range(2):
                ins = act.activation(rP["rt"][:, 512 * g:512 * g + 512], bank[3 + g][:, :], ACT.Sqrt, scale=1.0 / RN,
                                     bias=col("gn_eps"))
            ins.then_inc(gn_rt, 1)

        mix_ready = sem("mix_ready")

        def pe_proj(pe):
            pe.wait_ge(rw_out, 1)
            y4 = four(yb)

            def body(slot, bk):
                for half, x in enumerate((om, y4)):
                    for k in range(4):
                        mm = pe.matmul(bk[:, half * S:(half + 1) * S], blocks(slot, 4 * half + k), x[:, k, :],
                                       start=(k == 0), stop=(k == 3))
                return mm
            ring_tiles(pe, "proj", body)

        def dve_proj(dve, v):
            g2v = gates.rearrange("p (k m) t -> p k m t", k=2)
            for m in range(KT):
                tile_wait(dve, "proj", m)
                v.then(dve.tensor_tensor(mixt[:, m % 2], ring_bank("proj", m)[:, :].rearrange("p (k t) -> p k t", k=2),
                                         g2v[:, :, m, :], ALU.mult))
                dve.tensor_tensor(mix1[:, m, :], mixt[:, m % 2, 0, :], mixt[:, m % 2, 1, :], ALU.add).then_inc(ring_free, 1)

        def pe_w_out(pe):
            pe.wait_ge(ring_free, RING0["w_out"])
            ring_tiles(pe, "w_out", lambda slot, bk: matmul8(pe, bk[:, 0:S], slot, mix1))

        def dve_residual(dve, name, vec):
            for m in range(KT):
                tile_wait(dve, name, m)
                ins = dve.scalar_tensor_tensor(hT[:, m, :], ring_bank(name, m)[:, 0:S], modc(vec, m), hT[:, m, :],
                                               ALU.mult, ALU.add)
                ins.then_inc(ring_free, 1)
            dve.wait_ge(ring_free, RING0[name] + COUNT[name])

        sc_ready, sc_copied, pick_ready, t3_turned, t3_ready = (sem("sc_ready"), sem("sc_copied"), sem("pick_ready"),
                                                                sem("t3_turned"), sem("t3_ready"))
        gate_arg, gate_exp, iota_ready = sem("gate_arg"), sem("gate_exp"), sem("iota_ready")
        hot_pool = sem("hot_pool")
        hot, g_ready, g_copied = sem("hot"), sem("g_ready"), sem("g_copied")
        gelu_ready, w_hi, w_ready = sem("gelu_ready"), sem("w_hi"), sem("w_ready")

        def act_subk(act):
            act.wait_ge(xn_ready, 2 * KT)
            act.dma_start(rK["subk"], a["subk"]).then_inc(subk_loaded, 16)

        def pe_route(pe):
            pe.wait_ge(x_lo, 8)
            ring_tiles_split(pe, "wq")
            pe.wait_ge(ring_free, RING0["wq"] + COUNT["wq"])
            pe.wait_ge(subk_loaded, 16)
            for n in range(NR // 4):
                if n >= 4:
                    pe.wait_ge(sc_copied, n - 3)
                for i in range(4):
                    b, r = divmod(4 * n + i, 16)
                    mm = pe.matmul(bank[3 + n % 4][:, i * 128:(i + 1) * 128], qp[:, r, b * 128:(b + 1) * 128],
                                   subk[:, r, :], start=True, stop=True)
                mm.then_inc(sc_ready, 1)

        def act_route(act):
            act_subk(act)
            for t in range(2):
                act_hi_of(act, "wq", t)
            for t in range(COUNT["wq"]):
                act_hi_of(act, "wq", t + 2)
                tile_wait(act, "wq", t)
                act.copy(qp[:, t, :], ring_bank("wq", t)[:, 0:S]).then_inc(ring_free, 1)
            for n in range(NR // 4):
                act.wait_ge(sc_ready, n + 1)
                act.copy(sc[:, 4 * n:4 * n + 4, :], bank[3 + n % 4][:, :].rearrange("p (r n) -> p r n", r=4))\
                   .then_inc(sc_copied, 1)
            act.wait_ge(gate_arg, 1)
            act.activation(rK["gate"], rK["gate"], ACT.Exp).then_inc(gate_exp, 1)

        def pool_route(pool):
            pool.wait_ge(rw_out, 1)
            pool.iota(rG["iotai"].bitcast(I32), [[1, 128]], base=0, channel_multiplier=0).then_inc(gdone, 1)
            pool.wait_ge(gdone, 2)
            pool.tensor_copy(rG["iota"], rG["iotai"].bitcast(I32)).then_inc(iota_ready, 1)

        def top16(dve, v, rows):
            for values, _, row, _ in rows:
                v.did(dve.max(values[:, 0:8], row))
            v.settle()
            for values, index, row, scratch in rows:
                v.did(dve.max_index(index[:, 0:8], values[:, 0:8], row))
                v.did(dve.match_replace(scratch, values[:, 0:8], row, -3e38))
            v.settle()
            for values, _, _, scratch in rows:
                v.did(dve.max(values[:, 8:16], scratch))
            v.settle()
            for values, index, _, scratch in rows:
                v.did(dve.max_index(index[:, 8:16], values[:, 8:16], scratch))

        def dve_route(dve, v):
            for n in range(NR // 4):
                dve.wait_ge(sc_copied, n + 1)
                top16(dve, v, [(tv[:, r, :], ti[:, r, :], sc[:, r, :], rK["scr"][:, (r % 4) * 128:(r % 4) * 128 + 128])
                               for r in range(4 * n, 4 * n + 4)])
            v.settle()
            v.did(dve.tensor_copy(rK["tif"], rK["ti"].bitcast(U32)))
            t4 = rK["tv"].rearrange("p (r h k) -> p r h k", r=NQ, h=2)
            c4 = rK["cand"].rearrange("p (r a b) -> p r a b", r=NQ, a=PK)
            first = t4[:, :, 0, :].unsqueeze(3).to_broadcast([P, NQ, PK, PK])
            second = t4[:, :, 1, :].unsqueeze(2).to_broadcast([P, NQ, PK, PK])
            v.then(dve.tensor_tensor(c4, first, second, ALU.add))
            for n in range(NQ // 4):
                top16(dve, v, [(best[:, r, :], bi[:, r, :], cand[:, r, :], rK["scr2"][:, (r % 4) * 256:(r % 4) * 256 + 256])
                               for r in range(4 * n, 4 * n + 4)])
            v.settle()
            dve.tensor_tensor(gate[:, :, :], best[:, :, :], best[:, :, 0:1].to_broadcast([P, NQ, PK]), ALU.subtract)\
               .then_inc(gate_arg, 1)
            v.did(dve.tensor_scalar(ba[:, 0, :], rK["bi"].bitcast(U32), 4, None, ALU.logical_shift_right))
            v.then(dve.tensor_scalar(ba[:, 1, :], rK["bi"].bitcast(U32), 15, None, ALU.bitwise_and))
            v.then(dve.tensor_copy(rK["baf"], rK["ba"].bitcast(U32)))
            dve.wait_ge(iota_ready, 1)
            f4 = rK["tif"].rearrange("p (r h k) -> p r h k", r=NQ, h=2)
            big = rK["big"].rearrange("p (r k x) -> p r k x", r=NQ, k=PK)
            iota16 = rG["iota"][:, 0:PK].unsqueeze(1).unsqueeze(1).to_broadcast([P, NQ, PK, PK])
            for h in range(2):
                rank = baf[:, h, :].rearrange("p (r k) -> p r k", r=NQ).unsqueeze(3).to_broadcast([P, NQ, PK, PK])
                v.then(dve.tensor_tensor(big, rank, iota16, ALU.is_equal))
                table = f4[:, :, h, :].unsqueeze(2).to_broadcast([P, NQ, PK, PK])
                v.then(dve.tensor_tensor(big, big, table, ALU.mult))
                v.then(dve.tensor_reduce(pick[:, h, :].rearrange("p (r k) -> p r k", r=NQ), big, AX, ALU.add))
            dve.wait_ge(gate_exp, 1)
            v.then(dve.tensor_reduce(rK["gsum"][:, 0:NQ], gate[:, :, :], AX, ALU.add))
            v.then(dve.reciprocal(rK["gsum"][:, NQ:2 * NQ], rK["gsum"][:, 0:NQ]))
            dve.tensor_tensor(gate[:, :, :], gate[:, :, :], wide(rK["gsum"][:, NQ:2 * NQ], PK), ALU.mult)\
               .then_inc(pick_ready, 1)
            dve.wait_ge(t3_turned, 1)
            v.did(dve.tensor_copy(T3[:, 0:2, :], bank[3][:, :].rearrange("p (k t) -> p k t", k=2)))
            dve.tensor_copy(T3[:, 2, :], bank[4][:, 0:S]).then_inc(t3_ready, 1)
            dve.wait_ge(t3_ready, 1)

        def pe_turn_routes(pe):
            pe.wait_ge(pick_ready, 1)
            for k, x in enumerate((pick[:, 0, :], pick[:, 1, :], rK["gate"])):
                for b in range(TT):
                    mm = pe.transpose(bank[3 + k // 2][:, (k % 2) * S + b * 128:(k % 2) * S + (b + 1) * 128],
                                      x[:, b * 128:(b + 1) * 128], ident)
            mm.then_inc(t3_turned, 1)

        GROUPS = S // 8

        def dve_hot(dve):
            def group(b, t0, used):
                if used is not None:
                    dve.wait_ge(g_ready, used)
                dve.tensor_tensor(A8[:, b], over(rG["iota"], 8), wide(T3[:, 0, bass.ds(t0, 8)], 128), ALU.is_equal)
                for t in range(8 - POOL_ROWS):
                    ins = dve.tensor_scalar(B8[:, b, t, :], rG["iota"], T3[:, 1, bass.ds(t0 + t, 1)],
                                            T3[:, 2, bass.ds(t0 + t, 1)], ALU.is_equal, ALU.mult)
                ins.then_inc(hot, 1)
            group(0, 0, None)
            group(1, 8, None)
            with dve.Fori(1, GROUPS // 2) as i:
                for b in range(2):
                    group(b, 16 * i + 8 * b, 2 * i + (b - 1))

        POOL_ROWS = 3

        def pool_hot(pool):
            pool.wait_ge(t3_ready, 1)
            for n in range(GROUPS):
                if n >= 2:
                    pool.wait_ge(g_ready, n - 1)
                for t in range(8 - POOL_ROWS, 8):
                    ins = pool.tensor_scalar(B8[:, n % 2, t, :], rG["iota"], T3[:, 1, 8 * n + t:8 * n + t + 1],
                                             T3[:, 2, 8 * n + t:8 * n + t + 1], ALU.is_equal, ALU.mult)
                ins.then_inc(hot_pool, 1)

        def pe_gates(pe):
            def group(b, n, free):
                pe.wait_ge(hot, n)
                pe.wait_ge(hot_pool, n)
                if free is not None:
                    pe.wait_ge(g_copied, free)
                for t in range(8):
                    mm = pe.matmul(bank[3 + 2 * b + t // 4][:, (t % 4) * 128:(t % 4) * 128 + 128], A8[:, b, t, :],
                                   B8[:, b, t, :], start=True, stop=True)
                mm.then_inc(g_ready, 1)
            group(0, 1, None)
            group(1, 2, None)
            with pe.Fori(1, GROUPS // 2) as i:
                for b in range(2):
                    group(b, 2 * i + (b + 1), 2 * i + (b - 1))

        def act_gates(act):
            with act.Fori(0, GROUPS // 2) as i:
                for b in range(2):
                    act.wait_ge(g_ready, 2 * i + (b + 1))
                    for h in range(2):
                        ins = act.copy(G[:, bass.ds(16 * i + 8 * b + 4 * h, 4), :],
                                       bank[3 + 2 * b + h][:, :].rearrange("p (t j) -> p t j", t=4))
                    ins.then_inc(g_copied, 1)

        P0 = FIRST["peer"]
        u_tile = lambda j: P0 + (0 if j == 0 else 2 * j - 1)
        v_tile = lambda j: P0 + (2 * j + 2 if j < NK - 1 else 2 * NK - 1)
        accs = [bank[4 + m // 2][:, (m % 2) * S:(m % 2 + 1) * S] for m in range(KT)]

        def down8(pe, n, wb, first, last):
            for m in range(KT):
                mm = three(pe, accs[m], n, m, Whi[:, wb, :], Wlo[:, wb, :], first and m % 2 == 0, last,
                           skip_group_check=True)
            return mm

        def pe_peer(pe):
            def up(j, n, split, free):
                pe.wait_ge(lo_ready, split)
                if free is not None:
                    pe.wait_ge(gelu_ready, free)
                split8(pe, bank[j % 3][:, 0:S], n).then_inc(tile_done, 1)

            def down(j, n, split, weighed, first=False, last=False):
                pe.wait_ge(lo_ready, split)
                pe.wait_ge(w_ready, weighed)
                down8(pe, n, j % 3, first, last).then_inc(tile_done, 1)

            def turn(j, i=0):
                n, m = u_tile(j), v_tile(j - 1)
                up(j, n, 6 * i + nth_split[n], 3 * i + (j - 2) if j >= 3 else None)
                down(j - 1, m, 6 * i + nth_split[m], 3 * i + j, first=(j == 1))

            pe.wait_ge(g_copied, GROUPS)
            up(0, u_tile(0), nth_split[u_tile(0)], None)
            for j in range(1, 4):
                turn(j)
            with pe.Fori(0, ROUNDS) as i:
                for j in range(4, 7):
                    turn(j, i)
            for j in range(4 + 3 * ROUNDS, NK):
                turn(j)
            n = v_tile(NK - 1)
            down(NK - 1, n, nth_split[n], NK, last=True)

        ROUNDS = (NK - 5) // 3

        def act_peer(act):
            def hi(n, i=0):
                if n < P0 + COUNT["peer"]:
                    act_hi(act, n, 16 * i + count_at(n), 6 * i + (n - HSLOTS + 1) if n >= P0 + HSLOTS else None)

            def turn(j, i=0):
                n = u_tile(j)
                if j > 0:
                    hi(n + 2, i)
                act.wait_ge(tile_done, 6 * i + (n + 1))
                if j >= 3:
                    act.wait_ge(w_ready, 3 * i + (j - 2))
                act.activation(ge[:, j % 3, :], bank[j % 3][:, 0:S], ACT.Gelu).then_inc(gelu_ready, 1)
                if j > 0:
                    hi(n + 3, i)

            act.wait_ge(hot, GROUPS)
            act.dma_start(rG["crow2"], a["crow"][1:2, :].to_broadcast([P, D])).then_inc(crow_loaded, 16)
            for n in range(P0, P0 + 3):
                hi(n)
            act.wait_ge(crow_loaded, 32)
            act.activation(rG["crow2"], rG["crow2"], ACT.Silu).then_inc(half_free, 1)
            for j in range(4):
                turn(j)
            with act.Fori(0, ROUNDS) as i:
                for j in range(4, 7):
                    turn(j, i)
            for j in range(4 + 3 * ROUNDS, NK):
                turn(j)

        def dve_peer(dve, v):
            def lo(n, i=0):
                if n < P0 + COUNT["peer"]:
                    tile_lo(dve, n, 6 * i + nth_split[n])

            def turn(j, i=0):
                n, b = u_tile(j), j % 3
                if j > 0:
                    lo(n + 2, i)
                dve.wait_ge(gelu_ready, 3 * i + (j + 1))
                if j >= 3:
                    dve.wait_ge(tile_done, 6 * i + (v_tile(j - 3) + 1))
                g = G[:, :, 3 * i + j] if j >= 4 else G[:, :, j]
                dve.tensor_tensor(Whi[:, b, :], ge[:, b, :], g, ALU.mult).then_inc(w_hi, 1)
                dve.tensor_tensor(ge[:, b, :], ge[:, b, :], g, ALU.mult).then_inc(w_hi, 1)
                dve.wait_ge(w_hi, 6 * i + (2 * j + 2))
                dve.tensor_tensor(Wlo[:, b, :], ge[:, b, :], Whi[:, b, :].bitcast(F32), ALU.subtract).then_inc(w_ready, 1)
                if j > 0:
                    lo(n + 3, i)

            def half(u, i, second):
                dve.wait_ge(half_landed, 48 * i + 16 * (u + 1))
                c = rG["crow2"][:, AHALF:] if second else rG["crow2"][:, :AHALF]
                dve.tensor_tensor_reduce(rG["half"], rG["half"], c, 1.0, 0.0, ALU.mult, ALU.add,
                                         part[:, u:u + 1]).then_inc(half_free, 1)
                dve.wait_ge(half_free, 3 * i + (u + 2))
                dve.tensor_copy(mod2[:, bass.ds(3 * i + u, 1)], part[:, u:u + 1]).then_inc(half_kept, 1)

            dve.wait_ge(g_copied, GROUPS)
            for n in range(P0, P0 + 3):
                lo(n)
            for j in range(4):
                turn(j)
            halves = 2 * 6 * KT
            for start, end in ((0, halves // 6), (halves // 6, halves // 3), (halves // 3, ROUNDS)):
                with dve.Fori(start, end) as i:
                    for j in range(4, 7):
                        turn(j, i)
                        if end < ROUNDS:
                            half(j - 4, i, start > 0)
            for j in range(4 + 3 * ROUNDS, NK):
                turn(j)
            dve.wait_ge(half_kept, halves)
            v.then(dve.tensor_tensor(mod[:, 6 * KT:], mod2[:, 0:6 * KT], mod2[:, 6 * KT:], ALU.add))
            dve_add_bias(dve, v, 6 * KT, 12 * KT)
            for n in (2, 3):
                dve_gsc(dve, v, n)
            dve.wait_ge(tile_done, FIRST["peer"] + COUNT["peer"])
            dve_add_accs(dve, 5)

        acc_read = sem("acc_read")

        def dve_add_accs(dve, vec):
            for m in range(KT):
                ins = dve.scalar_tensor_tensor(hT[:, m, :], accs[m], modc(vec, m), hT[:, m, :], ALU.mult, ALU.add)
            ins.then_inc(acc_read, 1)
            dve.wait_ge(acc_read, 1 if vec == 5 else 2)

        def act_const2(act):
            act.wait_ge(acc_read, 1)
            act.dma_start(r2["const2"], a["const2"]).then_inc(c2_loaded, 16)

        def pe_w_in2(pe):
            pe.wait_ge(xn_ready, 3 * KT)
            first, ring0 = FIRST["w_in2"], RING0["w_in2"]
            for k in range(5):
                n, r = first + k, ring0 + k
                pe.wait_ge(landed[n % SLOTS], count_at(n))
                pe.wait_ge(ring_free, r - BANKS + 1)
                matmul8_tokens(pe, bank[r % BANKS], n % SLOTS).then_inc(tile_done, 1)
            pe.wait_ge(x_lo, 12)
            ring_tiles_split(pe, "w_in2", 5, 23)
            ring_tiles_split(pe, "w_in2", 23, SUMS_AT)
            pe_nsa_sums(pe)
            ring_tiles_split(pe, "w_in2", SUMS_AT, ROT_AT)
            pe_nsa_turn(pe)
            ring_tiles_split(pe, "w_in2", ROT_AT, 43)

        SUMS_AT, ROT_AT = 30, 40

        def act_w_in2(act):
            for k in range(43):
                if k + 2 >= SKIP["w_in2"]:
                    act_hi_of(act, "w_in2", k + 2)
                tile_wait(act, "w_in2", k)
                bk = ring_bank("w_in2", k)
                two = bk[:, 0:S].rearrange("p (b f) -> p b f", b=TT)
                if k < 4:
                    f = (k % 2) * 128
                    ins = act.copy((vs2, vw2)[k // 2][:, :, f:f + 128], two)
                elif k == 4:
                    ins = act.activation(gt2[:, :, :], two[:, :, 0:24], ACT.Sigmoid)
                elif k < 27:
                    ins = act.copy(F2[:, k - 5, :], bk[:, 0:S])
                else:
                    ins = act.activation(bg[:, k - 27, :], bk[:, 0:S], ACT.Sigmoid)
                ins.then_inc(ring_free, 1)
                if k == SUMS_AT - 1:
                    act_nsa_roots(act)

        n_sq, n_ss, n_rt, n_qn, n_rot, n_q = (sem("n_sq"), sem("n_ss"), sem("n_rt"), sem("n_qn"), sem("n_rot"),
                                              sem("n_q"))
        cm_x, cm_hs, cm_t, cm_ts, cm_o0, cm_kn, cm_kt, cm_kc, cm_rt = (sem(f"cm_{x}") for x in
                                    ("x", "hs", "t", "ts", "o0", "kn", "kt", "kc", "rt"))

        c_sq, c_ss, c_rt, c_n = sem("c_sq"), sem("c_ss"), sem("c_rt"), sem("c_n")
        l_sq, l_ss, l_rt, l_q, l_rot, l_k = (sem(f"l_{x}") for x in ("sq", "ss", "rt", "q", "rot", "k"))
        crs = r2["rot"][:, 0:512].rearrange("p (k t) -> p k t", k=2)
        kro = r2["rot"][:, 512:512 + 2048].rearrange("p (h t) -> p h t", h=MLH)
        krr = r2["rot"][:, 2560:2816]
        krt = r2["rot"][:, 2816:3072]
        csq = kb[:, 0:5, :]

        def dve_nsa(dve, v):
            f = r2["F2"]
            dve.wait_ge(ring_free, RING0["w_in2"] + 27)
            dve.tensor_tensor(sq14[:, 0:12, :], F2[:, 0:12, :], F2[:, 0:12, :], ALU.mult).then_inc(n_sq, 1)
            dve.tensor_tensor(csq, F2[:, 16:21, :], F2[:, 16:21, :], ALU.mult).then_inc(c_sq, 1)
            dve.wait_ge(n_rt, 6)
            v.then(dve.reciprocal(r2["rs"], r2["rs"]))
            for at, n, g in ((0, 8, "nsa_q_norm_2"), (8, 2, "nsa_ks_norm_2"), (10, 2, "nsa_kw_norm_2")):
                ins = dve.scalar_tensor_tensor(f[:, at * S:(at + n) * S], f[:, at * S:(at + n) * S], col(g),
                                               r2["rs"][:, at * S:(at + n) * S], ALU.mult, ALU.mult)
            ins.then_inc(n_qn, 1)
            dve.wait_ge(n_qn, 1)
            dve.wait_ge(c_rt, 2)
            v.then(dve.reciprocal(crs, crs))
            for k in range(5):
                g = col("mla_cq_norm_2", k) if k < 3 else col("mla_ckv_norm_2", k - 3)
                ins = dve.scalar_tensor_tensor(F2[:, 16 + k, :], F2[:, 16 + k, :], g, crs[:, k // 3, :], ALU.mult, ALU.mult)
            ins.then_inc(c_n, 1)
            dve.wait_ge(c_n, 1)
            for g in range(7):
                dve.wait_ge(n_rot, g + 1)
                ins = dve.tensor_tensor(ro14[:, 2 * g:2 * g + 2, :], bank[3 + g % 5][:, :].rearrange("p (m t) -> p m t", m=2),
                                        over(c2["nsa_sin"], 2), ALU.mult)
                ins.then_inc(n_q, 1)
            dve.wait_ge(n_q, 7)
            v.then(dve.tensor_tensor(F2[:, 0:14, :], F2[:, 0:14, :], over(c2["nsa_cos"], 14), ALU.mult))
            v.then(dve.tensor_tensor(F2[:, 0:14, :], F2[:, 0:14, :], ro14[:, :, :], ALU.add))
            for i, pe_name in enumerate(("cmp_k_pe", "cmp_v_pe")):
                for g in range(NG):
                    src = F2[:, 12 + 2 * i + g, :]
                    for half in range(CB // CS):
                        part = src[:, half * CS:half * CS + NCMP * CS].rearrange("p (n l) -> p l n", l=CS)
                        ins = dve.tensor_tensor(XP[:, i, half * CS:(half + 1) * CS, g * NCMP:(g + 1) * NCMP], part,
                                                wide(col(pe_name, half * CS, CS), NCMP), ALU.add)
            ins.then_inc(cm_x, 1)

        def dve_compressed(dve, v):
            kt = r2["cmt"][0:NCMP, 0:256].rearrange("p (g f) -> p g f", g=NG)
            st8 = r2["kst"][0:NCMP, :]
            dve.wait_ge(tile_done, FIRST["cmp_w2"] + 1)
            v.then(dve.tensor_copy(r2["cmt"][0:NCMP, 0:512], bank[6][0:NCMP, :]))
            for g in range(NG):
                ins = dve.tensor_tensor_reduce(r2["hid"][0:NCMP, g * 128:(g + 1) * 128], kt[:, g, :], kt[:, g, :],
                                               1.0, 0.0, ALU.mult, ALU.add, st8[:, g:g + 1])
            ins.then_inc(cm_kn, 1)
            dve.wait_ge(cm_rt, 1)
            v.then(dve.reciprocal(st8[:, 4:6], st8[:, 2:4]))
            for g in range(NG):
                ins = dve.tensor_scalar(kt[:, g, :], kt[:, g, :], st8[:, 4 + g:5 + g], None, ALU.mult)
            ins.then_inc(cm_kn, 1)
            dve.wait_ge(cm_kt, 1)
            dve.tensor_scalar(r2["kcT"][:, 0:30], bank[7][:, 0:30], col("nsa_kc_norm_2"), None, ALU.mult).then_inc(cm_kc, 1)
            dve.wait_ge(ring_free, RING0["w_in2"] + 43)
            g3 = r2["gt"].rearrange("p (b h k) -> p b h k", b=TT, h=NH)
            v.then(dve.tensor_tensor(g3[:, :, :, 0], g3[:, :, :, 0], wide(c2["cmp_valid"], NH), ALU.mult))

        def pe_nsa_sums(pe):
            pe.wait_ge(n_sq, 1)
            for g in range(6):
                if g == 5:
                    pe.wait_ge(n_rt, 1)
                pe.matmul(bank[3 + g % 5][:, :], ones, r2["sq"][:, 512 * g:512 * g + 512], start=True,
                          stop=True).then_inc(n_ss, 1)

            pe.wait_ge(c_sq, 1)
            pe.wait_ge(n_rt, 3)
            for k in range(5):
                mm = pe.matmul(bank[4 + k // 3][:, 0:S], ones, csq[:, k, :], start=(k in (0, 3)), stop=(k in (2, 4)))
            mm.then_inc(c_ss, 1)

        def pe_nsa_turn(pe):
            pe.wait_ge(n_qn, 1)
            pe.wait_ge(c_rt, 2)
            pe.wait_ge(c2_loaded, 16)
            for g in range(7):
                if g >= 5:
                    pe.wait_ge(n_q, g - 4)
                pe.matmul(bank[3 + g % 5][:, :], c2["rot_nsa"], r2["F2"][:, 512 * g:512 * g + 512], start=True,
                          stop=True).then_inc(n_rot, 1)

        def pe_compress(pe, i, name):
            if i == 0:
                pe.wait_ge(cm_x, 1)
                pe.wait_ge(ring_free, RING0["uv"] + COUNT["uv"])
            for t in range(8):
                n = FIRST[name] + t
                pe.wait_ge(landed[slot_of(n)], count_at(n))
                for k in range(4):
                    l = 4 * t + k
                    mm = pe.matmul(bank[i][0:30, 0:256], XP[:, i, l, :], blocks(slot_of(n), k, 256),
                                   start=(l == 0), stop=(l == CB - 1))
                mm.then_inc(tile_done, 1)

        def pe_compressed(pe):
            n = FIRST["cmp_w2"]
            pe.wait_ge(landed[slot_of(n)], count_at(n))
            for i in range(2):
                pe.wait_ge(cm_hs, i + 1)
                if i:
                    pe.wait_ge(cm_ts, 1)
                for h in range(2):
                    mm = pe.transpose(bank[2][:, h * 30:(h + 1) * 30], r2["hid"][0:30, h * 128:(h + 1) * 128],
                                      ident[0:30, 0:30])
                mm.then_inc(cm_t, 1)
                pe.wait_ge(cm_ts, i + 1)
                for g in range(NG):
                    for h in range(2):
                        mm = pe.matmul(bank[6][0:NCMP, i * 256 + g * 128:i * 256 + (g + 1) * 128],
                                       r2["hidT"][:, h * 30 + g * NCMP:h * 30 + (g + 1) * NCMP],
                                       blocks(slot_of(n), 2 * i + h), start=(h == 0), stop=(h == 1))
                if i == 0:
                    mm.then_inc(cm_o0, 1)
            mm.then_inc(tile_done, 1)
            pe.wait_ge(cm_kn, 2)
            for g in range(NG):
                mm = pe.transpose(bank[7][:, g * NCMP:(g + 1) * NCMP], r2["cmt"][0:NCMP, g * 128:(g + 1) * 128],
                                  ident[0:NCMP, 0:NCMP])
            mm.then_inc(cm_kt, 1)

        def act_nsa_roots(act):
            for g in range(6):
                act.wait_ge(n_ss, g + 1)
                act.activation(r2["rs"][:, 512 * g:512 * g + 512], bank[3 + g % 5][:, :], ACT.Sqrt, scale=1.0 / 128,
                               bias=col("eps")).then_inc(n_rt, 1)
            act.wait_ge(c_ss, 1)
            for k, n in enumerate((3, 2)):
                act.activation(crs[:, k, :], bank[4 + k][:, 0:S], ACT.Sqrt, scale=1.0 / (n * 128),
                               bias=col("eps")).then_inc(c_rt, 1)

        def act_compressed(act):
            for i, name in enumerate(("cmp_k", "cmp_v")):
                act.wait_ge(tile_done, FIRST[name] + 8)
                if i:
                    act.wait_ge(cm_t, 1)
                act.activation(r2["hid"][0:30, :], bank[i][0:30, 0:256], ACT.Silu).then_inc(cm_hs, 1)
                act.wait_ge(cm_t, i + 1)
                if i:
                    act.wait_ge(cm_o0, 1)
                act.copy(r2["hidT"][:, 0:60], bank[2][:, 0:60]).then_inc(cm_ts, 1)
            act.wait_ge(cm_kn, 1)
            act.activation(r2["kst"][0:NCMP, 2:4], r2["kst"][0:NCMP, 0:2], ACT.Sqrt, scale=1.0 / 128,
                           bias=col("eps")[0:NCMP]).then_inc(cm_rt, 1)

        vcv = r2["cmt"][0:NCMP, 256:512].rearrange("p (g f) -> p g f", g=NG)
        g3v = r2["gt"].rearrange("p (b h k) -> p b h k", b=TT, h=NH)
        masks2 = dict(causal=c2["causal"], cmp=c2["cmp_mask"])
        nsa_jobs = []
        for h in range(NH):
            g = h // (NH // NG)
            for k, (kind, key, val) in enumerate((("cmp", r2["kcT"][:, g * NCMP:(g + 1) * NCMP], lambda b, g=g: vcv[:, g, :]),
                                                  ("causal", F2[:, 8 + g, :], lambda b, g=g: vs2[:, b, g * 128:(g + 1) * 128]),
                                                  ("causal", F2[:, 10 + g, :], lambda b, g=g: vw2[:, b, g * 128:(g + 1) * 128]))):
                nsa_jobs.append(dict(n=MH + 3 * h + k, group=MH + h, first=(k == 0), last=(k == 2), kind=kind,
                                     scale=128 ** -0.5, gate=g3v[:, :, h, k], q=[F2[:, h, :]], k=[key], M=128,
                                     v=val, rows=all_rows, out=oA[:, h, :], buf=att2, masks=masks2))

        def dve_mla(dve, v):
            v.then(dve.memset(kro[:, :, :], 0.0))
            dve.wait_ge(ring_free, RING0["uq"] + 6)
            dve.tensor_tensor(sq14[:, 0:12, :], qb[:, :, :], qb[:, :, :], ALU.mult).then_inc(l_sq, 1)
            dve.wait_ge(l_rt, 4)
            rsv = rs12[:, 0:8, :]
            v.then(dve.reciprocal(rsv, rsv))
            v.did(dve.scalar_tensor_tensor(qb[:, 0:8, :], qb[:, 0:8, :], col("mla_q_nope"), rsv, ALU.mult, ALU.mult))
            pairs = r2["rs"][:, 0:2048].rearrange("p (m h t) -> p h m t", h=2, t=S)
            for h, r in enumerate((lo, hi)):
                ins = dve.scalar_tensor_tensor(qb[r, 8:12, :], qb[r, 8:12, :], col("mla_q_rope")[r], pairs[r, h],
                                               ALU.mult, ALU.mult)
            v.then(ins)
            dve.tensor_scalar(krr, F2[:, 21, :], col("mla_k_rope"), None, ALU.mult).then_inc(l_q, 1)
            dve.wait_ge(l_q, 1)
            ro = sq14[:, 0:5, :]
            dve.wait_ge(l_rot, 1)
            for g in range(2):
                dve.tensor_tensor(ro[:, 2 * g:2 * g + 2, :], bank[3 + g][:, :].rearrange("p (m t) -> p m t", m=2),
                                  over(c2["mla_sin"], 2), ALU.mult)
            v.did(dve.tensor_tensor(ro[:, 4, :], bank[5][:, 0:S], c2["mla_sin"], ALU.mult))
            v.did(dve.tensor_tensor(qb[:, 8:12, :], qb[:, 8:12, :], over(c2["mla_cos"], 4), ALU.mult))
            v.then(dve.tensor_tensor(krt, krr, c2["mla_cos"], ALU.mult))
            v.did(dve.tensor_tensor(qb[:, 8:12, :], qb[:, 8:12, :], ro[:, 0:4, :], ALU.add))
            v.then(dve.tensor_tensor(krt, krt, ro[:, 4, :], ALU.add))
            dve.wait_ge(ring_free, RING0["uk"] + 4)
            v.did(dve.tensor_tensor(sq14[:, 0:8, :], kb[:, :, :], kb[:, :, :], ALU.mult))
            dve.tensor_tensor(sq14[:, 8, :], F2[:, 21, :], F2[:, 21, :], ALU.mult).then_inc(l_sq, 1)
            dve_compressed(dve, v)
            dve.wait_ge(l_rt, 8)
            v.then(dve.reciprocal(rsv, rsv))
            v.did(dve.scalar_tensor_tensor(kb[:, :, :], kb[:, :, :], col("mla_k_nope"), rsv, ALU.mult, ALU.mult))
            for h, r in enumerate((lo, hi)):
                kr4 = kro.rearrange("p (m h) t -> p h m t", h=2)
                ins = dve.tensor_tensor(kr4[r, h], pairs[r, h], over(krt, 4)[r], ALU.mult)
            ins.then_inc(l_k, 1)
            dve.wait_ge(ring_free, RING0["uv"] + 4)
            att_dve(dve, v, nsa_jobs + mla_jobs)
            dve.wait_ge(a_free, MH + NH + MLH)
            v.did(dve.tensor_tensor(oA[:, :, :], oA[:, :, :], bg[:, 0:8, :], ALU.mult))
            v.then(dve.tensor_tensor(oB[:, :, :], oB[:, :, :], bg[:, 8:16, :], ALU.mult))
            dve.tensor_tensor(oA[:, :, :], oA[:, :, :], oB[:, :, :], ALU.add).then_inc(mix_ready, 1)

        def pe_mla(pe):
            pe.wait_ge(c_n, 1)

            def uq(slot, bk):
                for o in range(2):
                    for k in range(3):
                        mm = pe.matmul(bk[:, o * S:(o + 1) * S], blocks(slot, 3 * o + k), F2[:, 16 + k, :],
                                       start=(k == 0), stop=(k == 2))
                return mm

            def uk(slot, bk):
                for o in range(2):
                    for k in range(2):
                        mm = pe.matmul(bk[:, o * S:(o + 1) * S], blocks(slot, 2 * o + k), F2[:, 19 + k, :],
                                       start=(k == 0), stop=(k == 1))
                return mm

            def uv(slot, bk):
                for b in range(TT):
                    for k in range(2):
                        mm = pe.matmul(bk[:, b * S:(b + 1) * S], F2[:, 19 + k, b * 128:(b + 1) * 128],
                                       blocks(slot, k, 256), start=(k == 0), stop=(k == 1))
                return mm

            def sums(sq_count, rope_tile):
                pe.wait_ge(l_sq, sq_count)
                for g in range(4):
                    for i in range(2):
                        h = 2 * g + i
                        out = bank[3 + g][:, i * S:(i + 1) * S]
                        pe.matmul(out, ones, sq14[:, h, :], start=True, stop=False)
                        half = c2[("half0", "half1")[i]] if rope_tile is None else c2["half0"]
                        rope = sq14[:, 8 + g, :] if rope_tile is None else sq14[:, rope_tile, :]
                        mm = pe.matmul(out, half, rope, start=False, stop=True)
                    mm.then_inc(l_ss, 1)

            ring_tiles(pe, "uq", uq)
            ring_tiles(pe, "uk", uk)
            ring_tiles(pe, "uv", uv)
            sums(1, None)
            pe_compress(pe, 0, "cmp_k")
            pe.wait_ge(l_q, 1)
            for g in range(2):
                pe.matmul(bank[3 + g][:, :], c2["rot_mla"], r2["qb"][:, (8 + 2 * g) * S:(10 + 2 * g) * S],
                          start=True, stop=True)
            pe.matmul(bank[5][:, 0:S], c2["rot_mla"], krr, start=True, stop=True).then_inc(l_rot, 1)
            pe_compress(pe, 1, "cmp_v")
            pe_compressed(pe)
            sums(2, 8)
            pe.wait_ge(cm_kc, 1)
            pe.wait_ge(l_k, 1)
            att_pe(pe, nsa_jobs + mla_jobs)

        def act_mla(act):
            for t in range(6):
                tile_wait(act, "uq", t)
                act.copy(qb[:, 2 * t:2 * t + 2, :], ring_bank("uq", t)[:, :].rearrange("p (m t) -> p m t", m=2))\
                   .then_inc(ring_free, 1)
            for t in range(4):
                tile_wait(act, "uk", t)
                act.copy(kb[:, 2 * t:2 * t + 2, :], ring_bank("uk", t)[:, :].rearrange("p (m t) -> p m t", m=2))\
                   .then_inc(ring_free, 1)
            for t in range(4):
                tile_wait(act, "uv", t)
                act.copy(vb[:, :, 2 * t:2 * t + 2, :],
                         ring_bank("uv", t)[:, :].rearrange("p (b h f) -> p b h f", b=TT, h=2)).then_inc(ring_free, 1)
            for g in range(8):
                if g == 4:
                    act_compressed(act)
                act.wait_ge(l_ss, g + 1)
                if g == 4:
                    act.wait_ge(l_q, 1)
                act.activation(r2["rs"][:, 512 * (g % 4):512 * (g % 4) + 512], bank[3 + g % 4][:, :], ACT.Sqrt,
                               scale=1.0 / 192, bias=col("eps")).then_inc(l_rt, 1)
            att_act(act, nsa_jobs + mla_jobs)

        mla_jobs = [dict(n=MH + 3 * NH + h, group=MH + NH + h, first=True, last=True, kind="causal", scale=192 ** -0.5,
                         gate=None, q=[qb[:, h, :], qb[:, 8 + h // 2, :]], k=[kb[:, h, :], kro[:, h, :]], M=128,
                         v=lambda b, h=h: vb[:, b, h, :], rows=all_rows, out=oB[:, h, :], buf=att2, masks=masks2)
                    for h in range(MLH)]

        def pe_w_o(pe):
            pe.wait_ge(mix_ready, 1)
            ring_tiles(pe, "w_o", lambda slot, bk: matmul8(pe, bk[:, 0:S], slot, oA))

        f_z, f_u, f_g, f_whi, f_w = sem("f_z"), sem("f_u"), sem("f_g"), sem("f_whi"), sem("f_w")
        F0 = FIRST["ffn"]
        up_tile = lambda f: F0 + (0 if f == 0 else 3 * f - 1)
        down_tile = lambda f: F0 + (3 * f + 4 if f < FT - 1 else 3 * FT - 1)

        def pe_ffn(pe):
            pe.wait_ge(x_lo, 16)

            def up(f, i):
                for k in range(2):
                    n = up_tile(f) + k
                    pe.wait_ge(lo_ready, 6 * i + nth_split[n])
                    if k == 0 and f >= 2:
                        pe.wait_ge(f_z, 2 * i + (f - 1))
                    split8(pe, bank[f % 2][:, k * S:(k + 1) * S], n).then_inc(tile_done, 1)

            def down(f, i, first=False, last=False):
                n = down_tile(f)
                pe.wait_ge(lo_ready, 6 * i + nth_split[n])
                pe.wait_ge(f_w, 2 * i + (f + 1))
                down8(pe, n, f % 2, first, last).then_inc(tile_done, 1)

            up(0, 0)
            up(1, 0)
            down(0, 0, first=True)
            with pe.Fori(0, (FT - 2) // 2) as i:
                for u in range(2):
                    up(2 + u, i)
                    down(1 + u, i)
            down(FT - 1, 0, last=True)

        def act_ffn(act):
            def z(f, i):
                act.wait_ge(tile_done, 6 * i + (up_tile(f) + 2))
                if f >= 2:
                    act.wait_ge(f_u, 2 * i + (f - 1))
                act.copy(zf[:, f % 2, :, 2:258], bank[f % 2][:, :].rearrange("p (k t) -> p k t", k=2)).then_inc(f_z, 1)

            def silu(f, i):
                act.wait_ge(f_u, 2 * i + (f + 1))
                if f >= 2:
                    act.wait_ge(f_w, 2 * i + (f - 1))
                act.activation(sgf[:, f % 2, :], uf[:, f % 2, 1, :], ACT.Silu).then_inc(f_g, 1)
            def hi(n, i):
                if n < TILES:
                    act_hi(act, n, 16 * i + count_at(n), 6 * i + (n - HSLOTS + 1))

            def turn(f, i=0):
                n = up_tile(f)
                if f > 0:
                    hi(n + 2, i)
                    hi(n + 3, i)
                z(f, i)
                if f > 0:
                    hi(n + 4, i)
                silu(f, i)

            for n in range(F0, F0 + 4):
                hi(n, 0)
            act.wait_ge(pad_ready, 1)
            turn(0)
            turn(1)
            with act.Fori(0, (FT - 2) // 2 - 1) as i:
                turn(2, i)
                turn(3, i)
            turn(FT - 2)
            turn(FT - 1)

        pad_ready = sem("pad_ready")

        def dve_ffn(dve, v):
            dve.memset(zf[:, :, :, 0:2], 0.0).then_inc(pad_ready, 1)
            taps = [sem("tap0"), sem("tap1")]

            def lo(n, i):
                if n < TILES:
                    tile_lo(dve, n, 6 * i + nth_split[n])

            def one(f, i):
                n = up_tile(f)
                if f > 0:
                    lo(n + 2, i)
                    lo(n + 3, i)
                dve.wait_ge(f_z, 2 * i + (f + 1))
                if f >= 2:
                    dve.wait_ge(f_w, 2 * i + (f - 1))
                b = f % 2
                for k in range(2):
                    c = COL["conv"] + f * 8 + 4 * k
                    cc = (lambda x: cols[:, bass.ds(16 * i + (c + x), 1)]) if not isinstance(i, int) else \
                        (lambda x: cols[:, c + x:c + x + 1])
                    ins = dve.tensor_scalar(uf[:, b, k, :], zf[:, b, k, 2:258], cc(2), cc(3), ALU.mult, ALU.add)
                    if k == 1:
                        ins.then_inc(taps[0], 1)
                dve.wait_ge(taps[0], 2 * i + (f + 1))
                for x in (1, 0):
                    for k in range(2):
                        c = COL["conv"] + f * 8 + 4 * k
                        w = cols[:, bass.ds(16 * i + (c + x), 1)] if not isinstance(i, int) else cols[:, c + x:c + x + 1]
                        ins = dve.scalar_tensor_tensor(uf[:, b, k, :], zf[:, b, k, x:x + 256], w, uf[:, b, k, :],
                                                       ALU.mult, ALU.add)
                    ins.then_inc(taps[1] if x == 1 else f_u, 1)
                    if x == 1:
                        dve.wait_ge(taps[1], 2 * i + (f + 1))
                if f > 0:
                    lo(n + 4, i)
                dve.wait_ge(f_g, 2 * i + (f + 1))
                if f >= 2:
                    dve.wait_ge(tile_done, 6 * i + (down_tile(f - 2) + 1))
                dve.tensor_tensor(Whi[:, b, :], uf[:, b, 0, :], sgf[:, b, :], ALU.mult).then_inc(f_whi, 1)
                dve.tensor_tensor(Wf[:, b, :], uf[:, b, 0, :], sgf[:, b, :], ALU.mult).then_inc(f_whi, 1)
                dve.wait_ge(f_whi, 4 * i + (2 * f + 2))
                dve.tensor_tensor(Wlo[:, b, :], Wf[:, b, :], Whi[:, b, :].bitcast(F32), ALU.subtract).then_inc(f_w, 1)
            for n in range(F0, F0 + 4):
                lo(n, 0)
            one(0, 0)
            one(1, 0)
            with dve.Fori(0, (FT - 2) // 2 - 1) as i:
                for u in range(2):
                    one(2 + u, i)
            one(FT - 2, 0)
            one(FT - 1, 0)
            dve.wait_ge(tile_done, TILES)
            dve_add_accs(dve, 11)

        def sp_out(sp):
            sp.wait_ge(acc_read, 2)
            sp.dma_start(a["out"], hT[:, :, :]).then_inc(stored, 16)
            sp.wait_ge(stored, 16)

        block = ctx.enter_context(nc.Block())

        @block.sync
        def _(sp):
            sp_ada(sp)
            sp_w_in(sp)
            for name, _ in PHASES[1:]:
                if name == "peer":
                    sp_peer(sp)
                else:
                    sp_weights(sp, name)
            sp_out(sp)

        @block.tensor
        def _(pe):
            norm_pe(pe, 0, sq0)
            pe_w_in(pe)
            pe_moba(pe)
            pe_rwkv(pe)
            pe_proj(pe)
            pe_w_out(pe)
            norm_pe(pe, 1, nsq[1])
            pe_route(pe)
            pe_turn_routes(pe)
            pe_gates(pe)
            pe_peer(pe)
            norm_pe(pe, 2, nsq[2])
            pe_w_in2(pe)
            pe_mla(pe)
            pe_w_o(pe)
            norm_pe(pe, 3, nsq[3])
            pe_ffn(pe)

        @block.scalar
        def _(act):
            act_head(act)
            norm_act(act, 0, rtn[0])
            x_upper(act, 0)
            act_w_in(act)
            act_moba(act)
            act_rwkv(act)
            act_rwkv_out(act)
            norm_act(act, 1, rtn[1])
            x_upper(act, 1)
            act_route(act)
            act_gates(act)
            act_peer(act)
            act_const2(act)
            norm_act(act, 2, rtn[2])
            x_upper(act, 2)
            act_w_in2(act)
            act_mla(act)
            norm_act(act, 3, rtn[3])
            x_upper(act, 3)
            act_ffn(act)

        @block.vector
        def _(dve):
            v = Steps(dve, vdone)
            dve.wait_ge(crow_ready, 1)
            for n in range(2 * KT):
                if n == ASLOTS:
                    dve.wait_ge(loaded, 64)
                    norm_squares(dve, sq0)
                if n == 2 * KT - 4:
                    norm_scale(dve, v, 0, rtn[0])
                dve_ada(dve, n)
            dve.wait_ge(ada_used, 2 * KT)
            dve_add_bias(dve, v, 0, 2 * KT)
            dve_gsc(dve, v, 0)
            norm_shift(dve, 0, 0)
            for n in range(2 * KT, 6 * KT):
                if n == SHIFT_AT:
                    dve_shift(dve, v)
                if n == MOBA_AT:
                    dve_moba_start(dve, v)
                dve_ada(dve, n)
            dve.wait_ge(ada_used, 6 * KT)
            dve_add_bias(dve, v, 2 * KT, 6 * KT)
            dve_gsc(dve, v, 1)
            dve_moba(dve, v)
            dve_rwkv(dve, v)
            dve_proj(dve, v)
            dve_residual(dve, "w_out", 2)
            norm_squares(dve, nsq[1])
            norm_scale(dve, v, 1, rtn[1])
            norm_shift(dve, 1, 3)
            x_rest(dve, 1)
            lo_phase(dve, "wq")
            dve_route(dve, v)
            dve_hot(dve)
            dve_peer(dve, v)
            norm_squares(dve, nsq[2])
            norm_scale(dve, v, 2, rtn[2])
            norm_shift(dve, 2, 6)
            dve.wait_ge(tile_done, FIRST["w_in2"] + SKIP["w_in2"])
            x_rest(dve, 2)
            lo_phase(dve, "w_in2", SKIP["w_in2"], 27)
            dve_nsa(dve, v)
            dve_mla(dve, v)
            dve_residual(dve, "w_o", 8)
            norm_squares(dve, nsq[3])
            norm_scale(dve, v, 3, rtn[3])
            norm_shift(dve, 3, 9)
            x_rest(dve, 3)
            dve_ffn(dve, v)

        @block.gpsimd
        def _(pool):
            pool_moba(pool)
            pool_w_in(pool)
            att_pool(pool, moba_jobs)
            pool_rwkv(pool)
            pool_route(pool)
            pool_hot(pool)
            pool.wait_ge(lo_ready, nth_split[FIRST["w_in2"] + 26])
            lo_phase(pool, "w_in2", 27)
            att_pool(pool, nsa_jobs + mla_jobs)


def column_tiles(w):
    k, n = w.shape
    return w.reshape(k // 128, 128, n // 128, 128).transpose(2, 1, 0, 3).reshape(n // 128, 128, k)


def pack_weights(x):
    w = np.zeros((TILES, 128, D), np.float32)

    def put(name, tiles, at=0):
        first = FIRST[name] + at
        w[first:first + len(tiles), :, :tiles.shape[2]] = tiles

    w_in = x["w_in"][0]
    put("w_in", column_tiles(np.concatenate([w_in[:, 1024:1536], w_in[:, 1536:3328], w_in[:, 0:1024], w_in[:, 3328:]], 1)))
    put("proj", np.concatenate([column_tiles(x["w_proj_moba"][0]), column_tiles(x["w_proj_rwkv"][0])], 2))
    put("w_out", column_tiles(x["w_out"][0]))
    put("wq", column_tiles(x["peer_wq"][0]))
    u = x["peer_u"][0].reshape(NK, NK, KT, 128).transpose(1, 3, 2, 0).reshape(NK, 128, D)
    v = x["peer_v"][0].reshape(NK, NK, D).transpose(1, 0, 2)
    p0 = FIRST["peer"]
    w[p0] = u[0]
    w[p0 + 1:p0 + 2 * NK - 1:2] = u[1:]
    w[p0 + 2:p0 + 2 * NK - 1:2] = v[:-1]
    w[p0 + 2 * NK - 1] = v[-1]
    w2 = x["w_in_2"][0]
    kr = w2[:, 3224:3288]
    gate = np.concatenate([w2[:, 2560:2584], np.zeros((D, 104), np.float32)], 1)
    put("w_in2", column_tiles(np.concatenate(
        [w2[:, 1792:2048], w2[:, 2304:2560], gate, w2[:, 0:1024], w2[:, 1536:1792], w2[:, 2048:2304],
         w2[:, 1024:1280], w2[:, 1280:1536], w2[:, 2584:3224], kr, kr, w2[:, 3288:5336]], 1)))
    for name in ("k", "v"):
        put(f"cmp_{name}", x[f"cmp_{name}_w1_2"][0].reshape(8, 4, 128, 256).transpose(0, 2, 1, 3).reshape(8, 128, D))
    second = [x[f"cmp_{n}_w2_2"][0].reshape(2, 128, 128).transpose(1, 0, 2).reshape(128, 256) for n in "kv"]
    put("cmp_w2", np.concatenate(second, 1)[None])
    uq = x["w_uq_2"][0].reshape(384, MLH, 192)
    uq = np.concatenate([uq[:, :, :128].reshape(384, -1), uq[:, :, 128:].reshape(384, -1)], 1)
    put("uq", column_tiles(uq).reshape(6, 2, 128, 384).transpose(0, 2, 1, 3).reshape(6, 128, 768))
    ukv = x["w_ukv_2"][0].reshape(256, MLH, 2, 128)
    put("uk", column_tiles(ukv[:, :, 0].reshape(256, -1)).reshape(4, 2, 128, 256).transpose(0, 2, 1, 3).reshape(4, 128, 512))
    put("uv", ukv[:, :, 1].reshape(2, 128, 4, 256).transpose(2, 1, 0, 3).reshape(4, 128, 512))
    put("w_o", column_tiles(x["w_o_2"][0]))
    up, down = column_tiles(x["w_up_2"][0]), x["w_down_2"][0].reshape(FT, 128, D)
    order = [up[0], up[FT]]
    for f in range(1, FT):
        order += [up[f], up[FT + f], down[f - 1]]
    put("ffn", np.stack(order + [down[FT - 1]]))
    return w


def pack_columns(x):
    turned = lambda t: t.reshape(-1, 128).T
    twice = lambda t: np.tile(t.reshape(-1), 2).reshape(128, 1)
    inv = np.float32(500000.0) ** (-(np.arange(MD // 8, dtype=np.float32) * np.float32(2.0)) / np.float32(MD // 4))
    inv64 = np.zeros(64, np.float32)
    inv64[:MD // 4] = np.tile(inv, 2)
    part = {n: turned(x[n]) for n, k in COLS if n in x and x[n].size == 128 * k}
    part["q_norm_g"], part["k_norm_g"] = twice(x["q_norm_g"]), twice(x["k_norm_g"])
    for n in "qk":
        g = x[f"mla_{n}_norm_2"].reshape(-1)
        part[f"mla_{n}_nope"], part[f"mla_{n}_rope"] = g[:128].reshape(128, 1), twice(g[128:])
        part[f"cmp_{'kv'['qk'.index(n)]}_pe"] = x[f"cmp_{'kv'['qk'.index(n)]}_pe_2"][0].T
    conv = np.concatenate([x["w_conv_2"][0], x["b_conv_2"]], 0)
    part["conv"] = conv.reshape(4, 2, FT, 128).transpose(3, 2, 1, 0).reshape(128, FT * 8)
    part["rope_inv"] = twice(inv64)
    part["eps"], part["gn_eps"] = np.full((128, 1), RMS_EPS), np.full((128, 1), GN_EPS)
    return np.ascontiguousarray(np.concatenate([part[n].astype(np.float32) for n, _ in COLS], 1))


def lay_out(x):
    x = {k: np.asarray(v) for k, v in x.items()}
    keep, const1, const2 = shape_constants()
    ada = np.ascontiguousarray(x["w_ada"][0].T.reshape(6 * KT, 128, D))
    ada2 = x["w_ada_2"][0].T.reshape(6 * KT, 128, 2, AHALF).transpose(2, 0, 1, 3).reshape(12 * KT, 128, AHALF)
    lora = np.zeros((128, 3, 512), np.float32)
    lora[:64, 0], lora[64:, 1], lora[:, 2] = x["rwkv_w2"][0], x["rwkv_a2"][0], x["rwkv_g2"][0]
    return {
        "xT": np.ascontiguousarray(x["x"][0].T.reshape(KT, 128, S).transpose(1, 0, 2)),
        "positions": np.ascontiguousarray(x["positions"]), "cols": pack_columns(x), "keep": keep,
        "const1": const1, "const2": const2, "ada": ada, "ada2": np.ascontiguousarray(ada2), "lora": lora,
        "crow": np.concatenate([x["c"].reshape(1, D), x["c_2"].reshape(1, D)]),
        "subk": np.ascontiguousarray(x["peer_subkeys"][0].transpose(3, 0, 1, 2).reshape(128, 2 * PH * NK)),
        "w": pack_weights(x),
    }


def kernel(**inputs):
    import concourse.bacc as bacc
    from concourse.bass_utils import run_bass_kernel_spmd

    nc = bacc.Bacc("TRN2", target_bir_lowering=False, num_devices=1)
    arrays = {f"in_{k}": v for k, v in lay_out(inputs).items()}
    a = {k[3:]: nc.dram_tensor(k, v.shape, mybir.dt.from_np(v.dtype), kind="ExternalInput").ap()
         for k, v in arrays.items()}
    a["out"] = nc.dram_tensor("out_hT", [128, KT, S], F32, kind="ExternalOutput").ap()
    build_layer_pair(nc, a)
    r = run_bass_kernel_spmd(nc, [arrays], core_ids=[0])
    hT = r.results[0]["out_hT"]
    return np.ascontiguousarray(hT.transpose(2, 1, 0).reshape(1, S, D))
```
